# Optimizing a Trainium2 kernel written in Bass

```python
import jax, jax.numpy as jnp
from jax import lax
import numpy as np

D_MODEL = 1024
BATCH = 1
SEQ = 256
DEPTH = 2

N_A = DEPTH // 2
N_B = DEPTH - N_A
HEAD_DIM = 64
MIX_HEADS = 12
MIX_WIDTH = MIX_HEADS * HEAD_DIM
MEM_HEADS = 4
MEM_WIDTH = MEM_HEADS * HEAD_DIM
MEM_TOKENS = 256
D_FF = 2752
DECAY_LORA = 64
AAA_LORA = 64
GATE_LORA = 128
SHIFT_WIDTH = 3 * MIX_WIDTH + DECAY_LORA + AAA_LORA + GATE_LORA
A_IN_WIDTH = SHIFT_WIDTH + MEM_WIDTH
B_IN_WIDTH = MIX_WIDTH + MEM_WIDTH
KV_WIDTH = 2 * MIX_WIDTH
MOBA_BLOCK = 256
MOBA_TOPK = 3
Q_CHUNK = 128
ALIBI_MAX = 8.0
NORM_EPS = 1e-6
GN_EPS = 64e-5

kernel_name = "yoco_rwkv7_moba_macaron_memory"

def rms_norm(x, g, eps=NORM_EPS):
    xf = x.astype(jnp.float32)
    y = xf * lax.rsqrt(jnp.mean(xf * xf, axis=-1, keepdims=True) + eps)
    return (y * g.astype(jnp.float32)).astype(x.dtype)

def swiglu_ffn(x, g, w1, w3, w2):
    h = rms_norm(x, g)
    return (jax.nn.silu(h @ w1) * (h @ w3)) @ w2

def rwkv7_mixer(u, mu, w0, w2, a0, a2, g2, k_k, k_a, r_k, ln_w, ln_b):
    B_, S_, _ = u.shape
    f32 = jnp.float32
    prev = jnp.pad(u[:, :-1], ((0, 0), (1, 0), (0, 0)))
    u = u + (prev - u) * mu
    cuts = [MIX_WIDTH, 2 * MIX_WIDTH, 3 * MIX_WIDTH,
            3 * MIX_WIDTH + DECAY_LORA, 3 * MIX_WIDTH + DECAY_LORA + AAA_LORA]
    r, k, v, wd, ad, gd = jnp.split(u, cuts, axis=-1)
    w_log = -jax.nn.softplus(-(w0 + jnp.tanh(wd) @ w2).astype(f32)) - 0.5
    decay = jnp.exp(-jnp.exp(w_log))
    a = jax.nn.sigmoid((a0 + ad @ a2).astype(f32))
    g = jax.nn.sigmoid(gd) @ g2

    def heads(t):
        return t.astype(f32).reshape(B_, S_, MIX_HEADS, HEAD_DIM)

    def per_head(p):
        return p.astype(f32).reshape(MIX_HEADS, HEAD_DIM)

    r, k, v, decay, a = heads(r), heads(k), heads(v), heads(decay), heads(a)
    kk = k * per_head(k_k)
    kk = kk / jnp.maximum(jnp.sqrt(jnp.sum(kk * kk, axis=-1, keepdims=True)), 1e-12)
    k = k * (1.0 + (a - 1.0) * per_head(k_a))
    b = kk * a

    def step(state, inp):
        r_t, w_t, k_t, v_t, kk_t, b_t = inp
        sa = jnp.einsum('bhvk,bhk->bhv', state, kk_t)
        state = (state * w_t[:, :, None, :] - sa[..., None] * b_t[:, :, None, :]
                 + v_t[..., None] * k_t[:, :, None, :])
        y_t = jnp.einsum('bhvk,bhk->bhv', state, r_t)
        return state, y_t

    xs = tuple(jnp.moveaxis(t, 1, 0) for t in (r, decay, k, v, kk, b))
    state0 = jnp.zeros((B_, MIX_HEADS, HEAD_DIM, HEAD_DIM), f32)
    _, y = lax.scan(step, state0, xs)
    y = jnp.moveaxis(y, 0, 1)
    mean = jnp.mean(y, axis=-1, keepdims=True)
    var = jnp.mean(jnp.square(y - mean), axis=-1, keepdims=True)
    y = ((y - mean) * lax.rsqrt(var + GN_EPS)).reshape(B_, S_, MIX_WIDTH)
    y = y * ln_w.astype(f32) + ln_b.astype(f32)
    bonus = jnp.sum(r * k * per_head(r_k), axis=-1, keepdims=True) * v
    y = (y + bonus.reshape(B_, S_, MIX_WIDTH)) * g.astype(f32)
    return y.astype(u.dtype)

def memory_attention(q, mem, mem_norm, w_mem_kv, q_norm, k_norm):
    B_, S_, _ = q.shape
    M_ = mem.shape[1]
    q = rms_norm(q.reshape(B_, S_, MEM_HEADS, HEAD_DIM), q_norm)
    kv = rms_norm(mem, mem_norm) @ w_mem_kv
    k, v = jnp.split(kv, [MEM_WIDTH], axis=-1)
    k = rms_norm(k.reshape(B_, M_, MEM_HEADS, HEAD_DIM), k_norm)
    v = v.reshape(B_, M_, MEM_HEADS, HEAD_DIM)
    s = jnp.einsum('bshd,bmhd->bhsm', q, k, preferred_element_type=jnp.float32) * (HEAD_DIM ** -0.5)
    p = jax.nn.softmax(s, axis=-1).astype(v.dtype)
    o = jnp.einsum('bhsm,bmhd->bshd', p, v)
    return o.reshape(B_, S_, MEM_WIDTH)

def shared_kv(x, kv_norm, w_kv, k_norm):
    B_, S_, _ = x.shape
    nb = -(-S_ // MOBA_BLOCK)
    pad = nb * MOBA_BLOCK - S_
    kv = rms_norm(x, kv_norm) @ w_kv
    k, v = jnp.split(kv, [MIX_WIDTH], axis=-1)
    k = rms_norm(k.reshape(B_, S_, MIX_HEADS, HEAD_DIM), k_norm)
    v = v.reshape(B_, S_, MIX_HEADS, HEAD_DIM)
    k = jnp.pad(k, ((0, 0), (0, pad), (0, 0), (0, 0)))
    v = jnp.pad(v, ((0, 0), (0, pad), (0, 0), (0, 0)))
    k_blocks = k.reshape(B_, nb, MOBA_BLOCK, MIX_HEADS, HEAD_DIM).transpose(0, 3, 1, 2, 4)
    v_blocks = v.reshape(B_, nb, MOBA_BLOCK, MIX_HEADS, HEAD_DIM).transpose(0, 3, 1, 2, 4)
    k_mean = jnp.mean(k_blocks.astype(jnp.float32), axis=3).astype(k.dtype)
    return k_blocks, v_blocks, k_mean

def moba_attention(q, k_blocks, v_blocks, k_mean, q_norm):
    B_, S_, _ = q.shape
    nb = k_mean.shape[2]
    nc = S_ // Q_CHUNK
    topk = min(MOBA_TOPK, nb)
    scale = HEAD_DIM ** -0.5
    q = rms_norm(q.reshape(B_, S_, MIX_HEADS, HEAD_DIM), q_norm)
    q_chunks = q.reshape(B_, nc, Q_CHUNK, MIX_HEADS, HEAD_DIM).transpose(1, 0, 3, 2, 4)
    slopes = jnp.exp2(-ALIBI_MAX * jnp.arange(1, MIX_HEADS + 1, dtype=jnp.float32) / MIX_HEADS)
    b_idx = jnp.arange(B_)[:, None, None, None]
    h_idx = jnp.arange(MIX_HEADS)[None, :, None, None]
    offs = jnp.arange(MOBA_BLOCK)

    def one_chunk(args):
        qc, c = args
        t = c * Q_CHUNK + jnp.arange(Q_CHUNK)
        i_blk = (c * Q_CHUNK) // MOBA_BLOCK
        gate = jnp.einsum('bhcd,bhnd->bhcn', qc, k_mean, preferred_element_type=jnp.float32)
        gate = jnp.where(jnp.arange(nb) < i_blk, gate, -jnp.inf)
        _, sel = lax.top_k(gate, topk)
        valid = sel < i_blk
        kg = k_blocks[b_idx, h_idx, sel]
        vg = v_blocks[b_idx, h_idx, sel]
        s_sel = jnp.einsum('bhcd,bhckjd->bhckj', qc, kg, preferred_element_type=jnp.float32) * scale
        dist_sel = t[None, None, :, None, None] - (sel[..., None] * MOBA_BLOCK + offs)
        s_sel = jnp.where(valid[..., None],
                          s_sel - slopes[None, :, None, None, None] * dist_sel, -jnp.inf)
        k_own = lax.dynamic_index_in_dim(k_blocks, i_blk, axis=2, keepdims=False)
        v_own = lax.dynamic_index_in_dim(v_blocks, i_blk, axis=2, keepdims=False)
        s_own = jnp.einsum('bhcd,bhjd->bhcj', qc, k_own, preferred_element_type=jnp.float32) * scale
        dist_own = t[:, None] - (i_blk * MOBA_BLOCK + offs)[None, :]
        s_own = jnp.where(dist_own[None, None] >= 0,
                          s_own - slopes[None, :, None, None] * dist_own[None, None], -jnp.inf)
        scores = jnp.concatenate(
            [s_sel.reshape(B_, MIX_HEADS, Q_CHUNK, topk * MOBA_BLOCK), s_own], axis=-1)
        p = jax.nn.softmax(scores, axis=-1).astype(v_blocks.dtype)
        p_sel = p[..., :topk * MOBA_BLOCK].reshape(B_, MIX_HEADS, Q_CHUNK, topk, MOBA_BLOCK)
        p_own = p[..., topk * MOBA_BLOCK:]
        return (jnp.einsum('bhckj,bhckjd->bhcd', p_sel, vg)
                + jnp.einsum('bhcj,bhjd->bhcd', p_own, v_own))

    out = lax.map(one_chunk, (q_chunks, jnp.arange(nc)))
    return out.transpose(1, 0, 3, 2, 4).reshape(B_, S_, MIX_WIDTH)

def setup_inputs(seed: int = 0) -> dict:
    key = jax.random.key(seed)
    keys = jax.random.split(key, 40)
    ks = iter([keys[i] for i in range(40)])
    f32 = jnp.float32

    def w(shape, fan_in, scale=1.0):
        return jax.random.normal(next(ks), shape, f32) * (scale * fan_in ** -0.5)

    def gain(shape):
        return 1.0 + 0.02 * jax.random.normal(next(ks), shape, f32)

    def small(shape, s):
        return s * jax.random.normal(next(ks), shape, f32)

    D, L = D_MODEL, DEPTH
    return {
        "x": jax.random.normal(next(ks), (BATCH, SEQ, D), f32),
        "mem": jax.random.normal(next(ks), (BATCH, MEM_TOKENS, D), f32),
        "ffn1_norm": gain((L, D)),
        "ffn1_w1": w((L, D, D_FF), D),
        "ffn1_w3": w((L, D, D_FF), D),
        "ffn1_w2": w((L, D_FF, D), D_FF),
        "mix_norm": gain((L, D)),
        "w_out": w((L, MIX_WIDTH + MEM_WIDTH, D), MIX_WIDTH + MEM_WIDTH),
        "mem_norm": gain((L, D)),
        "w_mem_kv": w((L, D, 2 * MEM_WIDTH), D),
        "mem_q_norm": gain((L, HEAD_DIM)),
        "mem_k_norm": gain((L, HEAD_DIM)),
        "ffn2_norm": gain((L, D)),
        "ffn2_w1": w((L, D, D_FF), D),
        "ffn2_w3": w((L, D, D_FF), D),
        "ffn2_w2": w((L, D_FF, D), D_FF),
        "rwkv_w_in": w((N_A, D, A_IN_WIDTH), D),
        "rwkv_mu": jax.random.uniform(next(ks), (N_A, SHIFT_WIDTH), f32),
        "rwkv_w0": jax.random.uniform(next(ks), (N_A, MIX_WIDTH), f32, -5.0, 0.0),
        "rwkv_w2": w((N_A, DECAY_LORA, MIX_WIDTH), DECAY_LORA, 0.5),
        "rwkv_a0": small((N_A, MIX_WIDTH), 0.5),
        "rwkv_a2": w((N_A, AAA_LORA, MIX_WIDTH), AAA_LORA, 0.5),
        "rwkv_g2": w((N_A, GATE_LORA, MIX_WIDTH), GATE_LORA),
        "rwkv_k_k": 0.85 + small((N_A, MIX_WIDTH), 0.05),
        "rwkv_k_a": 1.0 + small((N_A, MIX_WIDTH), 0.05),
        "rwkv_r_k": small((N_A, MIX_HEADS, HEAD_DIM), 0.1),
        "rwkv_ln_w": gain((N_A, MIX_WIDTH)),
        "rwkv_ln_b": small((N_A, MIX_WIDTH), 0.02),
        "kv_norm": gain((D,)),
        "w_kv": w((D, KV_WIDTH), D),
        "kv_k_norm": gain((HEAD_DIM,)),
        "moba_w_in": w((N_B, D, B_IN_WIDTH), D),
        "moba_q_norm": gain((N_B, HEAD_DIM)),
    }

def reference(x, mem, ffn1_norm, ffn1_w1, ffn1_w3, ffn1_w2, mix_norm, w_out,
              mem_norm, w_mem_kv, mem_q_norm, mem_k_norm,
              ffn2_norm, ffn2_w1, ffn2_w3, ffn2_w2,
              rwkv_w_in, rwkv_mu, rwkv_w0, rwkv_w2, rwkv_a0, rwkv_a2, rwkv_g2,
              rwkv_k_k, rwkv_k_a, rwkv_r_k, rwkv_ln_w, rwkv_ln_b,
              kv_norm, w_kv, kv_k_norm, moba_w_in, moba_q_norm):
    shared = None
    for l in range(DEPTH):
        x = x + 0.5 * swiglu_ffn(x, ffn1_norm[l], ffn1_w1[l], ffn1_w3[l], ffn1_w2[l])
        h = rms_norm(x, mix_norm[l])
        if l < N_A:
            proj = h @ rwkv_w_in[l]
            mix = rwkv7_mixer(proj[..., :SHIFT_WIDTH], rwkv_mu[l], rwkv_w0[l], rwkv_w2[l],
                              rwkv_a0[l], rwkv_a2[l], rwkv_g2[l], rwkv_k_k[l], rwkv_k_a[l],
                              rwkv_r_k[l], rwkv_ln_w[l], rwkv_ln_b[l])
            mem_q = proj[..., SHIFT_WIDTH:]
        else:
            j = l - N_A
            proj = h @ moba_w_in[j]
            k_blocks, v_blocks, k_mean = shared
            mix = moba_attention(proj[..., :MIX_WIDTH], k_blocks, v_blocks, k_mean, moba_q_norm[j])
            mem_q = proj[..., MIX_WIDTH:]
        mem_out = memory_attention(mem_q, mem, mem_norm[l], w_mem_kv[l], mem_q_norm[l], mem_k_norm[l])
        x = x + jnp.concatenate([mix, mem_out], axis=-1) @ w_out[l]
        x = x + 0.5 * swiglu_ffn(x, ffn2_norm[l], ffn2_w1[l], ffn2_w3[l], ffn2_w2[l])
        if l == N_A - 1:
            shared = shared_kv(x, kv_norm, w_kv, kv_k_norm)
    return x


_drawn_inputs = setup_inputs


def setup_inputs(seed=0):
    import zlib

    import numpy as np

    out = dict(_drawn_inputs(seed))
    spreads = {}
    factors = {'ffn1_norm': 4.203,
     'mix_norm': 2.978,
     'mem_norm': 8.0,
     'mem_q_norm': 8.0,
     'mem_k_norm': 8.0,
     'ffn2_norm': 5.704,
     'rwkv_w2': 3.736,
     'rwkv_k_k': 3.86,
     'rwkv_ln_w': 5.875,
     'rwkv_ln_b': 5.322,
     'kv_norm': 8.0,
     'kv_k_norm': 8.0,
     'moba_q_norm': 8.0}
    for name, (base, spread) in spreads.items():
        noise = np.random.default_rng([zlib.crc32(name.encode()), seed]).standard_normal(out[name].shape)
        drawn = base * np.exp(spread * noise) if base else spread * noise
        out[name] = __import__('jax').numpy.asarray(drawn.astype(out[name].dtype))
    for name, factor in factors.items():
        out[name] = (out[name] * factor).astype(out[name].dtype)
    return out
```

```python
from contextlib import ExitStack

import concourse.bass as bass
from concourse import mybir

F32 = mybir.dt.float32
F32R = mybir.dt.float32r
BF16 = mybir.dt.bfloat16
I32 = mybir.dt.int32
ALU = mybir.AluOpType
ACT = mybir.ActivationFunctionType
AX = mybir.AxisListType

P = 128
D = 1024
S = 256
DFF = 2752
KT = D // P
TT = S // P
HD = 64
NH = 12
MIX = NH * HD
MEMW = 4 * HD
NP_ = NH // 2
SHIFTW = 3 * MIX + 256
FULL = DFF // 256
TAIL = DFF - 256 * FULL
NJ = -(-DFF // P)
LASTROWS = DFF - P * (NJ - 1)
RING = 3
EPS = 1e-6
GN_EPS = 64e-5
DECAY = float.fromhex("0x1.368b2fc6f9609p-1")
SCALE = HD ** -0.5
FAR = 1e30


def build(nc, T, out):
    ctx = ExitStack()
    sems = {}

    def sem(name):
        if name not in sems:
            sems[name] = ctx.enter_context(nc.semaphore(name))
        return sems[name]

    base = [-(-nc.sbuf_base // 64) * 64]
    arena0 = base[0]

    def place(name, shape, dt, at=None):
        size = (2 if dt == BF16 else 4)
        for n in shape[1:]:
            size *= n
        size = -(-size // 64) * 64
        off = base[0] if at is None else at
        if at is None:
            base[0] += size
        assert off + size <= 229368, (name, off, size)
        return nc.alloc_sbuf_tensor_at(name, shape, dt, offset=off), off + size

    def sb(name, shape, dt=F32):
        return place(name, shape, dt)[0]

    raw = sb("raw", [P, RING, 2048])
    rings_at = base[0]
    whi = sb("whi", [P, 2 * RING, 1024], F32R)
    wlo = sb("wlo", [P, 2 * RING, 1024], F32R)
    rings_end = base[0]
    xT = sb("xT", [P, KT, S])
    h_at = base[0]
    hhi = sb("hhi", [P, KT, S], F32R)
    hlo = sb("hlo", [P, KT, S], F32R)
    sq = sb("sq", [P, KT, S])
    sq_end = base[0]
    kmT = sb("kmT", [P, 2, 2, S])
    vm = sb("vm", [P, 2, 2, MEMW])
    ident = sb("ident", [P, P])
    ones_col = sb("ones_col", [P, 1])
    head_sel = sb("head_sel", [P, 2])
    centre = sb("centre", [P, P])
    invmask = sb("invmask", [P, 7, P])
    z1mask = sb("z1mask", [P, P])
    tri = sb("tri", [P, 3, P])
    tri4 = sb("tri4", [P, 4, P])
    dist = sb("dist", [P, TT, S])
    prm = sb("prm", [P, 144])
    omu = sb("omu", [P, 32])
    stat = sb("stat", [P, 24, 24])
    ones_row = sb("ones_row", [P, P])
    zw = sb("zw", [P, P], BF16)
    zm = sb("zm", [P, 512], BF16)
    region = base[0]

    bank = [ctx.enter_context(nc.psum_tensor(f"bank{i}", [P, 512], F32)) for i in range(8)]

    at = region
    sg, at = place("sg", [P, 2, S], F32, at)
    g32, at = place("g32", [P, 2, S], F32, at)
    ghi, at = place("ghi", [P, 2, S], F32R, at)
    glo, at = place("glo", [P, 2, S], F32R, at)
    ffn_end = at
    kT, at = place("kT", [P, NP_, S], F32, at)
    vt2, at = place("vt2", [P, TT, MIX], F32, at)
    attn_at = at
    at = ffn_end
    xrow, at = place("xrow", [P, TT, D], F32, at)
    mrow, at = place("mrow", [P, TT, D], F32, at)
    prow, at = place("prow", [P, 2, P], F32, at)
    mT, at = place("mT", [P, KT, S], F32, at)
    mhi, at = place("mhi", [P, KT, S], F32R, at)
    mlo, at_start = place("mlo", [P, KT, S], F32R, at)
    at = region
    uk, at = place("uk", [P, NP_, S], F32, at)
    uv, at = place("uv", [P, NP_, S], F32, at)
    ua, at = place("ua", [P, NP_, S], F32, at)
    gT, at = place("gT", [P, NP_, S], F32, at)
    KR, at = place("KR", [P, 2 * NP_, 2, P], F32, at)
    vt, at = place("vt", [P, TT, MIX], F32, at)
    mq, at = place("mq", [P, 2, S], F32, at)
    wa, at = place("wa", [P, S], F32, at)
    gd, at = place("gd", [P, S], F32, at)
    la_at = at
    la, at = place("la", [P, MIX], F32, at)
    lg, at = place("lg", [P, MIX], F32, at)
    c12, at = place("c12", [P, 2 * NP_, 1], F32, at)
    sfin, at = place("sfin", [P, 2, NP_], F32, at)
    sT, at = place("sT", [P, NP_, HD], F32, at)
    pw_at = at
    pw, at = place("pw", [P, 2 * NP_, P + 1], F32, at)
    pr_at = at
    pr, at = place("pr", [P, 2 * NP_, P + 1], F32, at)
    kk_at = at
    kk, at = place("kk", [P, NP_, S], F32, at)
    ur_at = at
    ur, at = place("ur", [P, NP_, S], F32, at)
    rwkv_end = at
    bt, _e = place("bt", [P, MIX], F32, pr_at)
    ktp, _e = place("ktp", [P, MIX], F32, _e)
    assert _e <= kk_at
    rhsb, _e = place("rhsb", [P, NH, HD], F32, kk_at)
    uneg, _e = place("uneg", [P, NH, HD], F32, _e)
    assert _e <= ur_at
    yT, _e = place("yT", [P, NP_, S], F32, ur_at)
    dT, _e = place("dT", [P, NP_, S], F32, la_at)
    om, _e = place("om", [P, 2, S], F32, pw_at)
    LT, _e = place("LT", [P, 2 * NH, P], F32, rings_at)
    Zi, _e = place("Zi", [P, 2 * NH, P], F32, _e)
    Xi, _e = place("Xi", [P, 2 * NH, P], F32, _e)
    Ri, _e = place("Ri", [P, 2 * NH, P], F32, _e)
    assert _e <= rings_end
    MQ, _e = place("MQ", [P, 2 * NH, 2 * P], F32, h_at)
    assert _e <= sq_end
    at = attn_at
    qT, at = place("qT", [P, 4 * 2, S], F32, at)
    oT, at = place("oT", [P, 4 * 2, S], F32, at)
    attn_end = at
    prb, _e = place("prb", [P, 2, TT, S], F32, kk_at)
    prT, _e = place("prT", [P, 2, TT, S], F32, _e)
    sml, _e = place("sml", [P, 2, 8], F32, _e)
    assert attn_end <= kk_at and _e <= 229368, (attn_end, kk_at, _e)
    start_end = at_start
    assert max(start_end, attn_at, rwkv_end) <= 229368, (start_end, attn_at, rwkv_end)

    rowsA, rowsB = 72, 68
    G_FFN1, G_MIX, G_MEM, G_FFN2, G_KV = 0, 16, 32, 48, 64
    C_MU = rowsA
    C_W0, C_A0, C_KK, C_KA, C_RK, C_LNW, C_LNB = (rowsA + 20 + 6 * i for i in range(7))
    C_MQ, C_MK, C_KVK, C_BQ = rowsA + 62, rowsA + 64, rowsA + 66, rowsA + 67

    def col(c):
        return prm[:, c:c + 1]

    def fl(ap):
        return ap.rearrange("p a b -> p (a b)")

    def cols_of(w, c):
        return w.rearrange("(k p) c -> p k c", p=P)[:, :, 256 * c:256 * c + 256]

    W_IN_ORDER = [9, 3, 4, 5, 0, 1, 2, 6, 7, 8, 10]
    stream = []

    n_slot = [0]

    def take(n):
        n_slot[0] += n
        return n_slot[0] - n

    n_mem = take(4)
    n_ffn = {}
    n_ffn[0] = take(3 * (FULL + 1))
    n_win = take(11)
    n_wout = {0: take(4)}
    n_ffn[1] = take(3 * (FULL + 1))
    n_kv = take(6)
    n_ffn[2] = take(3 * (FULL + 1))
    n_bin = take(4)
    n_wout[1] = take(4)
    n_ffn[3] = take(3 * (FULL + 1))

    static = {}
    for l in range(2):
        for c in range(2):
            static[n_mem + 2 * l + c] = cols_of(T["w_mem_kv"][l], c)
        for c in range(4):
            static[n_wout[l] + c] = cols_of(T["w_out"][l], c)
    for i, c in enumerate(W_IN_ORDER):
        static[n_win + i] = cols_of(T["rwkv_w_in"][0], c)
    for c in range(6):
        static[n_kv + c] = cols_of(T["w_kv"], c)
    for c in range(4):
        static[n_bin + c] = cols_of(T["moba_w_in"][0], c)

    ffn_w = [(T[f"ffn{1 + i % 2}_w1"][i // 2], T[f"ffn{1 + i % 2}_w3"][i // 2], T[f"ffn{1 + i % 2}_w2"][i // 2])
             for i in range(4)]
    raw_ready = [sem(f"raw_ready{c}") for c in range(RING)]
    tail_ready = sem("tail_ready")
    hi_ready = [sem(f"hi_ready{u}") for u in range(2 * RING)]
    lo_ready = [sem(f"lo_ready{u}") for u in range(2 * RING)]
    unit_used = [sem(f"unit_used{u}") for u in range(2 * RING)]

    def raw8(n):
        return raw[:, n % RING, :].rearrange("p (k c) -> p k c", k=KT)

    def unit_src(n, half, rows):
        if rows:
            return raw[:, n % RING, 1024 * half:1024 * half + 1024]
        return raw8(n)[:, :, P * half:P * half + P]

    def unit_dst(ring, n, half, rows):
        u = ring[:, 2 * (n % RING) + half, :]
        return u if rows else u.rearrange("p (k c) -> p k c", k=KT)

    SLOT = {"kn0": 0, "kn1": 1, "kkn": 2, "bn": 3, "gn": 4, "mq0": 5, "kvn": 6, "bq": 7, "mq1": 8}
    TILES = {"kn0": 2, "kn1": 2, "kkn": 6, "bn": 6, "gn": 6, "mq0": 2, "kvn": 6, "bq": 6, "mq1": 2}
    STAT = {n: stat[:, SLOT[n], 0:4 * TILES[n]] for n in SLOT}
    mgv = [sq, sq]
    N_ROW_LOADS = 21
    UPD_LAST = 28
    NORM_WAITS = {"ffn0": [("head_done", 4)]}
    NORM_WAITS.update({n: [] for n in ("mix0", "ffn1", "kv", "mix1", "ffn3")})
    NORM_WAITS["ffn2"] = [(f"unit_used{2 * ((n_kv + 5) % RING) + 1}", (n_kv + 5) // RING + 1), ("head_done", 2 + 2 + 3 * NP_ + 2 + NP_)]

    def inst(par, ch, p):
        return NH * par + NP_ * ch + p

    INSTANCES = [(par, ch, p) for par in range(2) for ch in range(2) for p in range(NP_)]
    NG = 2 * NH // 4
    TRIANGLES = [(par, ch, p) for ch in range(2) for par in range(2) for p in range(NP_)]

    def part(par):
        return slice(HD * par, HD * par + HD)

    def tokens(ch):
        return slice(P * ch, P * ch + P)

    def mem_heads(l, q, o):
        return [(q[:, p, :], kmT[:, l, p, :], lambda kt, h=2 * p + e: vm[:, l, kt, HD * h:HD * h + HD], o[:, p, :], e, None)
                for p in range(2) for e in range(2)]

    HEADS = {
        "at0": mem_heads(0, mq, om),
        "at1": [(qT[:, p, :], kT[:, p, :], lambda kt, h=2 * p + e: vt2[:, kt, HD * h:HD * h + HD], oT[:, p, :], e,
                 2.0 ** (-8.0 * (2 * p + e + 1) / NH)) for p in range(NP_) for e in range(2)]
        + mem_heads(1, qT[:, NP_:NP_ + 2, :], oT[:, NP_:NP_ + 2, :]),
    }
    U_TILES = []
    for c in W_IN_ORDER:
        U_TILES.append((wa[:, :], gd[:, :]) if c == 9 else
                       None if c == 10 else
                       tuple((ur, uk, uv)[c // 3][:, 2 * (c % 3) + half, :] for half in range(2)))

    SQ_COUNT = {"kn0": 1, "kn1": 1, "kkn": NP_, "bn": NP_, "gn": 3, "mq0": 1, "kvn": 3, "bq": 3, "mq1": 1}
    START, total = {}, {}
    for name in ("kn0", "kn1", "kkn", "bn", "gn", "mq0", "kvn", "bq", "mq1"):
        nt = TILES[name]
        for what, n in (("sq", SQ_COUNT[name]), ("stat", 1), ("var", 0 if name == "bn" else 1),
                        ("std", 0 if name == "bn" else 1), ("wide", 1), ("rb", -(-nt // 2)), ("done", nt)):
            START[name, what] = total.get(what, 0)
            total[what] = total.get(what, 0) + n

    def head_count(name, what, n):
        return sem(f"head_{what}"), START[name, what] + n

    def attn_count(name, what, n):
        heads0 = len(HEADS["at0"])
        return sem(f"attn_{what}"), n + (0 if name == "at0" else heads0 // 2 if what == "o" else heads0)

    block = ctx.enter_context(nc.Block())

    upd = {"load": 4, "ffn0": 8, "mix0": 12, "ffn1": 16, "ffn2": 20, "mix1": 24, "ffn3": 28}
    norm_no = {"ffn0": 0, "mix0": 1, "ffn1": 2, "kv": 3, "ffn2": 4, "mix1": 5, "ffn3": 6}
    norm_after = {"ffn0": "load", "mix0": "ffn0", "ffn1": "mix0", "kv": "ffn1", "ffn2": "ffn1", "mix1": "ffn2",
                  "ffn3": "mix1"}
    norm_gain = {"ffn0": G_FFN1, "mix0": G_MIX, "ffn1": G_FFN2, "kv": G_KV, "ffn2": G_FFN1 + 8,
                 "mix1": G_MIX + 8, "ffn3": G_FFN2 + 8}

    @block.sync
    def _(sp):
        x2 = T["x"][0].rearrange("(t p) d -> p t d", p=P)
        m2 = T["mem"][0].rearrange("(t p) d -> p t d", p=P)
        sp.dma_start(mrow[:, :, :], m2).then_inc(sem("mem_loaded"), 16)
        r = 0
        for name, rows in (("ffn1_norm", 16), ("mix_norm", 16), ("mem_norm", 16), ("ffn2_norm", 16), ("kv_norm", 8)):
            src = T[name].rearrange("l (r c) -> (l r) c", c=P) if name != "kv_norm" else T[name].rearrange("(r c) -> r c", c=P)
            sp.dma_start(prow[r:r + rows, 0, :], src).then_inc(sem("rows_loaded"), 16)
            r += rows
        r = 0
        for name in ("rwkv_mu", "rwkv_w0", "rwkv_a0", "rwkv_k_k", "rwkv_k_a"):
            src = T[name][0].rearrange("(r c) -> r c", c=P)
            sp.dma_start(prow[r:r + src.shape[0], 1, :], src).then_inc(sem("rows_loaded"), 16)
            r += src.shape[0]
        sp.dma_start(prow[r:r + 6, 1, :], T["rwkv_r_k"][0].rearrange("(r e) c -> r (e c)", e=2)).then_inc(sem("rows_loaded"), 16)
        r += 6
        for name in ("rwkv_ln_w", "rwkv_ln_b"):
            sp.dma_start(prow[r:r + 6, 1, :], T[name][0].rearrange("(r c) -> r c", c=P)).then_inc(sem("rows_loaded"), 16)
            r += 6
        for name in ("mem_q_norm", "mem_k_norm"):
            for e in range(2):
                sp.dma_start(prow[r:r + 2, 1, HD * e:HD * e + HD], T[name]).then_inc(sem("rows_loaded"), 16)
            r += 2
        for e in range(2):
            sp.dma_start(prow[r:r + 1, 1, HD * e:HD * e + HD], T["kv_k_norm"].rearrange("(a c) -> a c", a=1)).then_inc(sem("rows_loaded"), 16)
            sp.dma_start(prow[r + 1:r + 2, 1, HD * e:HD * e + HD], T["moba_q_norm"]).then_inc(sem("rows_loaded"), 16)

        def load_slot(n, src, dst=None):
            if n >= RING:
                sp.wait_ge(lo_ready[2 * (n % RING) + 1], n // RING)
            sp.dma_start(raw8(n) if dst is None else dst, src).then_inc(raw_ready[n % RING], 16)

        def load_ffn(f):
            w1, w3, w2 = ffn_w[f]
            n0 = n_ffn[f]
            w1v = w1.rearrange("(k p) c -> p k c", p=P)
            w3v = w3.rearrange("(k p) c -> p k c", p=P)
            rows2 = [raw[:, (n0 + 2) % RING, :].rearrange("p (j d) -> p j d", j=2)]
            with sp.Fori(0, FULL) as t:
                for c, wv in ((0, w1v), (1, w3v)):
                    n = n0 + c
                    sp.wait_ge(lo_ready[2 * (n % RING) + 1], t + n // RING)
                    sp.dma_start(raw8(n), wv[:, :, bass.ds(t * 256, 256)]).then_inc(raw_ready[n % RING], 16)
                n = n0 + 2
                sp.wait_ge(lo_ready[2 * (n % RING) + 1], t + n // RING)
                sp.dma_start(rows2[0], w2[bass.ds(t * 256, 256), :].rearrange("(j p) d -> p j d", p=P))\
                    .then_inc(raw_ready[n % RING], 16)
            n = n0 + 3 * FULL
            load_slot(n, w1v[:, :, 256 * FULL:DFF], raw8(n)[:, :, 0:TAIL])
            load_slot(n + 1, w3v[:, :, 256 * FULL:DFF], raw8(n + 1)[:, :, 0:TAIL])
            load_slot(n + 2, w2[256 * FULL:256 * FULL + P, :], raw[:, (n + 2) % RING, 0:1024])
            sp.dma_start(raw[0:LASTROWS, (n + 2) % RING, 1024:2048], w2[DFF - LASTROWS:DFF, :]).then_inc(tail_ready, 16)

        for n in range(n_mem, n_mem + 4):
            load_slot(n, static[n])
            if n == n_mem:
                sp.dma_start(xrow[:, :, :], x2).then_inc(sem("x_loaded"), 16)
        load_ffn(0)
        sp.wait_ge(*head_count("kn1", "done", 2))
        sp.wait_ge(sem("x_ready"), 4)
        sp.dma_start(la[0:HD, :], T["rwkv_w2"][0]).then_inc(sem("lora_loaded"), 16)
        sp.dma_start(la[HD:P, :], T["rwkv_a2"][0]).then_inc(sem("lora_loaded"), 16)
        sp.dma_start(lg[:, :], T["rwkv_g2"][0]).then_inc(sem("lora_loaded"), 16)
        for n in range(n_win, n_win + 11):
            load_slot(n, static[n])
        for n in range(n_wout[0], n_wout[0] + 4):
            load_slot(n, static[n])
        load_ffn(1)
        for n in range(n_kv, n_kv + 6):
            load_slot(n, static[n])
        load_ffn(2)
        for n in range(n_bin, n_bin + 4):
            load_slot(n, static[n])
        for n in range(n_wout[1], n_wout[1] + 4):
            load_slot(n, static[n])
        load_ffn(3)
        for t in range(TT):
            sp.wait_ge(sem("out_rows_ready"), 2 * t + 2)
            sp.dma_start(out[0, P * t:P * t + P, :], xrow[:, t, :]).then_inc(sem("stored"), 16)
        sp.wait_ge(sem("stored"), 16 * TT)


    def slot_done(eng, n):
        eng.wait_ge(unit_used[2 * (n % RING) + 1], n // RING + 1)

    def pool_rwkv(pool):
        slot_done(pool, n_win + 10)
        nc.gpsimd.memset(fl(LT[:, :, :]), 0.0).then_inc(sem("lt_step"), 1)
        pool.wait_ge(sem("lt_step"), 1)
        nc.gpsimd.affine_select(out=LT[:, :, :], in_=LT[:, :, :], compare_op=ALU.not_equal, fill=1.0, base=0,
                                pattern=[[0, 2 * NH], [-1, P]], channel_multiplier=1).then_inc(sem("lt_unit"), 1)
        pool.wait_ge(*head_count("bn", "done", NP_))
        nc.gpsimd.memset(MQ[:, :, :], 0.0).then_inc(sem("mq_zero"), 1)

    @block.gpsimd
    def _(pool):
        made = sem("const_step")
        n = [0]

        def step(ins):
            n[0] += 1
            ins.then_inc(made, 1)

        def done():
            pool.wait_ge(made, n[0])

        def diag(ap, pattern, fill, keep=ALU.not_equal, cbase=0, mult=1):
            step(nc.gpsimd.affine_select(out=ap, in_=ap, compare_op=keep, fill=fill, base=cbase, pattern=pattern,
                                         channel_multiplier=mult))

        step(nc.gpsimd.memset(ident[:, :], 0.0))
        step(nc.gpsimd.memset(ones_col[:, :], 1.0))
        done()
        diag(ident[:, :], [[-1, P]], 1.0)
        done()
        nc.gpsimd.memset(head_sel[:, :], 1.0).then_inc(made, 1)
        n[0] += 1
        done()
        diag(head_sel[:, :], [[-HD, 2]], 0.0, ALU.is_ge)
        done()
        step(nc.gpsimd.affine_select(out=head_sel[:, :], in_=head_sel[:, :], compare_op=ALU.is_ge, fill=0.0,
                                     base=HD - 1, pattern=[[HD, 2]], channel_multiplier=-1))
        done()
        nc.gpsimd.memset(zw[:, :], 0.0).then_inc(sem("base_consts"), 1)
        nc.gpsimd.memset(zm[:, :], 0.0).then_inc(sem("base_consts"), 1)
        step(nc.gpsimd.memset(centre[:, :], -1.0 / HD))
        step(nc.gpsimd.memset(invmask[:, :, :], 0.0))
        step(nc.gpsimd.memset(z1mask[:, :], 0.0))
        step(nc.gpsimd.memset(tri[:, :, :], 1.0))
        step(nc.gpsimd.memset(tri4[:, :, :], 1.0))
        step(nc.gpsimd.iota(fl(dist[:, :, :]), pattern=[[P, TT], [-1, S]], base=0, channel_multiplier=1,
                            allow_small_or_imprecise_dtypes=True))
        done()
        v = centre[:, :].rearrange("p (e c) -> p e c", e=2)
        diag(v, [[-HD, 2], [0, HD]], 0.0, ALU.is_ge)
        done()
        step(nc.gpsimd.affine_select(out=v, in_=v, compare_op=ALU.is_ge, fill=0.0, base=HD - 1,
                                     pattern=[[HD, 2], [0, HD]], channel_multiplier=-1))
        done()
        diag(centre[:, :], [[-1, P]], 1.0 - 1.0 / HD)
        for q in range(7):
            s = 1 << q
            nb = P // (2 * s)
            left = invmask[:, q, :].rearrange("p (b e c) -> p b e c", e=2, c=s)[:, :, 0, :]
            step(nc.gpsimd.memset(left, -1.0))
            done()
            step(nc.gpsimd.affine_select(out=left, in_=left, compare_op=ALU.is_ge, fill=0.0, base=-s,
                                         pattern=[[-2 * s, nb], [0, s]], channel_multiplier=1))
            done()
            step(nc.gpsimd.affine_select(out=left, in_=left, compare_op=ALU.is_ge, fill=0.0, base=2 * s - 1,
                                         pattern=[[2 * s, nb], [0, s]], channel_multiplier=-1))
            done()
            diag(invmask[:, q, :], [[-1, P]], 1.0)
        odd = z1mask[:, :].rearrange("p (b e) -> p b e", e=2)[:, :, 1]
        step(nc.gpsimd.affine_select(out=odd, in_=odd, compare_op=ALU.not_equal, fill=-1.0, base=0,
                                     pattern=[[-2, P // 2]], channel_multiplier=1))
        done()
        diag(z1mask[:, :], [[-1, P]], 1.0)
        for q, op in ((0, ALU.is_ge), (1, ALU.is_gt), (2, ALU.is_ge)):
            step(nc.gpsimd.affine_select(out=tri[:, q, :], in_=tri[:, q, :], compare_op=op, fill=0.0, base=0,
                                         pattern=[[1, P]], channel_multiplier=-1))
        step(nc.gpsimd.affine_select(out=tri4[:, :, :], in_=tri4[:, :, :], compare_op=ALU.is_gt, fill=0.0, base=0,
                                     pattern=[[0, 4], [1, P]], channel_multiplier=-1))
        step(nc.gpsimd.affine_select(out=fl(dist[:, :, :]), in_=fl(dist[:, :, :]), compare_op=ALU.is_ge, fill=FAR, base=0,
                                     pattern=[[P, TT], [-1, S]], channel_multiplier=1))
        done()
        nc.gpsimd.memset(ones_row[:, :], 1.0).then_inc(sem("all_consts"), 1)
        pool_rwkv(pool)


    @block.tensor
    def _(pe):
        def transpose(o, i, n=P):
            return nc.tensor.transpose(o, i, ident[0:n, 0:n])

        def product(o, a_hi, a_lo, b_hi, b_lo, first, last, open_=False):
            nc.tensor.matmul(o, a_hi, b_hi, start=first, stop=False, skip_group_check=open_)
            nc.tensor.matmul(o, a_hi, b_lo, start=False, stop=False, skip_group_check=open_)
            return nc.tensor.matmul(o, a_lo, b_hi, start=False, stop=last, skip_group_check=open_)

        def fp_unit(o, u, width=P, h=(hhi, hlo)):
            for k in range(KT):
                m = product(o, whi[:, u, P * k:P * k + width], wlo[:, u, P * k:P * k + width],
                            h[0][:, k, :], h[1][:, k, :], k == 0, k == KT - 1)
            return m

        def fp_slot(n, b, h=(hhi, hlo)):
            for half in range(2):
                u = 2 * (n % RING) + half
                pe.wait_ge(lo_ready[u], n // RING + 1)
                m = fp_unit(bank[b][:, S * half:S * half + S], u, h=h)
                m.then_inc(unit_used[u], 1)

        def tp_slot(n, b, h=(hhi, hlo)):
            u = 2 * (n % RING)
            pe.wait_ge(lo_ready[u + 1], n // RING + 1)
            for t in range(TT):
                for k in range(KT if t < TT - 1 else KT - 1):
                    product(bank[b][:, 256 * t:256 * t + 256], h[0][:, k, P * t:P * t + P],
                            h[1][:, k, P * t:P * t + P], whi[:, u:u + 2, P * k:P * k + P],
                            wlo[:, u:u + 2, P * k:P * k + P], k == 0, k == KT - 1, t == TT - 1)
            for half in range(2):
                k, c = KT - 1, 256 * (TT - 1) + P * half
                product(bank[b][:, c:c + P], h[0][:, k, P * t:P * t + P], h[1][:, k, P * t:P * t + P],
                        whi[:, u + half, P * k:P * k + P], wlo[:, u + half, P * k:P * k + P], False, True, True)\
                    .then_inc(unit_used[u + half], 1)

        def head_stats(name, nt, src, b, rb, at0=0, ready=None):
            pe.wait_ge(*head_count(name, "sq", nt if ready is None else ready))
            for t in range(TT):
                for p in range(nt):
                    m = nc.tensor.matmul(bank[b][:, 2 * nt * t + 2 * p:2 * nt * t + 2 * p + 2],
                                         src[:, p, P * t:P * t + P], head_sel[:, :], start=True, stop=True)
            m.then_inc(sem("head_stat"), 1)

        def head_spread(name, nt, src, rb):
            pe.wait_ge(*head_count(name, "wide", 1))
            wide = fl(src).rearrange("p (t c) -> p t c", t=TT)
            for p in range(nt):
                if p % 2 == 0 and p // 2 >= len(rb):
                    pe.wait_ge(*head_count(name, "done", 2 * (p // 2 - len(rb)) + 2))
                for t in range(TT):
                    c = S * (p % 2) + P * t
                    m = transpose(bank[rb[p // 2 % len(rb)]][:, c:c + P], wide[:, t, P * p:P * p + P])
                if p % 2 or p == nt - 1:
                    m.then_inc(sem("head_rb"), 1)

        def norm(name):
            i = norm_no[name]
            for j in range(4):
                pe.wait_ge(sem("sq_ready"), 4 * i + j + 1)
                for k in (2 * j, 2 * j + 1):
                    for t in range(TT):
                        m = nc.tensor.matmul(bank[6][:, t:t + 1], sq[:, k, P * t:P * t + P], ones_col[:, :],
                                             start=(k == 0 and t == 0), stop=(k == KT - 1), skip_group_check=True)
            m.then_inc(sem("norm_stat"), 1)
            pe.wait_ge(sem("norm_rstd"), i + 1)
            for t in range(TT):
                m = transpose(bank[7][:, P * t:P * t + P], stat[:, 16, 2 * i + t:2 * i + t + 1].broadcast_to([P, P]))
            m.then_inc(sem("norm_rb"), 1)
            pe.wait_ge(sem("h_ready"), 8 * i + 8)

        def ffn(f):
            n0, j0 = n_ffn[f], NJ * f
            u1, u3, u2 = (2 * ((n0 + c) % RING) for c in range(3))
            r1, r3, r2 = ((n0 + c) // RING for c in range(3))

            def h(j, half, r, width=P):
                if not (isinstance(j, int) and j == 0):
                    pe.wait_ge(sem("g32_done"), j0 + j)
                b = bank[4 + half]
                pe.wait_ge(lo_ready[u1 + half], r + r1 + 1)
                fp_unit(b[0:width, 0:S], u1 + half, width).then_inc(unit_used[u1 + half], 1)
                pe.wait_ge(lo_ready[u3 + half], r + r3 + 1)
                fp_unit(b[0:width, S:2 * S], u3 + half, width).then_inc(unit_used[u3 + half], 1)

            def o(j, half, r, rows=P, last=False):
                u = u2 + half
                pe.wait_ge(sem("g_ready"), j0 + j + 1)
                pe.wait_ge(lo_ready[u], r + r2 + 1)
                for d in range(KT):
                    m = product(bank[d // 2][:, S * (d % 2):S * (d % 2) + S], whi[0:rows, u, P * d:P * d + P],
                                wlo[0:rows, u, P * d:P * d + P], ghi[0:rows, half, :], glo[0:rows, half, :],
                                False, last, True)
                m.then_inc(unit_used[u], 1)

            for b in range(4):
                nc.tensor.matmul(bank[b][:, :], zw[:, :], zm[:, :], start=True, stop=False, skip_group_check=True)
            h(0, 0, 0)
            with pe.Fori(0, FULL) as t:
                h(2 * t + 1, 1, t)
                o(2 * t, 0, t)
                h(2 * t + 2, 0, t + 1)
                o(2 * t + 1, 1, t)
            h(NJ - 1, 1, FULL, LASTROWS)
            o(NJ - 2, 0, FULL)
            o(NJ - 1, 1, FULL, LASTROWS, True)

        pe.wait_ge(sem("base_consts"), 2)
        pe.wait_ge(sem("rows_loaded"), 16 * N_ROW_LOADS)
        transpose(bank[7][:, 0:rowsA], prow[0:rowsA, 0, :], rowsA)
        transpose(bank[7][:, rowsA:rowsA + rowsB], prow[0:rowsB, 1, :], rowsB).then_inc(sem("prm_t"), 1)
        for j in range(4):
            if j == 0:
                pe.wait_ge(sem("mem_scaled"), 2)
            for k in (2 * j, 2 * j + 1):
                for t in range(TT):
                    c = S * (k % 2) + P * t
                    m = transpose(bank[j][:, c:c + P], mrow[:, t, P * k:P * k + P])
            m.then_inc(sem("m_t"), 1)
        for j in range(4):
            if j == 0:
                pe.wait_ge(sem("x_loaded"), 16)
            b = 4 + j % 2
            if j >= 2:
                pe.wait_ge(sem("x_ready"), j - 1)
            for k in (2 * j, 2 * j + 1):
                for t in range(TT):
                    c = S * (k % 2) + P * t
                    m = transpose(bank[b][:, c:c + P], xrow[:, t, P * k:P * k + P])
            m.then_inc(sem("x_t"), 1)
        for l in range(2):
            hm = (hhi, hlo) if l == 0 else (mhi, mlo)
            pe.wait_ge(sem("mem_h"), 8 * l + 8)
            fp_slot(n_mem + 2 * l, 2 * l, hm)
            tp_slot(n_mem + 2 * l + 1, 2 * l + 1, hm)
        for l in range(2):
            head_stats(f"kn{l}", 2, sq[:, 2 * l:2 * l + 2, :], 6, None, ready=1)
            head_spread(f"kn{l}", 2, sq[:, 2 * l:2 * l + 2, :], [7])
            pe.wait_ge(*head_count(f"kn{l}", "done", 2))
        pe.wait_ge(sem("mem_v_done"), 2)

        norm("ffn0")
        ffn(0)
        def attend(name):
            heads = HEADS[name]

            def scores(n):
                q, k, _, _, e, _ = heads[n]
                if n >= 2:
                    pe.wait_ge(*attn_count(name, "exp", n - 1))
                for t in range(TT):
                    m = nc.tensor.matmul(bank[n % 2][:, S * t:S * t + S], q[part(e), tokens(t)], k[part(e), :],
                                         start=True, stop=True)
                m.then_inc(sem("attn_scores"), 1)

            def turn(n):
                pe.wait_ge(*attn_count(name, "probs", n + 1))
                if n >= 2:
                    pe.wait_ge(*attn_count(name, "turned", n - 1))
                for kt in range(TT):
                    for t in range(TT):
                        c = S * kt + P * t
                        m = transpose(bank[2 + n % 2][:, c:c + P], prb[:, n % 2, t, tokens(kt)])
                m.then_inc(sem("attn_turn"), 1)

            def values(n):
                _, _, v, _, e, _ = heads[n]
                pe.wait_ge(*attn_count(name, "turned", n + 1))
                if n >= 4:
                    pe.wait_ge(*attn_count(name, "o", n // 2 - 1))
                for kt in range(TT):
                    m = nc.tensor.matmul(bank[4 + n // 2 % 2][part(e), 0:S], v(kt), prT[:, n % 2, kt, :],
                                         start=(kt == 0), stop=(kt == TT - 1))
                m.then_inc(sem("attn_values"), 1)

            scores(0)
            for n in range(len(heads)):
                if n + 1 < len(heads):
                    scores(n + 1)
                if n >= 1:
                    values(n - 1)
                turn(n)
            values(len(heads) - 1)

        def w_out(l):
            pe.wait_ge(sem(f"mixed{l}"), KT)
            for c in range(4):
                fp_slot(n_wout[l] + c, c)

        pe.wait_ge(sem("all_consts"), 1)
        norm("mix0")

        def w_in(i):
            if i >= 4:
                pe.wait_ge(sem("win_free"), i - 3)
            fp_slot(n_win + i, i % 4)

        def loras():
            pe.wait_ge(sem("lora_loaded"), 48)
            pe.wait_ge(sem("lora_in"), 2)
            for p in range(NP_):
                if p >= 2:
                    pe.wait_ge(sem("a_ready"), p - 1)
                nc.tensor.matmul(bank[4 + p % 2][:, 0:S], la[0:HD, P * p:P * p + P], wa[0:HD, :], start=True, stop=True)
                nc.tensor.matmul(bank[6 + p % 2][:, 0:S], la[HD:P, P * p:P * p + P], wa[HD:P, :], start=True, stop=True)\
                    .then_inc(sem("lora_wa"), 1)
            pe.wait_ge(sem("a_ready"), NP_)
            for q in range(3):
                if q == 2:
                    pe.wait_ge(sem("g_out"), 1)
                for p in (2 * q, 2 * q + 1):
                    m = nc.tensor.matmul(bank[6 + q % 2][:, S * (p % 2):S * (p % 2) + S], lg[:, P * p:P * p + P], gd[:, :],
                                         start=True, stop=True)
                m.then_inc(sem("lora_g"), 1)

        def to_tokens(j, src, ch, q):
            if j >= 2:
                pe.wait_ge(sem("tp_out"), j - 1)
            for p in range(3):
                m = transpose(bank[4 + j % 2][:, P * p:P * p + P], src[:, 3 * q + p, tokens(ch)])
            m.then_inc(sem("tp_t"), 1)

        w_in(0)
        w_in(1)
        w_in(2)
        loras()
        w_in(3)
        w_in(4)
        w_in(5)
        pe.wait_ge(sem("g_out"), 3)
        head_stats("kkn", NP_, sq, 6, None)
        w_in(6)
        head_spread("kkn", NP_, sq[:, 0:NP_, :], [7, 6])
        for i in range(7, 11):
            w_in(i)
        pe.wait_ge(sem("win_free"), 10)
        pe.wait_ge(sem("a_ready"), NP_)
        for j in range(4):
            to_tokens(j, uv, j // 2, j % 2)
        head_stats("bn", NP_, sq, 6, None)
        head_spread("bn", NP_, sq[:, 0:NP_, :], [7, 6])
        pe.wait_ge(sem("powers_used"), 4)
        for j in range(4):
            to_tokens(4 + j, (ua, uk)[j // 2], 0, j % 2)

        def triangle(g):
            if g >= 2:
                pe.wait_ge(sem("lt_done"), g - 1)
            for q in range(4):
                par, ch, p = INSTANCES[4 * g + q]
                m = nc.tensor.matmul(bank[g % 2][:, P * q:P * q + P], ua[part(par), p, tokens(ch)],
                                     KR[part(par), 2 * p + ch, 0, :], start=True, stop=True)
            m.then_inc(sem("lt_ps"), 1)

        def first_blocks(g):
            pe.wait_ge(sem("z_done"), g + 1)
            if g >= 2:
                pe.wait_ge(sem("x_done"), g - 1)
            for q in range(4):
                m = transpose(bank[2 + g % 2][:, P * q:P * q + P], Zi[:, 4 * g + q, :])
            m.then_inc(sem("x1_t"), 1)

        triangle(0)
        triangle(1)
        for g in range(NG):
            if g + 2 < NG:
                first_blocks(g)
                triangle(g + 2)
            else:
                first_blocks(g)

        def level(lv, last=False):
            for g in range(NG):
                pe.wait_ge(sem("x_done"), NG * lv + g + 1)
                if g >= 2:
                    pe.wait_ge(sem("r_done"), NG * lv + g - 1)
                for q in range(4):
                    i = 4 * g + q
                    m = nc.tensor.matmul(bank[g % 2][:, P * q:P * q + P], LT[:, i, :], Xi[:, i, :], start=True, stop=True)
                m.then_inc(sem("inv_a"), 1)
            pe.wait_ge(sem("z_done"), NG * lv + NG)
            for g in range(NG):
                pe.wait_ge(sem("r_done"), NG * lv + g + 1)
                if not last:
                    if g >= 2:
                        pe.wait_ge(sem("x_done"), NG * lv + NG + g - 1)
                    for q in range(4):
                        i = 4 * g + q
                        m = nc.tensor.matmul(bank[2 + g % 2][:, P * q:P * q + P], Zi[:, i, :], Ri[:, i, :], start=True, stop=True)
                    m.then_inc(sem("inv_b"), 1)
                if g >= 2:
                    pe.wait_ge(sem("z_done"), NG * lv + NG + g - 1)
                for q in range(4):
                    i = 4 * g + q
                    m = nc.tensor.matmul(bank[4 + g % 2][:, P * q:P * q + P], Ri[:, i, :], Zi[:, i, :], start=True, stop=True)
                m.then_inc(sem("inv_c"), 1)

        with pe.Fori(0, 5) as lv:
            level(lv)
        level(5, True)

        def triangles(lo, hi):
            for n in range(lo, hi):
                par, ch, p = TRIANGLES[n]
                if n == 0:
                    pe.wait_ge(*head_count("bn", "done", NP_))
                if n >= 2:
                    pe.wait_ge(sem("nmq_done"), n - 1)
                b = bank[6 + n % 2]
                nc.tensor.matmul(b[:, 0:P], ua[part(par), p, tokens(ch)], KR[part(par), 2 * p + ch, 1, :],
                                 start=True, stop=True)
                nc.tensor.matmul(b[:, P:3 * P], uk[part(par), p, tokens(ch)], KR[part(par), 2 * p + ch, :, :], start=True, stop=True).then_inc(sem("nmq_ps"), 1)

        def rhs(ch, par):
            pe.wait_ge(sem("nmq_done"), NH * ch + NP_ * par + NP_)
            if ch:
                pe.wait_ge(sem("state"), 1)
            for p in range(NP_):
                i, h = inst(par, ch, p), 2 * p + par
                o = bank[par][:, HD * p:HD * p + HD]
                m = nc.tensor.matmul(o, MQ[:, i, 0:P], vt[:, ch, HD * h:HD * h + HD], start=True, stop=(ch == 0))
                if ch:
                    m = nc.tensor.matmul(o, KR[part(par), 2 * p + 1, 0, :], sT[part(par), p, :], start=False, stop=True)
            m.then_inc(sem("rhs_ps"), 1)

        def solve(ch, par):
            pe.wait_ge(sem("rhs_out"), 2 * ch + par + 1)
            if ch == 0 and par == 0:
                pe.wait_ge(sem("z_done"), NG * 7)
            for p in range(NP_):
                m = nc.tensor.matmul(bank[2 + par][:, HD * p:HD * p + HD], Zi[:, inst(par, ch, p), :], rhsb[:, NP_ * par + p, :],
                                     start=True, stop=True)
            m.then_inc(sem("u_ps"), 1)

        def outputs(ch):
            pe.wait_ge(sem("u_out"), 2 * ch + 2)
            if ch:
                pe.wait_ge(sem("y_out"), 2)
            for par in range(2):
                for p in range(NP_):
                    i, h = inst(par, ch, p), 2 * p + par
                    o = bank[4 + p // 3][part(par), P * (p % 3):P * (p % 3) + P]
                    nc.tensor.matmul(o, uneg[:, NP_ * par + p, :], LT[:, i, :], start=True, stop=False)
                    m = nc.tensor.matmul(o, vt[:, ch, HD * h:HD * h + HD], MQ[:, i, P:2 * P], start=False, stop=(ch == 0))
                    if ch:
                        m = nc.tensor.matmul(o, sT[part(par), p, :], KR[part(par), 2 * p + 1, 1, :], start=False, stop=True)
            m.then_inc(sem("y_ps"), 1)

        def state():
            pe.wait_ge(sem("u_out"), 2)
            for par in range(2):
                for p in range(NP_):
                    h = 2 * p + par
                    o = bank[0][part(par), HD * p:HD * p + HD]
                    nc.tensor.matmul(o, bt[:, HD * h:HD * h + HD], uneg[:, NP_ * par + p, :], start=True, stop=False)
                    m = nc.tensor.matmul(o, ktp[:, HD * h:HD * h + HD], vt[:, 0, HD * h:HD * h + HD], start=False, stop=True)
            m.then_inc(sem("s_ps"), 1)

        pe.wait_ge(sem("tp_out"), 8)
        triangles(0, NH)
        rhs(0, 0)
        rhs(0, 1)
        triangles(NH, NH + NP_)
        solve(0, 0)
        solve(0, 1)
        triangles(NH + NP_, 2 * NH)
        state()
        outputs(0)
        rhs(1, 0)
        rhs(1, 1)
        solve(1, 0)
        solve(1, 1)
        outputs(1)
        pe.wait_ge(sem("y_out"), 4)
        for q in range(3):
            for p in (2 * q, 2 * q + 1):
                m = nc.tensor.matmul(bank[q][:, S * (p % 2):S * (p % 2) + S], centre[:, :], yT[:, p, :], start=True, stop=True)
            m.then_inc(sem("centred"), 1)
        head_stats("gn", NP_, sq, 6, None, ready=3)
        head_spread("gn", NP_, sq[:, 0:NP_, :], [7, 6])
        pe.wait_ge(*head_count("gn", "done", NP_))
        head_stats("mq0", 2, sq[:, 0:2, :], 6, None, ready=1)
        head_spread("mq0", 2, sq[:, 0:2, :], [7])
        pe.wait_ge(*head_count("mq0", "done", 2))
        attend("at0")
        w_out(0)
        norm("ffn1")
        ffn(1)
        norm("kv")
        for c in range(6):
            if c >= 4:
                pe.wait_ge(sem("k_out"), c - 3)
            (fp_slot if c < 3 else tp_slot)(n_kv + c, c % 4)
        head_stats("kvn", NP_, sq, 6, None, ready=3)
        head_spread("kvn", NP_, sq[:, 0:NP_, :], [7, 6])
        pe.wait_ge(sem("v_out"), 3)
        norm("ffn2")
        ffn(2)
        norm("mix1")
        for c in range(4):
            fp_slot(n_bin + c, c)
        head_stats("bq", NP_, sq, 6, None, ready=3)
        head_spread("bq", NP_, sq[:, 0:NP_, :], [7, 6])
        pe.wait_ge(*head_count("bq", "done", NP_))
        head_stats("mq1", 2, sq[:, NP_:NP_ + 2, :], 6, None, ready=1)
        head_spread("mq1", 2, sq[:, NP_:NP_ + 2, :], [7])
        pe.wait_ge(*head_count("mq1", "done", 2))
        attend("at1")
        w_out(1)
        norm("ffn3")
        ffn(3)
        for t in range(TT):
            for half in range(2):
                b = 4 + 2 * t + half
                if t == 0 and half == 0:
                    pe.wait_ge(sem("x_ready"), UPD_LAST)
                for q in range(4):
                    k = 4 * half + q
                    m = transpose(bank[b][:, P * q:P * q + P], xT[:, k, P * t:P * t + P])
                m.then_inc(sem("out_t"), 1)

    @block.scalar
    def _(act):
        def split(n, half, r=None, rows=False, part=P, tail=False):
            u = 2 * (n % RING) + half
            if r is None:
                r = n // RING
            if tail:
                act.wait_ge(tail_ready, 16 * tail)
            else:
                act.wait_ge(raw_ready[n % RING], 16 * r + 16)
            if not (isinstance(r, int) and r == 0):
                act.wait_ge(unit_used[u], r)
            nc.scalar.activation(unit_dst(whi, n, half, rows)[0:part], unit_src(n, half, rows)[0:part], ACT.Copy)\
                .then_inc(hi_ready[u], 1)

        def split2(n):
            split(n, 0)
            split(n, 1)

        def root(name):
            act.wait_ge(*head_count(name, "var", 1))
            v = STAT[name]
            nc.scalar.activation(v, v, ACT.Sqrt).then_inc(sem("head_std"), 1)

        def norm(name):
            i = norm_no[name]
            if i:
                act.wait_ge(sem("h_ready"), 8 * i)
            for w, v in NORM_WAITS[name]:
                act.wait_ge(sem(w), v)
            for j in range(4):
                act.wait_ge(sem("x_ready"), upd[norm_after[name]] - 4 + j + 1)
                nc.scalar.activation(sq[:, 2 * j:2 * j + 2, :], xT[:, 2 * j:2 * j + 2, :], ACT.Square)\
                    .then_inc(sem("sq_ready"), 1)
            act.wait_ge(sem("norm_var"), i + 1)
            v = stat[:, 16, 2 * i:2 * i + 2]
            nc.scalar.activation(v, v, ACT.Sqrt).then_inc(sem("norm_std"), 1)
            for k in range(KT):
                act.wait_ge(sem("hf_ready"), 8 * i + k + 1)
                nc.scalar.activation(hhi[:, k, :], sq[:, k, :], ACT.Copy).then_inc(sem("hhi_ready"), 1)

        def ffn(f, following):
            n0, j0 = n_ffn[f], NJ * f
            q = [(n0 + c) // RING for c in range(3)]

            def silu(half, r, rows=P):
                act.wait_ge(unit_used[2 * ((n0 + 1) % RING) + half], r + q[1] + 1)
                nc.scalar.activation(sg[0:rows, half, :], bank[4 + half][0:rows, 0:S], ACT.Silu)\
                    .then_inc(sem("silu_done"), 1)

            def g_hi(j, half, rows=P):
                act.wait_ge(sem("g32_done"), j0 + 1 + j + 1)
                nc.scalar.activation(ghi[0:rows, half, :], g32[0:rows, half, :], ACT.Copy).then_inc(sem("ghi_done"), 1)

            for c, half in ((0, 0), (1, 0), (0, 1), (1, 1), (2, 0)):
                split(n0 + c, half, rows=(c == 2))
            with act.Fori(0, FULL) as t:
                silu(0, t)
                split(n0, 0, t + 1 + q[0])
                g_hi(2 * t, 0)
                split(n0 + 1, 0, t + 1 + q[1])
                split(n0 + 2, 1, t + q[2], True)
                silu(1, t)
                split(n0, 1, t + 1 + q[0])
                g_hi(2 * t + 1, 1)
                split(n0 + 1, 1, t + 1 + q[1])
                split(n0 + 2, 0, t + 1 + q[2], True)
            silu(0, FULL)
            g_hi(NJ - 2, 0)
            split(n0 + 2, 1, FULL + q[2], True, LASTROWS, tail=f + 1)
            silu(1, FULL, LASTROWS)
            g_hi(NJ - 1, 1, LASTROWS)
            if following is not None:
                split2(following)

        act.wait_ge(sem("mem_loaded"), 16)
        for t in range(TT):
            m = nc.scalar.activation(sq[:, 4 * t:4 * t + 4, :].rearrange("p a b -> p (a b)"), mrow[:, t, :], ACT.Square,
                                     accum_out=stat[:, 17, t:t + 1])
        m.then_inc(sem("mem_ss"), 1)
        act.wait_ge(sem("mem_var"), 1)
        nc.scalar.activation(stat[:, 17, 0:2], stat[:, 17, 0:2], ACT.Sqrt).then_inc(sem("mem_std"), 1)
        split2(n_mem)
        for l in range(2):
            dst = hhi if l == 0 else mhi
            for k in range(KT):
                act.wait_ge(sem("mg_ready"), 8 * l + k + 1)
                nc.scalar.activation(dst[:, k, :], mgv[l][:, k, :], ACT.Copy).then_inc(sem("mhi_ready"), 1)
            if l == 0:
                split2(n_mem + 1)
                split2(n_mem + 2)
        split2(n_mem + 3)
        for l in range(2):
            act.wait_ge(sem("mem_k_out"), l + 1)
            act.wait_ge(sem("mem_h"), 16)
            nc.scalar.activation(sq[:, 2 * l:2 * l + 2, :], kmT[:, l, :, :], ACT.Square).then_inc(sem("head_sq"), 1)
            slot_done(act, n_mem + 2 * l + 1)
            nc.scalar.activation(fl(vm[:, l, :, :]), bank[2 * l + 1][:, :], ACT.Copy).then_inc(sem("mem_v_done"), 1)
            root(f"kn{l}")
        norm("ffn0")
        ffn(0, n_win)
        def attend(name):
            heads = HEADS[name]

            def exps(n):
                _, _, _, _, _, slope = heads[n]
                act.wait_ge(*attn_count(name, "max", n + 1))
                for t in range(TT):
                    src = bank[n % 2][:, S * t:S * t + S] if slope is None else prb[:, n % 2, t, :]
                    m = nc.scalar.activation(prb[:, n % 2, t, :], src, ACT.Exp, bias=sml[:, n % 2, t:t + 1], scale=SCALE,
                                             accum_out=sml[:, n % 2, 2 + t:3 + t])
                m.then_inc(sem("attn_exp"), 1)

            def turned(n):
                act.wait_ge(*attn_count(name, "turn", n + 1))
                if n >= 2:
                    act.wait_ge(*attn_count(name, "values", n - 1))
                nc.scalar.activation(prT[:, n % 2, :, :], bank[2 + n % 2][:, :].rearrange("p (t s) -> p t s", t=TT), ACT.Copy)\
                    .then_inc(sem("attn_turned"), 1)

            exps(0)
            for n in range(len(heads)):
                if n + 1 < len(heads):
                    exps(n + 1)
                turned(n)

        def high(l, k, src, w, v):
            act.wait_ge(w, v)
            nc.scalar.activation(hhi[:, k, :], src, ACT.Copy).then_inc(sem(f"mixhi{l}"), 1)

        def split_w_out(l):
            for c in range(3):
                split2(n_wout[l] + c)

        norm("mix0")
        split2(n_win + 1)
        split2(n_win + 2)

        def w_in_out(i):
            slot_done(act, n_win + i)
            b = bank[i % 4]
            for half in range(2):
                c = W_IN_ORDER[i] * 2 + half
                m = nc.scalar.activation(U_TILES[i][half], b[:, S * half:S * half + S], ACT.Copy, scale=omu[:, c:c + 1])
            m.then_inc(sem("shift_a"), 1)
            if i + 3 < 11:
                split2(n_win + i + 3)

        w_in_out(0)
        act.wait_ge(sem("win_free"), 1)
        nc.scalar.activation(wa[0:HD, :], wa[0:HD, :], ACT.Tanh).then_inc(sem("lora_in"), 1)
        nc.scalar.activation(gd[:, :], gd[:, :], ACT.Sigmoid).then_inc(sem("lora_in"), 1)
        w_in_out(1)
        w_in_out(2)
        for p in range(NP_):
            act.wait_ge(sem("lora_wa"), p + 1)
            nc.scalar.activation(pw[:, 2 * p:2 * p + 2, 1:P + 1], bank[4 + p % 2][:, 0:S].rearrange("p (c t) -> p c t", c=2), ACT.Sigmoid,
                                 bias=col(C_W0 + p)).then_inc(sem("lw_ready"), 1)
            nc.scalar.activation(ua[:, p, :], bank[6 + p % 2][:, 0:S], ACT.Sigmoid, bias=col(C_A0 + p)).then_inc(sem("a_ready"), 1)
        for q in range(3):
            act.wait_ge(sem("lora_g"), q + 1)
            nc.scalar.activation(fl(gT[:, 2 * q:2 * q + 2, :]), bank[6 + q % 2][:, :], ACT.Copy).then_inc(sem("g_out"), 1)
        w_in_out(3)
        act.wait_ge(sem("win_free"), 4)
        for p in range(NP_):
            nc.scalar.activation(sq[:, p, :], uk[:, p, :], ACT.Square, scale=col(C_KK + p)).then_inc(sem("head_sq"), 1)
        w_in_out(4)
        w_in_out(5)
        root("kkn")
        w_in_out(6)
        act.wait_ge(sem("cum_ready"), 1)
        nc.scalar.activation(sfin[:, 1, :], c12[:, 1::2, 0], ACT.Exp, scale=-DECAY).then_inc(sem("mid_power"), 1)
        nc.scalar.activation(pr[:, :, :], pw[:, :, :], ACT.Exp, scale=-DECAY).then_inc(sem("powers"), 1)
        nc.scalar.activation(pw[:, :, :], pw[:, :, :], ACT.Exp, scale=DECAY).then_inc(sem("powers"), 1)
        for i in range(7, 10):
            w_in_out(i)
        slot_done(act, n_win + 10)
        nc.scalar.activation(fl(mq[:, :, :]), bank[10 % 4][:, :], ACT.Copy).then_inc(sem("mq_out"), 1)
        for j in range(8):
            act.wait_ge(sem("tp_t"), j + 1)
            if j == 4:
                act.wait_ge(sem("powers_used"), 4)
            q = j % 2
            dst = vt[:, j // 2, 384 * q:384 * q + 384] if j < 4 else (bt, ktp)[j // 2 - 2][:, 384 * q:384 * q + 384]
            nc.scalar.activation(dst, bank[4 + j % 2][:, 0:384], ACT.Copy).then_inc(sem("tp_out"), 1)
        for g in range(NG):
            act.wait_ge(sem("x1_t"), g + 1)
            nc.scalar.activation(fl(Xi[:, 4 * g:4 * g + 4, :]), bank[2 + g % 2][:, :], ACT.Copy).then_inc(sem("x_done"), 1)

        def level(lv, last=False):
            for g in range(NG):
                if not last:
                    act.wait_ge(sem("inv_b"), NG * lv + g + 1)
                    nc.scalar.activation(fl(Xi[:, 4 * g:4 * g + 4, :]), bank[2 + g % 2][:, :], ACT.Copy).then_inc(sem("x_done"), 1)
                act.wait_ge(sem("inv_c"), NG * lv + g + 1)
                nc.scalar.activation(fl(Zi[:, 4 * g:4 * g + 4, :]), bank[4 + g % 2][:, :], ACT.Copy).then_inc(sem("z_done"), 1)

        with act.Fori(0, 5) as lv:
            level(lv)
        level(5, True)
        for ch in range(2):
            for par in range(2):
                act.wait_ge(sem("rhs_ps"), 2 * ch + par + 1)
                nc.scalar.activation(fl(rhsb[:, NP_ * par:NP_ * par + NP_, :]), bank[par][:, 0:384], ACT.Copy)\
                    .then_inc(sem("rhs_out"), 1)
            for par in range(2):
                act.wait_ge(sem("u_ps"), 2 * ch + par + 1)
                if ch:
                    act.wait_ge(sem("y_ps"), 1)
                nc.scalar.activation(fl(uneg[:, NP_ * par:NP_ * par + NP_, :]), bank[2 + par][:, 0:384], ACT.Copy,
                                     scale=-1.0).then_inc(sem("u_out"), 1)
            act.wait_ge(sem("y_ps"), ch + 1)
            for q in range(2):
                nc.scalar.activation(yT[:, 3 * q:3 * q + 3, tokens(ch)], bank[4 + q][:, 0:384].rearrange("p (a t) -> p a t", a=3),
                                     ACT.Copy).then_inc(sem("y_out"), 1)
        split_w_out(0)
        for q in range(3):
            act.wait_ge(sem("d_out"), q + 1)
            nc.scalar.activation(sq[:, 2 * q:2 * q + 2, :], dT[:, 2 * q:2 * q + 2, :], ACT.Square).then_inc(sem("head_sq"), 1)
        root("gn")
        act.wait_ge(*head_count("gn", "done", NP_))
        nc.scalar.activation(sq[:, 0:2, :], mq[:, :, :], ACT.Square).then_inc(sem("head_sq"), 1)
        root("mq0")
        for p in range(NP_):
            high(0, p, dT[:, p, :], sem("mix_f"), p + 1)
        attend("at0")
        for p in range(2):
            high(0, NP_ + p, om[:, p, :], *attn_count("at0", "o", p + 1))
        split2(n_wout[0] + 3)
        norm("ffn1")
        ffn(1, n_kv)
        norm("kv")
        split2(n_kv + 1)
        split2(n_kv + 2)
        for c in range(6):
            if c < 3:
                act.wait_ge(sem("k_out"), c + 1)
                nc.scalar.activation(sq[:, 2 * c:2 * c + 2, :], kT[:, 2 * c:2 * c + 2, :], ACT.Square).then_inc(sem("head_sq"), 1)
                split2(n_kv + c + 3)
            else:
                slot_done(act, n_kv + c)
                nc.scalar.activation(vt2[:, :, 256 * (c - 3):256 * (c - 3) + 256],
                                     bank[c % 4][:, :].rearrange("p (t c) -> p t c", t=TT), ACT.Copy).then_inc(sem("v_out"), 1)
        root("kvn")
        norm("ffn2")
        ffn(2, n_bin)
        norm("mix1")
        split2(n_bin + 1)
        split2(n_bin + 2)
        for c in range(4):
            act.wait_ge(sem("q_out"), c + 1)
            nc.scalar.activation(sq[:, 2 * c:2 * c + 2, :], qT[:, 2 * c:2 * c + 2, :], ACT.Square)\
                .then_inc(sem("head_sq"), 1)
            if c == 0:
                split2(n_bin + 3)
        root("bq")
        root("mq1")
        split_w_out(1)
        attend("at1")
        for p in range(8):
            high(1, p, oT[:, p, :], *attn_count("at1", "o", p + 1))
        split2(n_wout[1] + 3)
        norm("ffn3")
        ffn(3, None)

    @block.vector
    def _(dve):
        TTo = nc.vector.tensor_tensor
        TS = nc.vector.tensor_scalar
        STT = nc.vector.scalar_tensor_tensor
        seq = sem("dve_seq")
        cnt = [0]

        def mark(ins):
            cnt[0] += 1
            ins.then_inc(seq, 1)
            return ins

        def settle():
            dve.wait_ge(seq, cnt[0])

        def split(n, half, r=None, rows=False, part=P):
            u = 2 * (n % RING) + half
            if r is None:
                r = n // RING
            dve.wait_ge(hi_ready[u], r + 1)
            TTo(unit_dst(wlo, n, half, rows)[0:part], unit_src(n, half, rows)[0:part],
                unit_dst(whi, n, half, rows)[0:part].bitcast(F32), ALU.subtract).then_inc(lo_ready[u], 1)

        def split2(n):
            split(n, 0)
            split(n, 1)

        def head_norm(name, nt, b, rb, sqv, src, dst, gain, eps=EPS, mode="rms"):
            flat = stat[:, SLOT[name], 0:4 * nt]
            dve.wait_ge(*head_count(name, "stat", 1))
            if mode == "sum":
                mark(nc.vector.tensor_copy(flat, bank[b][:, 0:4 * nt]))
            else:
                if mode == "rms":
                    TS(flat, bank[b][:, 0:4 * nt], 1.0 / HD, eps, ALU.mult, ALU.add).then_inc(sem("head_var"), 1)
                else:
                    nc.vector.tensor_copy(flat, bank[b][:, 0:4 * nt]).then_inc(sem("head_var"), 1)
                dve.wait_ge(*head_count(name, "std", 1))
                if mode == "l2":
                    mark(nc.vector.tensor_scalar_max(flat, flat, 1e-12))
                    settle()
                mark(nc.vector.reciprocal(flat, flat))
            settle()
            nc.vector.tensor_copy(fl(sqv).rearrange("p (n c) -> p n c", c=HD),
                                  flat.unsqueeze(2).broadcast_to([P, 4 * nt, HD])).then_inc(sem("head_wide"), 1)
            for p in range(nt):
                dve.wait_ge(*head_count(name, "rb", p // 2 + 1))
                r = bank[rb[p // 2 % len(rb)]][:, S * (p % 2):S * (p % 2) + S]
                if gain is None:
                    m = TTo(dst[:, p, :], src[:, p, :], r, ALU.mult)
                else:
                    m = STT(dst[:, p, :], src[:, p, :], gain(p), r, ALU.mult, ALU.mult)
                m.then_inc(sem("head_done"), 1)

        def norm(name):
            i = norm_no[name]
            v = stat[:, 16, 2 * i:2 * i + 2]
            dve.wait_ge(sem("norm_stat"), i + 1)
            TS(v, bank[6][:, 0:2], 1.0 / D, EPS, ALU.mult, ALU.add).then_inc(sem("norm_var"), 1)
            dve.wait_ge(sem("norm_std"), i + 1)
            nc.vector.reciprocal(v, v).then_inc(sem("norm_rstd"), 1)
            dve.wait_ge(sem("norm_rb"), i + 1)

            def low(k):
                dve.wait_ge(sem("hhi_ready"), 8 * i + k + 1)
                TTo(hlo[:, k, :], sq[:, k, :], hhi[:, k, :].bitcast(F32), ALU.subtract).then_inc(sem("h_ready"), 1)

            for k in range(KT):
                STT(sq[:, k, :], xT[:, k, :], col(norm_gain[name] + k), bank[7][:, 0:S], ALU.mult, ALU.mult)\
                    .then_inc(sem("hf_ready"), 1)
                if k >= 2:
                    low(k - 2)
            low(KT - 2)
            low(KT - 1)

        def ffn(f, following):
            n0, j0 = n_ffn[f], NJ * f
            q = [(n0 + c) // RING for c in range(3)]

            def gate(j, half, rows=P):
                dve.wait_ge(sem("silu_done"), j0 + j + 1)
                TTo(g32[0:rows, half, :], sg[0:rows, half, :], bank[4 + half][0:rows, S:2 * S], ALU.mult)\
                    .then_inc(sem("g32_done"), 1)

            def g_lo(j, half, rows=P):
                dve.wait_ge(sem("ghi_done"), j0 + j + 1)
                TTo(glo[0:rows, half, :], g32[0:rows, half, :], ghi[0:rows, half, :].bitcast(F32), ALU.subtract)\
                    .then_inc(sem("g_ready"), 1)

            for c, half in ((0, 0), (1, 0), (0, 1), (1, 1), (2, 0)):
                split(n0 + c, half, rows=(c == 2))
            with dve.Fori(0, FULL) as t:
                gate(2 * t, 0)
                split(n0, 0, t + 1 + q[0])
                g_lo(2 * t, 0)
                split(n0 + 1, 0, t + 1 + q[1])
                split(n0 + 2, 1, t + q[2], True)
                gate(2 * t + 1, 1)
                split(n0, 1, t + 1 + q[0])
                g_lo(2 * t + 1, 1)
                split(n0 + 1, 1, t + 1 + q[1])
                split(n0 + 2, 0, t + 1 + q[2], True)
            gate(NJ - 2, 0)
            g_lo(NJ - 2, 0)
            split(n0 + 2, 1, FULL + q[2], True, LASTROWS)
            gate(NJ - 1, 1, LASTROWS)
            g_lo(NJ - 1, 1, LASTROWS)
            if following is not None:
                split2(following)
            slot_done(dve, n0 + 3 * FULL + 2)
            for b in range(4):
                STT(fl(xT[:, 2 * b:2 * b + 2, :]), bank[b][:, :], 0.5, fl(xT[:, 2 * b:2 * b + 2, :]), ALU.mult, ALU.add)\
                    .then_inc(sem("x_ready"), 1)

        nc.vector.memset(stat[:, 20, :], 0.0).then_inc(sem("g32_done"), 1)
        dve.wait_ge(sem("prm_t"), 1)
        mark(nc.vector.tensor_copy(prm[:, 0:rowsA + rowsB], bank[7][:, 0:rowsA + rowsB]))
        settle()
        mark(TS(omu[:, 0:20], prm[:, C_MU:C_MU + 20], -1.0, 1.0, ALU.mult, ALU.add))
        TS(omu[:, 20:26], prm[:, C_KA:C_KA + 6], -1.0, 1.0, ALU.mult, ALU.add).then_inc(sem("prm_ready"), 1)
        dve.wait_ge(sem("prm_ready"), 1)
        dve.wait_ge(sem("mem_ss"), 1)
        TS(stat[:, 17, 0:2], stat[:, 17, 0:2], 1.0 / D, EPS, ALU.mult, ALU.add).then_inc(sem("mem_var"), 1)
        dve.wait_ge(sem("mem_std"), 1)
        mark(nc.vector.reciprocal(stat[:, 17, 0:2], stat[:, 17, 0:2]))
        settle()
        for t in range(TT):
            TS(mrow[:, t, :], mrow[:, t, :], stat[:, 17, t:t + 1], None, ALU.mult).then_inc(sem("mem_scaled"), 1)
        for j in range(4):
            dve.wait_ge(sem("m_t"), j + 1)
            mark(nc.vector.tensor_copy(fl(mT[:, 2 * j:2 * j + 2, :]), bank[j][:, :]))
        settle()
        for l in range(2):
            def low(k):
                dve.wait_ge(sem("mhi_ready"), 8 * l + k + 1)
                TTo((hlo if l == 0 else mlo)[:, k, :], mgv[l][:, k, :],
                    (hhi if l == 0 else mhi)[:, k, :].bitcast(F32), ALU.subtract).then_inc(sem("mem_h"), 1)
            for k in range(KT):
                TS(mgv[l][:, k, :], mT[:, k, :], col(G_MEM + 8 * l + k), None, ALU.mult).then_inc(sem("mg_ready"), 1)
                if k >= 2:
                    low(k - 2)
            low(KT - 2)
            low(KT - 1)
            if l == 0:
                split2(n_mem)
                for j in range(4):
                    dve.wait_ge(sem("x_t"), j + 1)
                    nc.vector.tensor_copy(fl(xT[:, 2 * j:2 * j + 2, :]), bank[4 + j % 2][:, :]).then_inc(sem("x_ready"), 1)
                split2(n_mem + 1)
                split2(n_mem + 2)
        split2(n_mem + 3)
        for l in range(2):
            slot_done(dve, n_mem + 2 * l)
            nc.vector.tensor_copy(fl(kmT[:, l, :, :]), bank[2 * l][:, :]).then_inc(sem("mem_k_out"), 1)
            dve.wait_ge(sem("mem_k_out"), l + 1)
            head_norm(f"kn{l}", 2, 6, [7], sq[:, 2 * l:2 * l + 2, :], kmT[:, l, :, :], kmT[:, l, :, :], lambda p: col(C_MK + l))
        norm("ffn0")
        ffn(0, n_win)
        def attend(name):
            heads = HEADS[name]

            def maxima(n):
                slope = heads[n][5]
                dve.wait_ge(*attn_count(name, "scores", n + 1))
                if slope is None:
                    src = bank[n % 2][:, :].rearrange("p (t s) -> p t s", t=TT)
                    if n >= 2:
                        dve.wait_ge(*attn_count(name, "turn", n - 1))
                else:
                    src = prb[:, n % 2, :, :]
                    if n >= 2:
                        dve.wait_ge(*attn_count(name, "turn", n - 1))
                    mark(STT(fl(src), fl(dist[:, :, :]), -slope / SCALE, bank[n % 2][:, :], ALU.mult, ALU.add))
                    settle()
                mark(nc.vector.tensor_reduce(sml[:, n % 2, 0:TT], src, AX.X, ALU.max))
                settle()
                TS(sml[:, n % 2, 0:TT], sml[:, n % 2, 0:TT], -SCALE, None, ALU.mult).then_inc(sem("attn_max"), 1)

            def normalise(n):
                dve.wait_ge(*attn_count(name, "exp", n + 1))
                mark(nc.vector.reciprocal(sml[:, n % 2, 4:4 + TT], sml[:, n % 2, 2:2 + TT]))
                settle()
                for t in range(TT):
                    m = TS(prb[:, n % 2, t, :], prb[:, n % 2, t, :], sml[:, n % 2, 4 + t:5 + t], None, ALU.mult)
                m.then_inc(sem("attn_probs"), 1)

            def evict(p):
                dve.wait_ge(*attn_count(name, "values", 2 * p + 2))
                nc.vector.tensor_copy(heads[2 * p][3], bank[4 + p % 2][:, 0:S]).then_inc(sem("attn_o"), 1)

            maxima(0)
            for n in range(len(heads)):
                if n + 1 < len(heads):
                    maxima(n + 1)
                if n >= 4 and n % 2 == 0:
                    evict(n // 2 - 2)
                normalise(n)
            evict(len(heads) // 2 - 2)
            evict(len(heads) // 2 - 1)

        def low_mix(l, k, src):
            dve.wait_ge(sem(f"mixhi{l}"), k + 1)
            TTo(hlo[:, k, :], src, hhi[:, k, :].bitcast(F32), ALU.subtract).then_inc(sem(f"mixed{l}"), 1)

        def split_w_out(l):
            for c in range(3):
                split2(n_wout[l] + c)

        def w_out(l):
            split2(n_wout[l] + 3)
            for c in range(4):
                slot_done(dve, n_wout[l] + c)
                x = fl(xT[:, 2 * c:2 * c + 2, :])
                TTo(x, bank[c][:, :], x, ALU.add).then_inc(sem("x_ready"), 1)

        dve.wait_ge(sem("all_consts"), 1)
        norm("mix0")
        split2(n_win + 1)
        split2(n_win + 2)

        def shift(i):
            dve.wait_ge(sem("shift_a"), i + 1)
            for half in range(2):
                c = W_IN_ORDER[i] * 2 + half
                u = U_TILES[i][half]
                m = STT(u[:, 1:S], bank[i % 4][:, S * half:S * half + S - 1], col(C_MU + c), u[:, 1:S], ALU.mult, ALU.add)
            m.then_inc(sem("win_free"), 1)
            if i + 3 < 11:
                split2(n_win + i + 3)

        mark(nc.vector.memset(pw[:, :, 0:1], 0.0))
        for i in range(4):
            shift(i)
        for p in range(NP_):
            dve.wait_ge(sem("lw_ready"), p + 1)
            for j in (2 * p, 2 * p + 1):
                mark(nc.vector.tensor_tensor_scan(pw[:, j, 1:P + 1], ones_row[:, :], pw[:, j, 1:P + 1], 0.0, ALU.mult, ALU.add))
        settle()
        mark(nc.vector.tensor_copy(c12[:, :, :], pw[:, :, HD:HD + 1]))
        settle()
        TTo(pw[:, :, :], pw[:, :, :], c12[:, :, :].broadcast_to([P, 2 * NP_, P + 1]), ALU.subtract).then_inc(sem("cum_ready"), 1)
        shift(4)
        shift(5)
        head_norm("kkn", NP_, 6, [7, 6], sq[:, 0:NP_, :], uk, kk, lambda p: col(C_KK + p), mode="l2")
        shift(6)
        dve.wait_ge(sem("a_ready"), NP_)
        tmp = KR[:, :, :, :].rearrange("p a b c -> p (a b c)")[:, 0:NP_ * S].rearrange("p (a s) -> p a s", a=NP_)
        for p in range(NP_):
            mark(TS(tmp[:, p, :], ua[:, p, :], col(C_KA + p), omu[:, 20 + p:21 + p], ALU.mult, ALU.add))
        settle()
        mark(TTo(fl(uk[:, :, :]), fl(uk[:, :, :]), fl(tmp), ALU.mult))
        mark(TTo(fl(ua[:, :, :]), fl(kk[:, :, :]), fl(ua[:, :, :]), ALU.mult))
        settle()
        shift(7)
        dve.wait_ge(*head_count("kkn", "done", NP_))
        for p in range(NP_):
            STT(sq[:, p, :], ur[:, p, :], col(C_RK + p), uk[:, p, :], ALU.mult, ALU.mult).then_inc(sem("head_sq"), 1)
        shift(8)
        shift(9)
        dve.wait_ge(sem("powers"), 2)
        dve.wait_ge(sem("mid_power"), 1)
        dve.wait_ge(*head_count("bn", "sq", NP_))

        def per_chunk(t):
            return t[:, :, :].rearrange("p a (c t) -> p (a c) t", c=2)

        TTo(KR[:, :, 0, :], per_chunk(kk), pr[:, :, 0:P], ALU.mult).then_inc(sem("powers_used"), 1)
        TTo(KR[:, :, 1, :], per_chunk(ur), pr[:, :, 1:P + 1], ALU.mult).then_inc(sem("powers_used"), 1)
        TTo(sfin[:, 0, :], sfin[:, 1, :], pr[:, 0::2, P], ALU.mult).then_inc(sem("powers_used"), 1)
        mark(TTo(per_chunk(ua), per_chunk(ua), pw[:, :, 1:P + 1], ALU.mult))
        TTo(per_chunk(uk), per_chunk(uk), pw[:, :, 1:P + 1], ALU.mult).then_inc(sem("powers_used"), 1)
        dve.wait_ge(sem("tp_t"), 4)
        head_norm("bn", NP_, 6, [7, 6], sq[:, 0:NP_, :], uv, uv, None, mode="sum")
        dve.wait_ge(sem("lt_unit"), 1)

        def strict(n):
            return tri[:, 1:2, :].broadcast_to([P, n, P]).bitcast(I32)

        def lt(g):
            dve.wait_ge(sem("lt_ps"), g + 1)
            nc.vector.copy_predicated(LT[:, 4 * g:4 * g + 4, :], tri4[:, :, :].bitcast(I32),
                                      bank[g % 2][:, :].rearrange("p (a t) -> p a t", a=4)).then_inc(sem("lt_done"), 1)

        def z1(g):
            dve.wait_ge(sem("lt_done"), g + 1)
            TTo(Zi[:, 4 * g:4 * g + 4, :], LT[:, 4 * g:4 * g + 4, :], z1mask[:, :].unsqueeze(1).broadcast_to([P, 4, P]), ALU.mult)\
                .then_inc(sem("z_done"), 1)

        lt(0)
        for g in range(NG):
            if g + 1 < NG:
                lt(g + 1)
            z1(g)

        def level(lv):
            q = bass.ds(lv + 1, 1)
            for g in range(NG):
                dve.wait_ge(sem("inv_a"), NG * lv + g + 1)
                TTo(Ri[:, 4 * g:4 * g + 4, :], bank[g % 2][:, :].rearrange("p (a t) -> p a t", a=4),
                    invmask[:, q, :].broadcast_to([P, 4, P]), ALU.mult).then_inc(sem("r_done"), 1)

        with dve.Fori(0, 5) as lv:
            level(lv)
        level(5)
        dve.wait_ge(sem("mq_zero"), 1)
        for n in range(2 * NH):
            par, ch, p = TRIANGLES[n]
            i = inst(par, ch, p)
            dve.wait_ge(sem("nmq_ps"), n + 1)
            nc.vector.copy_predicated(LT[:, i, :], tri[:, 0, :].bitcast(I32), bank[6 + n % 2][:, 0:P])
            nc.vector.copy_predicated(MQ[:, i, :], fl(tri[:, 1:3, :]).bitcast(I32), bank[6 + n % 2][:, P:3 * P])\
                .then_inc(sem("nmq_done"), 1)
        dve.wait_ge(sem("s_ps"), 1)
        TTo(sT[:, :, :], bank[0][:, 0:384].rearrange("p (a v) -> p a v", a=NP_),
            sfin[:, 0, :].unsqueeze(2).broadcast_to([P, NP_, HD]), ALU.mult).then_inc(sem("state"), 1)
        split_w_out(0)
        for q in range(3):
            dve.wait_ge(sem("centred"), q + 1)
            nc.vector.tensor_copy(fl(dT[:, 2 * q:2 * q + 2, :]), bank[q][:, :]).then_inc(sem("d_out"), 1)
        dve.wait_ge(sem("d_out"), 3)
        head_norm("gn", NP_, 6, [7, 6], sq[:, 0:NP_, :], dT, dT, lambda p: col(C_LNW + p), eps=GN_EPS)
        dve.wait_ge(*head_count("gn", "done", NP_))
        for p in range(NP_):
            mark(STT(dT[:, p, :], dT[:, p, :], col(C_LNB + p), uv[:, p, :], ALU.add, ALU.add))
        settle()
        for p in range(NP_):
            TTo(dT[:, p, :], dT[:, p, :], gT[:, p, :], ALU.mult).then_inc(sem("mix_f"), 1)
        dve.wait_ge(sem("mq_out"), 1)
        head_norm("mq0", 2, 6, [7], sq[:, 0:2, :], mq, mq, lambda p: col(C_MQ))
        for p in range(NP_):
            low_mix(0, p, dT[:, p, :])
        attend("at0")
        for p in range(2):
            low_mix(0, NP_ + p, om[:, p, :])
        w_out(0)
        norm("ffn1")
        ffn(1, n_kv)
        norm("kv")
        split2(n_kv + 1)
        split2(n_kv + 2)
        for c in range(3):
            slot_done(dve, n_kv + c)
            nc.vector.tensor_copy(fl(kT[:, 2 * c:2 * c + 2, :]), bank[c][:, :]).then_inc(sem("k_out"), 1)
            split2(n_kv + c + 3)
        dve.wait_ge(sem("k_out"), 3)
        head_norm("kvn", NP_, 6, [7, 6], sq[:, 0:NP_, :], kT, kT, lambda p: col(C_KVK))
        norm("ffn2")
        ffn(2, n_bin)
        norm("mix1")
        split2(n_bin + 1)
        split2(n_bin + 2)
        for c in range(4):
            slot_done(dve, n_bin + c)
            nc.vector.tensor_copy(fl(qT[:, 2 * c:2 * c + 2, :]), bank[c][:, :]).then_inc(sem("q_out"), 1)
            if c == 0:
                split2(n_bin + 3)
        dve.wait_ge(sem("q_out"), 4)
        head_norm("bq", NP_, 6, [7, 6], sq[:, 0:NP_, :], qT, qT, lambda p: col(C_BQ))
        head_norm("mq1", 2, 6, [7], sq[:, NP_:NP_ + 2, :], qT[:, NP_:NP_ + 2, :], qT[:, NP_:NP_ + 2, :],
                  lambda p: col(C_MQ + 1))
        split_w_out(1)
        attend("at1")
        for p in range(8):
            low_mix(1, p, oT[:, p, :])
        w_out(1)
        norm("ffn3")
        ffn(3, None)
        for t in range(TT):
            for half in range(2):
                dve.wait_ge(sem("out_t"), 2 * t + half + 1)
                nc.vector.tensor_copy(xrow[:, t, 512 * half:512 * half + 512], bank[4 + 2 * t + half][:, :])\
                    .then_inc(sem("out_rows_ready"), 1)

    ctx.close()


_INS = ["x", "mem", "ffn1_norm", "ffn1_w1", "ffn1_w3", "ffn1_w2", "mix_norm", "w_out", "mem_norm", "w_mem_kv",
        "mem_q_norm", "mem_k_norm", "ffn2_norm", "ffn2_w1", "ffn2_w3", "ffn2_w2", "rwkv_w_in", "rwkv_mu", "rwkv_w0",
        "rwkv_w2", "rwkv_a0", "rwkv_a2", "rwkv_g2", "rwkv_k_k", "rwkv_k_a", "rwkv_r_k", "rwkv_ln_w", "rwkv_ln_b",
        "kv_norm", "w_kv", "kv_k_norm", "moba_w_in", "moba_q_norm"]


def kernel(**inputs):
    import numpy as np
    import concourse.bacc as bacc
    from concourse.bass_utils import run_bass_kernel_spmd

    nc = bacc.Bacc("TRN2", target_bir_lowering=False, num_devices=1)
    arrays, T = {}, {}
    for name in _INS:
        arrays[name] = np.ascontiguousarray(inputs[name])
        T[name] = nc.dram_tensor(name, arrays[name].shape, F32, kind="ExternalInput").ap()
    out = nc.dram_tensor("out", (1, S, D), F32, kind="ExternalOutput").ap()
    build(nc, T, out)
    return run_bass_kernel_spmd(nc, [arrays], core_ids=[0]).results[0]["out"]
```

```python
from contextlib import ExitStack

import concourse.bass as bass
from concourse import mybir

F32 = mybir.dt.float32
F32R = mybir.dt.float32r
BF16 = mybir.dt.bfloat16
I32 = mybir.dt.int32
ALU = mybir.AluOpType
ACT = mybir.ActivationFunctionType
AX = mybir.AxisListType

P = 128
D = 1024
S = 256
DFF = 2752
KT = D // P
TT = S // P
HD = 64
NH = 12
MIX = NH * HD
MEMW = 4 * HD
NP_ = NH // 2
SHIFTW = 3 * MIX + 256
FULL = DFF // 256
TAIL = DFF - 256 * FULL
NJ = -(-DFF // P)
LASTROWS = DFF - P * (NJ - 1)
RING = 3
EPS = 1e-6
GN_EPS = 64e-5
DECAY = float.fromhex("0x1.368b2fc6f9609p-1")
SCALE = HD ** -0.5
FAR = 1e30


def build(nc, T, out):
    ctx = ExitStack()
    sems = {}

    def sem(name):
        if name not in sems:
            sems[name] = ctx.enter_context(nc.semaphore(name))
        return sems[name]

    base = [-(-nc.sbuf_base // 64) * 64]
    arena0 = base[0]

    def place(name, shape, dt, at=None):
        size = (2 if dt == BF16 else 4)
        for n in shape[1:]:
            size *= n
        size = -(-size // 64) * 64
        off = base[0] if at is None else at
        if at is None:
            base[0] += size
        assert off + size <= 229368, (name, off, size)
        return nc.alloc_sbuf_tensor_at(name, shape, dt, offset=off), off + size

    def sb(name, shape, dt=F32):
        return place(name, shape, dt)[0]

    raw = sb("raw", [P, RING, 2048])
    rings_at = base[0]
    whi = sb("whi", [P, 2 * RING, 1024], F32R)
    wlo = sb("wlo", [P, 2 * RING, 1024], F32R)
    rings_end = base[0]
    xT = sb("xT", [P, KT, S])
    h_at = base[0]
    hhi = sb("hhi", [P, KT, S], F32R)
    hlo = sb("hlo", [P, KT, S], F32R)
    sq = sb("sq", [P, KT, S])
    sq_end = base[0]
    kmT = sb("kmT", [P, 2, 2, S])
    vm = sb("vm", [P, 2, 2, MEMW])
    ident = sb("ident", [P, P])
    ones = sb("ones", [P, P])
    rb = sb("rb", [P, S])
    rcol = sb("rcol", [P, TT])
    head_sel = sb("head_sel", [P, 2])
    centre = sb("centre", [P, P])
    invmask = sb("invmask", [P, 7, P])
    z1mask = sb("z1mask", [P, P])
    tri = sb("tri", [P, 3, P])
    tri4 = sb("tri4", [P, 4, P])
    dist = sb("dist", [P, 3, P])
    prm = sb("prm", [P, 144])
    omu = sb("omu", [P, 32])
    stat = sb("stat", [P, 24, 24])
    zw = sb("zw", [P, P], BF16)
    zm = sb("zm", [P, 512], BF16)
    region = base[0]

    bank = [ctx.enter_context(nc.psum_tensor(f"bank{i}", [P, 512], F32)) for i in range(8)]

    at = region
    pre, at = place("pre", [P, 2, 2 * S], F32, at)
    sg, at = place("sg", [P, 2, S], F32, at)
    g32, at = place("g32", [P, 2, S], F32, at)
    ghi, at = place("ghi", [P, 2, S], F32R, at)
    glo, at = place("glo", [P, 2, S], F32R, at)
    ffn_end = at
    kT, at = place("kT", [P, NP_, S], F32, at)
    vt2, at = place("vt2", [P, TT, MIX], F32, at)
    attn_at = at
    h2hi, at = place("h2hi", [P, KT, S], F32R, at)
    h2lo, h2_end = place("h2lo", [P, KT, S], F32R, at)
    assert h2_end <= 229368
    at = ffn_end
    xrow, at = place("xrow", [P, TT, D], F32, at)
    mrow, at = place("mrow", [P, TT, D], F32, at)
    prow, at = place("prow", [P, 2, P], F32, at)
    mT, at = place("mT", [P, KT, S], F32, at)
    mem_h_at = {}
    for l in range(2):
        for what in ("hi", "lo"):
            mem_h_at[l, what], at = place(f"m{l}{what}", [P, KT, S], F32R, at)
    start_end = at
    at = region
    uk, at = place("uk", [P, NP_, S], F32, at)
    uv, at = place("uv", [P, NP_, S], F32, at)
    ua, at = place("ua", [P, NP_, S], F32, at)
    gT, at = place("gT", [P, NP_, S], F32, at)
    KR, at = place("KR", [P, 2 * NP_, 2, P], F32, at)
    vt, at = place("vt", [P, TT, MIX], F32, at)
    mq, at = place("mq", [P, 2, S], F32, at)
    wa, at = place("wa", [P, S], F32, at)
    gd, at = place("gd", [P, S], F32, at)
    la_at = at
    la, at = place("la", [P, MIX], F32, at)
    lg, at = place("lg", [P, MIX], F32, at)
    c12, at = place("c12", [P, 2 * NP_, 1], F32, at)
    sfin, at = place("sfin", [P, 2, NP_], F32, at)
    sT, at = place("sT", [P, NP_, HD], F32, at)
    pw_at = at
    pw, at = place("pw", [P, 2 * NP_, P + 1], F32, at)
    pr_at = at
    pr, at = place("pr", [P, 2 * NP_, P + 1], F32, at)
    kk_at = at
    kk, at = place("kk", [P, NP_, S], F32, at)
    ur_at = at
    ur, at = place("ur", [P, NP_, S], F32, at)
    rwkv_end = at
    bt, _e = place("bt", [P, MIX], F32, pr_at)
    ktp, _e = place("ktp", [P, MIX], F32, _e)
    assert _e <= kk_at
    rhsb, _e = place("rhsb", [P, NH, HD], F32, kk_at)
    uneg, _e = place("uneg", [P, NH, HD], F32, _e)
    assert _e <= ur_at
    yT, _e = place("yT", [P, NP_, S], F32, ur_at)
    dT, _e = place("dT", [P, NP_, S], F32, la_at)
    LT, _e = place("LT", [P, 2 * NH, P], F32, rings_at)
    Zi, _e = place("Zi", [P, 2 * NH, P], F32, _e)
    Xi, _e = place("Xi", [P, 2 * NH, P], F32, _e)
    Ri, _e = place("Ri", [P, 2 * NH, P], F32, _e)
    assert _e <= rings_end
    MQ, _e = place("MQ", [P, 2 * NH, 2 * P], F32, h_at)
    assert _e <= sq_end
    at = attn_at
    qT, at = place("qT", [P, 4 * 2, S], F32, at)
    attn_end = at
    prb, _e = place("prb", [P, 3, 4 * P], F32, pw_at)
    prT, _e = place("prT", [P, 2, 4 * P], F32, _e)
    orow, _e = place("orow", [P, 2, TT, P], F32, _e)
    sml, _e = place("sml", [P, 4, 8], F32, _e)
    assert attn_end <= pw_at and _e <= ur_at, (attn_end, pw_at, _e)
    assert max(start_end, attn_at, rwkv_end) <= 229368, (start_end, attn_at, rwkv_end)

    rowsA, rowsB = 72, 68
    G_FFN1, G_MIX, G_MEM, G_FFN2, G_KV = 0, 16, 32, 48, 64
    C_MU = rowsA
    C_W0, C_A0, C_KK, C_KA, C_RK, C_LNW, C_LNB = (rowsA + 20 + 6 * i for i in range(7))
    C_MQ, C_MK, C_KVK, C_BQ = rowsA + 62, rowsA + 64, rowsA + 66, rowsA + 67

    def col(c):
        return prm[:, c:c + 1]

    def fl(ap):
        return ap.rearrange("p a b -> p (a b)")

    def cols_of(w, c):
        return w.rearrange("(k p) c -> p k c", p=P)[:, :, 256 * c:256 * c + 256]

    W_IN_ORDER = [9, 3, 4, 5, 0, 1, 2, 6, 7, 8, 10]
    stream = []

    n_slot = [0]

    def take(n):
        n_slot[0] += n
        return n_slot[0] - n

    n_ffn = {}
    n_ffn[0] = take(3 * (FULL + 1))
    n_mem = take(4)
    n_win = take(11)
    n_wout = {0: take(4)}
    n_ffn[1] = take(3 * (FULL + 1))
    n_kv = take(6)
    n_ffn[2] = take(3 * (FULL + 1))
    n_bin = take(4)
    n_wout[1] = take(4)
    n_ffn[3] = take(3 * (FULL + 1))

    static = {}
    for l in range(2):
        for c in range(2):
            static[n_mem + 2 * l + c] = cols_of(T["w_mem_kv"][l], c)
        for c in range(4):
            static[n_wout[l] + c] = cols_of(T["w_out"][l], c)
    for i, c in enumerate(W_IN_ORDER):
        static[n_win + i] = cols_of(T["rwkv_w_in"][0], c)
    for c in range(6):
        static[n_kv + c] = cols_of(T["w_kv"], c)
    for c in range(4):
        static[n_bin + c] = cols_of(T["moba_w_in"][0], c)

    ffn_w = [(T[f"ffn{1 + i % 2}_w1"][i // 2], T[f"ffn{1 + i % 2}_w3"][i // 2], T[f"ffn{1 + i % 2}_w2"][i // 2])
             for i in range(4)]
    raw_ready = [sem(f"raw_ready{c}") for c in range(RING)]
    tail_ready = sem("tail_ready")
    hi_ready = [sem(f"hi_ready{u}") for u in range(2 * RING)]
    lo_ready = [sem(f"lo_ready{u}") for u in range(2 * RING)]
    unit_used = [sem(f"unit_used{u}") for u in range(2 * RING)]

    def raw8(n):
        return raw[:, n % RING, :].rearrange("p (k c) -> p k c", k=KT)

    def unit_src(n, half, rows):
        if rows:
            return raw[:, n % RING, 1024 * half:1024 * half + 1024]
        return raw8(n)[:, :, P * half:P * half + P]

    def unit_dst(ring, n, half, rows):
        u = ring[:, 2 * (n % RING) + half, :]
        return u if rows else u.rearrange("p (k c) -> p k c", k=KT)

    SLOT = {"kn0": 0, "kn1": 1, "kkn": 2, "bn": 3, "gn": 4, "mq0": 5, "kvn": 6, "bq": 7, "mq1": 8}
    TILES = {"kn0": 2, "kn1": 2, "kkn": 6, "bn": 6, "gn": 6, "mq0": 2, "kvn": 6, "bq": 6, "mq1": 2}
    STAT = {n: stat[:, SLOT[n], 0:4 * TILES[n]] for n in SLOT}
    N_ROW_LOADS = 20
    UPD_LAST = 28
    NORM_WAITS = {"ffn0": []}
    NORM_WAITS.update({n: [] for n in ("mix0", "ffn1", "kv", "mix1", "ffn3")})
    NORM_WAITS["mix1"] = [("head_done", 2 + 2 + 3 * NP_ + 2 + NP_)]
    H = {n: (h2hi, h2lo) if n in ("ffn1", "ffn2", "ffn3") else (hhi, hlo)
         for n in ("ffn0", "mix0", "ffn1", "kv", "ffn2", "mix1", "ffn3")}
    PEEL = 4
    FFN_UNITS = ([(0, 0), (1, 0), (0, 1)], [(1, 1), (2, 0)])
    SLOT_UNITS = ([(0, 0), (0, 1), (1, 0)], [(1, 1), (2, 0), (2, 1)])
    PHASE = {"ffn0": (n_ffn[0], FFN_UNITS), "mix0": (n_mem, SLOT_UNITS), "ffn1": (n_ffn[1], FFN_UNITS), "kv": (n_kv, SLOT_UNITS),
             "ffn2": (n_ffn[2], FFN_UNITS), "mix1": (n_bin, SLOT_UNITS), "ffn3": (n_ffn[3], FFN_UNITS)}

    def inst(par, ch, p):
        return NH * par + NP_ * ch + p

    INSTANCES = [(par, ch, p) for par in range(2) for ch in range(2) for p in range(NP_)]
    NG = 2 * NH // 4
    TRIANGLES = [(par, ch, p) for ch in range(2) for par in range(2) for p in range(NP_)]

    def part(par):
        return slice(HD * par, HD * par + HD)

    def tokens(ch):
        return slice(P * ch, P * ch + P)

    def mem_heads(l, q):
        return [(q[part(e), p, :], kmT[part(e), l, p, :], lambda kt, h=2 * p + e: vm[:, l, kt, HD * h:HD * h + HD], None)
                for p in range(2) for e in range(2)]

    HEADS = {
        "at0": mem_heads(0, mq),
        "at1": [(qT[part(e), p, :], kT[part(e), p, :], lambda kt, h=2 * p + e: vt2[:, kt, HD * h:HD * h + HD],
                 2.0 ** (-8.0 * (2 * p + e + 1) / NH)) for p in range(NP_) for e in range(2)]
        + mem_heads(1, qT[:, NP_:NP_ + 2, :]),
    }
    OUT_TILE = {"at0": NP_, "at1": 0}

    def blocks(head):
        return [(t, kt) for t in range(TT) for kt in range(TT) if head[3] is None or kt <= t]

    def query_cols(head, t):
        mine = [i for i, (bt_, _) in enumerate(blocks(head)) if bt_ == t]
        return slice(P * mine[0], P * mine[-1] + P)

    U_TILES = []
    for c in W_IN_ORDER:
        U_TILES.append((wa[:, :], gd[:, :]) if c == 9 else
                       None if c == 10 else
                       tuple((ur, uk, uv)[c // 3][:, 2 * (c % 3) + half, :] for half in range(2)))

    SQ_COUNT = {"kn0": 1, "kn1": 1, "kkn": NP_, "bn": NP_, "gn": 3, "mq0": 1, "kvn": 3, "bq": 3, "mq1": 1}
    START, total = {}, {}
    for name in ("kn0", "kn1", "kkn", "bn", "gn", "mq0", "kvn", "bq", "mq1"):
        nt = TILES[name]
        for what, n in (("sq", SQ_COUNT[name]), ("stat", 1), ("var", 0 if name == "bn" else 1),
                        ("std", 0 if name == "bn" else 1), ("wide", 1), ("rb", -(-nt // 2)), ("done", nt)):
            START[name, what] = total.get(what, 0)
            total[what] = total.get(what, 0) + n

    def head_count(name, what, n):
        return sem(f"head_{what}"), START[name, what] + n

    def attn_count(name, what, n):
        heads0 = len(HEADS["at0"])
        return sem(f"attn_{what}"), n + (0 if name == "at0" else heads0 // 2 if what == "rows_t" else heads0)

    def mixed(name, p):
        return sem(f"mixed{name[2]}"), OUT_TILE[name] + p + 1

    block = ctx.enter_context(nc.Block())

    upd = {"load": 4, "ffn0": 8, "mix0": 12, "ffn1": 16, "ffn2": 20, "mix1": 24, "ffn3": 28}
    norm_no = {"ffn0": 0, "mix0": 1, "ffn1": 2, "kv": 3, "ffn2": 4, "mix1": 5, "ffn3": 6}
    stat_no = {"ffn0": 0, "mix0": 1, "ffn1": 2, "kv": 3, "mix1": 4, "ffn3": 5}
    norm_after = {"ffn0": "load", "mix0": "ffn0", "ffn1": "mix0", "kv": "ffn1", "mix1": "ffn2", "ffn3": "mix1"}
    norm_gain = {"ffn0": G_FFN1, "mix0": G_MIX, "ffn1": G_FFN2, "kv": G_KV, "ffn2": G_FFN1 + 8,
                 "mix1": G_MIX + 8, "ffn3": G_FFN2 + 8}

    def slot_done(eng, n):
        eng.wait_ge(unit_used[2 * (n % RING) + 1], n // RING + 1)

    @block.sync
    def _(sp):
        x2 = T["x"][0].rearrange("(t p) d -> p t d", p=P)
        m2 = T["mem"][0].rearrange("(t p) d -> p t d", p=P)
        sp.dma_start(xrow[:, :, :], x2).then_inc(sem("x_loaded"), 16)
        sp.dma_start(prow[0:16, 0, :], T["ffn1_norm"].rearrange("l (r c) -> (l r) c", c=P)).then_inc(sem("first_rows"), 16)
        for c in range(2):
            sp.dma_start(raw8(c), cols_of(ffn_w[0][c], 0)).then_inc(raw_ready[c], 16)
        sp.dma_start(raw[:, 2, :].rearrange("p (j d) -> p j d", j=2), ffn_w[0][2][0:256, :].rearrange("(j p) d -> p j d", p=P))\
            .then_inc(raw_ready[2], 16)
        sp.dma_start(mrow[:, :, :], m2).then_inc(sem("mem_loaded"), 16)
        r = 16
        for name, rows in (("mix_norm", 16), ("mem_norm", 16), ("ffn2_norm", 16), ("kv_norm", 8)):
            src = T[name].rearrange("l (r c) -> (l r) c", c=P) if name != "kv_norm" else T[name].rearrange("(r c) -> r c", c=P)
            sp.dma_start(prow[r:r + rows, 0, :], src).then_inc(sem("rows_loaded"), 16)
            r += rows
        r = 0
        for name in ("rwkv_mu", "rwkv_w0", "rwkv_a0", "rwkv_k_k", "rwkv_k_a"):
            src = T[name][0].rearrange("(r c) -> r c", c=P)
            sp.dma_start(prow[r:r + src.shape[0], 1, :], src).then_inc(sem("rows_loaded"), 16)
            r += src.shape[0]
        sp.dma_start(prow[r:r + 6, 1, :], T["rwkv_r_k"][0].rearrange("(r e) c -> r (e c)", e=2)).then_inc(sem("rows_loaded"), 16)
        r += 6
        for name in ("rwkv_ln_w", "rwkv_ln_b"):
            sp.dma_start(prow[r:r + 6, 1, :], T[name][0].rearrange("(r c) -> r c", c=P)).then_inc(sem("rows_loaded"), 16)
            r += 6
        for name in ("mem_q_norm", "mem_k_norm"):
            for e in range(2):
                sp.dma_start(prow[r:r + 2, 1, HD * e:HD * e + HD], T[name]).then_inc(sem("rows_loaded"), 16)
            r += 2
        for e in range(2):
            sp.dma_start(prow[r:r + 1, 1, HD * e:HD * e + HD], T["kv_k_norm"].rearrange("(a c) -> a c", a=1)).then_inc(sem("rows_loaded"), 16)
            sp.dma_start(prow[r + 1:r + 2, 1, HD * e:HD * e + HD], T["moba_q_norm"]).then_inc(sem("rows_loaded"), 16)

        def load_slot(n, src, dst=None):
            if n >= RING:
                sp.wait_ge(lo_ready[2 * (n % RING) + 1], n // RING)
            sp.dma_start(raw8(n) if dst is None else dst, src).then_inc(raw_ready[n % RING], 16)

        def load_ffn(f):
            w1, w3, w2 = ffn_w[f]
            n0 = n_ffn[f]
            w1v = w1.rearrange("(k p) c -> p k c", p=P)
            w3v = w3.rearrange("(k p) c -> p k c", p=P)
            rows2 = [raw[:, (n0 + 2) % RING, :].rearrange("p (j d) -> p j d", j=2)]
            with sp.Fori(1 if f == 0 else 0, FULL) as t:
                for c, wv in ((0, w1v), (1, w3v)):
                    n = n0 + c
                    sp.wait_ge(lo_ready[2 * (n % RING) + 1], t + n // RING)
                    sp.dma_start(raw8(n), wv[:, :, bass.ds(t * 256, 256)]).then_inc(raw_ready[n % RING], 16)
                n = n0 + 2
                sp.wait_ge(lo_ready[2 * (n % RING) + 1], t + n // RING)
                sp.dma_start(rows2[0], w2[bass.ds(t * 256, 256), :].rearrange("(j p) d -> p j d", p=P))\
                    .then_inc(raw_ready[n % RING], 16)
            n = n0 + 3 * FULL
            load_slot(n, w1v[:, :, 256 * FULL:DFF], raw8(n)[:, :, 0:TAIL])
            load_slot(n + 1, w3v[:, :, 256 * FULL:DFF], raw8(n + 1)[:, :, 0:TAIL])
            load_slot(n + 2, w2[256 * FULL:256 * FULL + P, :], raw[:, (n + 2) % RING, 0:1024])
            sp.dma_start(raw[0:LASTROWS, (n + 2) % RING, 1024:2048], w2[DFF - LASTROWS:DFF, :]).then_inc(tail_ready, 16)

        load_ffn(0)
        for n in range(n_mem, n_mem + 4):
            load_slot(n, static[n])
        for n in range(n_win, n_win + 11):
            load_slot(n, static[n])
            if n == n_win + 3:
                slot_done(sp, n_mem + 3)
                sp.dma_start(la[0:HD, :], T["rwkv_w2"][0]).then_inc(sem("lora_loaded"), 16)
                sp.dma_start(la[HD:P, :], T["rwkv_a2"][0]).then_inc(sem("lora_loaded"), 16)
                sp.dma_start(lg[:, :], T["rwkv_g2"][0]).then_inc(sem("lora_loaded"), 16)
        for n in range(n_wout[0], n_wout[0] + 4):
            load_slot(n, static[n])
        load_ffn(1)
        for n in range(n_kv, n_kv + 6):
            load_slot(n, static[n])
        load_ffn(2)
        for n in range(n_bin, n_bin + 4):
            load_slot(n, static[n])
        for n in range(n_wout[1], n_wout[1] + 4):
            load_slot(n, static[n])
        load_ffn(3)
        for t in range(TT):
            sp.wait_ge(sem("out_rows_ready"), 2 * t + 2)
            sp.dma_start(out[0, P * t:P * t + P, :], xrow[:, t, :]).then_inc(sem("stored"), 16)
        sp.wait_ge(sem("stored"), 16 * TT)


    def pool_rwkv(pool):
        slot_done(pool, n_win + 10)
        nc.gpsimd.memset(fl(LT[:, :, :]), 0.0).then_inc(sem("lt_step"), 1)
        pool.wait_ge(sem("lt_step"), 1)
        nc.gpsimd.affine_select(out=LT[:, :, :], in_=LT[:, :, :], compare_op=ALU.not_equal, fill=1.0, base=0,
                                pattern=[[0, 2 * NH], [-1, P]], channel_multiplier=1).then_inc(sem("lt_unit"), 1)
        pool.wait_ge(*head_count("bn", "done", NP_))
        nc.gpsimd.memset(MQ[:, :, :], 0.0).then_inc(sem("mq_zero"), 1)

    @block.gpsimd
    def _(pool):
        made = sem("const_step")
        n = [0]

        def step(ins):
            n[0] += 1
            ins.then_inc(made, 1)

        def done():
            pool.wait_ge(made, n[0])

        def diag(ap, pattern, fill, keep=ALU.not_equal, cbase=0, mult=1):
            step(nc.gpsimd.affine_select(out=ap, in_=ap, compare_op=keep, fill=fill, base=cbase, pattern=pattern,
                                         channel_multiplier=mult))

        step(nc.gpsimd.memset(ident[:, :], 0.0))
        step(nc.gpsimd.memset(ones[:, :], 1.0))
        done()
        diag(ident[:, :], [[-1, P]], 1.0)
        done()
        nc.gpsimd.memset(head_sel[:, :], 1.0).then_inc(made, 1)
        n[0] += 1
        done()
        diag(head_sel[:, :], [[-HD, 2]], 0.0, ALU.is_ge)
        done()
        step(nc.gpsimd.affine_select(out=head_sel[:, :], in_=head_sel[:, :], compare_op=ALU.is_ge, fill=0.0,
                                     base=HD - 1, pattern=[[HD, 2]], channel_multiplier=-1))
        done()
        nc.gpsimd.memset(zw[:, :], 0.0).then_inc(sem("base_consts"), 1)
        nc.gpsimd.memset(zm[:, :], 0.0).then_inc(sem("base_consts"), 1)
        step(nc.gpsimd.memset(centre[:, :], -1.0 / HD))
        step(nc.gpsimd.memset(invmask[:, :, :], 0.0))
        step(nc.gpsimd.memset(z1mask[:, :], 0.0))
        step(nc.gpsimd.memset(tri[:, :, :], 1.0))
        step(nc.gpsimd.memset(tri4[:, :, :], 1.0))
        step(nc.gpsimd.iota(dist[:, 0:2, :], pattern=[[P, 2], [-1, P]], base=0, channel_multiplier=1,
                            allow_small_or_imprecise_dtypes=True))
        step(nc.gpsimd.iota(dist[:, 2:3, :], pattern=[[0, 1], [-1, P]], base=0, channel_multiplier=1,
                            allow_small_or_imprecise_dtypes=True))
        done()
        v = centre[:, :].rearrange("p (e c) -> p e c", e=2)
        diag(v, [[-HD, 2], [0, HD]], 0.0, ALU.is_ge)
        done()
        step(nc.gpsimd.affine_select(out=v, in_=v, compare_op=ALU.is_ge, fill=0.0, base=HD - 1,
                                     pattern=[[HD, 2], [0, HD]], channel_multiplier=-1))
        done()
        diag(centre[:, :], [[-1, P]], 1.0 - 1.0 / HD)
        for q in range(7):
            s = 1 << q
            nb = P // (2 * s)
            left = invmask[:, q, :].rearrange("p (b e c) -> p b e c", e=2, c=s)[:, :, 0, :]
            step(nc.gpsimd.memset(left, -1.0))
            done()
            step(nc.gpsimd.affine_select(out=left, in_=left, compare_op=ALU.is_ge, fill=0.0, base=-s,
                                         pattern=[[-2 * s, nb], [0, s]], channel_multiplier=1))
            done()
            step(nc.gpsimd.affine_select(out=left, in_=left, compare_op=ALU.is_ge, fill=0.0, base=2 * s - 1,
                                         pattern=[[2 * s, nb], [0, s]], channel_multiplier=-1))
            done()
            diag(invmask[:, q, :], [[-1, P]], 1.0)
        odd = z1mask[:, :].rearrange("p (b e) -> p b e", e=2)[:, :, 1]
        step(nc.gpsimd.affine_select(out=odd, in_=odd, compare_op=ALU.not_equal, fill=-1.0, base=0,
                                     pattern=[[-2, P // 2]], channel_multiplier=1))
        done()
        diag(z1mask[:, :], [[-1, P]], 1.0)
        for q, op in ((0, ALU.is_ge), (1, ALU.is_gt), (2, ALU.is_ge)):
            step(nc.gpsimd.affine_select(out=tri[:, q, :], in_=tri[:, q, :], compare_op=op, fill=0.0, base=0,
                                         pattern=[[1, P]], channel_multiplier=-1))
        step(nc.gpsimd.affine_select(out=tri4[:, :, :], in_=tri4[:, :, :], compare_op=ALU.is_gt, fill=0.0, base=0,
                                     pattern=[[0, 4], [1, P]], channel_multiplier=-1))
        for b in (0, 2):
            step(nc.gpsimd.affine_select(out=dist[:, b, :], in_=dist[:, b, :], compare_op=ALU.is_ge, fill=FAR, base=0,
                                         pattern=[[-1, P]], channel_multiplier=1))
        done()
        nc.gpsimd.memset(rcol[:, :], 0.0).then_inc(sem("all_consts"), 1)
        pool_rwkv(pool)


    @block.tensor
    def _(pe):
        def transpose(o, i, n=P):
            return nc.tensor.transpose(o, i, ident[0:n, 0:n])

        def product(o, a_hi, a_lo, b_hi, b_lo, first, last, open_=False):
            nc.tensor.matmul(o, a_hi, b_hi, start=first, stop=False, skip_group_check=open_)
            nc.tensor.matmul(o, a_hi, b_lo, start=False, stop=False, skip_group_check=open_)
            return nc.tensor.matmul(o, a_lo, b_hi, start=False, stop=last, skip_group_check=open_)

        def fp_unit(o, u, width=P, h=(hhi, hlo)):
            for k in range(KT):
                m = product(o, whi[:, u, P * k:P * k + width], wlo[:, u, P * k:P * k + width],
                            h[0][:, k, :], h[1][:, k, :], k == 0, k == KT - 1)
            return m

        def fp_slot(n, b, h=(hhi, hlo)):
            for half in range(2):
                u = 2 * (n % RING) + half
                pe.wait_ge(lo_ready[u], n // RING + 1)
                m = fp_unit(bank[b][:, S * half:S * half + S], u, h=h)
                m.then_inc(unit_used[u], 1)

        def tp_slot(n, b, h=(hhi, hlo)):
            u = 2 * (n % RING)
            pe.wait_ge(lo_ready[u + 1], n // RING + 1)
            for t in range(TT):
                for k in range(KT if t < TT - 1 else KT - 1):
                    product(bank[b][:, 256 * t:256 * t + 256], h[0][:, k, P * t:P * t + P],
                            h[1][:, k, P * t:P * t + P], whi[:, u:u + 2, P * k:P * k + P],
                            wlo[:, u:u + 2, P * k:P * k + P], k == 0, k == KT - 1, t == TT - 1)
            for half in range(2):
                k, c = KT - 1, 256 * (TT - 1) + P * half
                product(bank[b][:, c:c + P], h[0][:, k, P * t:P * t + P], h[1][:, k, P * t:P * t + P],
                        whi[:, u + half, P * k:P * k + P], wlo[:, u + half, P * k:P * k + P], False, True, True)\
                    .then_inc(unit_used[u + half], 1)

        def head_stats(name, nt, src, b, rb, at0=0, ready=None):
            pe.wait_ge(*head_count(name, "sq", nt if ready is None else ready))
            for t in range(TT):
                for p in range(nt):
                    m = nc.tensor.matmul(bank[b][:, 2 * nt * t + 2 * p:2 * nt * t + 2 * p + 2],
                                         src[:, p, P * t:P * t + P], head_sel[:, :], start=True, stop=True)
            m.then_inc(sem("head_stat"), 1)

        def head_spread(name, nt, src, rb):
            pe.wait_ge(*head_count(name, "wide", 1))
            wide = fl(src).rearrange("p (t c) -> p t c", t=TT)
            for p in range(nt):
                if p % 2 == 0 and p // 2 >= len(rb):
                    pe.wait_ge(*head_count(name, "done", 2 * (p // 2 - len(rb)) + 2))
                for t in range(TT):
                    c = S * (p % 2) + P * t
                    m = transpose(bank[rb[p // 2 % len(rb)]][:, c:c + P], wide[:, t, P * p:P * p + P])
                if p % 2 or p == nt - 1:
                    m.then_inc(sem("head_rb"), 1)

        def square_sums(name, j):
            i = stat_no[name]
            pe.wait_ge(sem("sq_ready"), 4 * i + j + 1)
            for k in (2 * j, 2 * j + 1):
                m = nc.tensor.matmul(bank[6][:, 0:S], ones[:, :], sq[:, k, :], start=(k == 0), stop=(k == KT - 1),
                                     skip_group_check=True)
            if j == 3:
                m.then_inc(sem("norm_stat"), 1)

        def first_pair(name, u0, o0, u1, o1, n0, n1):
            pe.wait_ge(lo_ready[u0], n0 // RING + 1)
            pe.wait_ge(lo_ready[u1], n1 // RING + 1)
            for k in range(KT):
                pe.wait_ge(sem("h_ready"), 8 * norm_no[name] + k + 1)
                for o, u in ((o0, u0), (o1, u1)):
                    m = product(o, whi[:, u, P * k:P * k + P], wlo[:, u, P * k:P * k + P], H[name][0][:, k, :], H[name][1][:, k, :],
                                k == 0 and u == u0, k == KT - 1, True)
                    if k == KT - 1:
                        m.then_inc(unit_used[u], 1)
                if name in stat_no and k % 2:
                    square_sums(name, k // 2)

        def first_slot(name, n, b):
            u = 2 * (n % RING)
            first_pair(name, u, bank[b][:, 0:S], u + 1, bank[b][:, S:2 * S], n, n)

        def ffn(f):
            n0, j0 = n_ffn[f], NJ * f
            u1, u3, u2 = (2 * ((n0 + c) % RING) for c in range(3))
            r1, r3, r2 = ((n0 + c) // RING for c in range(3))

            def h(j, half, r, width=P):
                pe.wait_ge(sem("pre_ready"), j0 + j)
                b = bank[4 + half]
                pe.wait_ge(lo_ready[u1 + half], r + r1 + 1)
                fp_unit(b[0:width, 0:S], u1 + half, width, H[f"ffn{f}"]).then_inc(unit_used[u1 + half], 1)
                pe.wait_ge(lo_ready[u3 + half], r + r3 + 1)
                fp_unit(b[0:width, S:2 * S], u3 + half, width, H[f"ffn{f}"]).then_inc(unit_used[u3 + half], 1)

            def o(j, half, r, rows=P, last=False):
                u = u2 + half
                pe.wait_ge(sem("g_ready"), j0 + j + 1)
                pe.wait_ge(lo_ready[u], r + r2 + 1)
                for d in range(KT):
                    m = product(bank[d // 2][:, S * (d % 2):S * (d % 2) + S], whi[0:rows, u, P * d:P * d + P],
                                wlo[0:rows, u, P * d:P * d + P], ghi[0:rows, half, :], glo[0:rows, half, :],
                                False, last, True)
                m.then_inc(unit_used[u], 1)

            first_pair(f"ffn{f}", u1, bank[4][:, 0:S], u3, bank[4][:, S:2 * S], n0, n0 + 1)
            for b in range(4):
                nc.tensor.matmul(bank[b][:, :], zw[:, :], zm[:, :], start=True, stop=False, skip_group_check=True)
            def double(t, between=None):
                h(2 * t + 1, 1, t)
                o(2 * t, 0, t)
                if between:
                    between(2 * t)
                h(2 * t + 2, 0, t + 1)
                o(2 * t + 1, 1, t)
                if between:
                    between(2 * t + 1)

            first = PEEL if f == 0 else 0
            for t in range(first):
                double(t, mem_step)
            with pe.Fori(first, FULL) as t:
                double(t)
            h(NJ - 1, 1, FULL, LASTROWS)
            o(NJ - 2, 0, FULL)
            o(NJ - 1, 1, FULL, LASTROWS, True)

        def mem_step(n):
            if n == 0:
                pe.wait_ge(sem("rows_loaded"), 16 * N_ROW_LOADS)
                transpose(bank[7][:, 0:rowsA], prow[0:rowsA, 0, :], rowsA)
                transpose(bank[7][:, rowsA:rowsA + rowsB], prow[0:rowsB, 1, :], rowsB).then_inc(sem("prm_t"), 1)
            if n in (2, 3):
                pe.wait_ge(sem("mem_scaled"), 2)
                if n == 2:
                    pe.wait_ge(sem("prm_ready"), 1)
                for j in (2 * (n - 2), 2 * (n - 2) + 1):
                    if j >= 2:
                        pe.wait_ge(sem("mt_out"), j - 1)
                    for k in (2 * j, 2 * j + 1):
                        for t in range(TT):
                            c = S * (k % 2) + P * t
                            m = transpose(bank[6 + j % 2][:, c:c + P], mrow[:, t, P * k:P * k + P])
                    m.then_inc(sem("m_t"), 1)

        pe.wait_ge(sem("base_consts"), 2)
        pe.wait_ge(sem("first_rows"), 16)
        transpose(bank[7][:, 0:16], prow[0:16, 0, :], 16).then_inc(sem("gains_t"), 1)
        pe.wait_ge(sem("x_loaded"), 16)
        for j in range(4):
            for k in (2 * j, 2 * j + 1):
                for t in range(TT):
                    c = S * (k % 2) + P * t
                    m = transpose(bank[j][:, c:c + P], xrow[:, t, P * k:P * k + P])
            m.then_inc(sem("x_t"), 1)
        ffn(0)
        def attend(name):
            heads = HEADS[name]
            pairs = len(heads) // 2

            def scores(n):
                q, k, _, _ = heads[n]
                if n >= 3:
                    pe.wait_ge(*attn_count(name, "exp", n - 2))
                for t in range(TT):
                    c = query_cols(heads[n], t)
                    m = nc.tensor.matmul(bank[n % 3][:, c], q[:, tokens(t)], k[:, 0:c.stop - c.start], start=True, stop=True)
                m.then_inc(sem("attn_scores"), 1)

            def turn(n):
                pe.wait_ge(*attn_count(name, "exp", n + 1))
                if n >= 2:
                    pe.wait_ge(*attn_count(name, "turned", n - 1))
                for i in range(len(blocks(heads[n]))):
                    m = transpose(bank[3 + n % 2][:, P * i:P * i + P], prb[:, n % 3, P * i:P * i + P])
                m.then_inc(sem("attn_turn"), 1)

            def values(n):
                pe.wait_ge(*attn_count(name, "turned", n + 1))
                if n >= 2:
                    pe.wait_ge(*attn_count(name, "rows", n - 1))
                mine = blocks(heads[n])
                for i, (t, kt) in enumerate(mine):
                    m = nc.tensor.matmul(bank[5 + n % 2][:, HD * t:HD * t + HD], prT[:, n % 2, P * i:P * i + P], heads[n][2](kt),
                                         start=(kt == 0), stop=(i + 1 == len(mine) or mine[i + 1][0] != t))
                m.then_inc(sem("attn_values"), 1)

            def rows_turn(p):
                pe.wait_ge(*attn_count(name, "rows", 2 * p + 2))
                if p >= 1:
                    pe.wait_ge(*mixed(name, p - 1))
                for t in range(TT):
                    m = transpose(bank[7][:, P * t:P * t + P], orow[:, p % 2, t, :])
                m.then_inc(sem("attn_rows_t"), 1)

            scores(0)
            scores(1)
            for n in range(len(heads)):
                if n + 2 < len(heads):
                    scores(n + 2)
                if n >= 1:
                    values(n - 1)
                turn(n)
                if n >= 4 and n % 2 == 0:
                    rows_turn(n // 2 - 2)
            values(len(heads) - 1)
            rows_turn(pairs - 2)
            rows_turn(pairs - 1)

        def w_out(l):
            pe.wait_ge(sem(f"mixed{l}"), KT)
            for c in range(4):
                fp_slot(n_wout[l] + c, c)

        pe.wait_ge(sem("all_consts"), 1)
        def mem_h(l):
            pe.wait_ge(sem("mem_h"), 8 * l + 8)
            return mem_h_at[l, "hi"], mem_h_at[l, "lo"]

        fp_slot(n_mem, 4, mem_h(0))
        for j in range(4):
            square_sums("mix0", j)
        tp_slot(n_mem + 1, 5, mem_h(0))
        fp_slot(n_mem + 2, 3, mem_h(1))
        tp_slot(n_mem + 3, 2, mem_h(1))
        pe.wait_ge(sem("h_ready"), 8 * norm_no["mix0"] + 8)

        def w_in(i):
            if i >= 4:
                pe.wait_ge(sem("win_free"), i - 3)
            fp_slot(n_win + i, i % 4)

        def loras():
            pe.wait_ge(sem("lora_loaded"), 48)
            pe.wait_ge(sem("lora_in"), 2)
            for p in range(NP_):
                if p >= 2:
                    pe.wait_ge(sem("a_ready"), p - 1)
                nc.tensor.matmul(bank[4 + p % 2][:, 0:S], la[0:HD, P * p:P * p + P], wa[0:HD, :], start=True, stop=True)
                nc.tensor.matmul(bank[6 + p % 2][:, 0:S], la[HD:P, P * p:P * p + P], wa[HD:P, :], start=True, stop=True)\
                    .then_inc(sem("lora_wa"), 1)
            pe.wait_ge(sem("a_ready"), NP_)
            for q in range(3):
                if q == 2:
                    pe.wait_ge(sem("g_out"), 1)
                for p in (2 * q, 2 * q + 1):
                    m = nc.tensor.matmul(bank[6 + q % 2][:, S * (p % 2):S * (p % 2) + S], lg[:, P * p:P * p + P], gd[:, :],
                                         start=True, stop=True)
                m.then_inc(sem("lora_g"), 1)

        def to_tokens(j, src, ch, q):
            if j >= 2:
                pe.wait_ge(sem("tp_out"), j - 1)
            for p in range(3):
                m = transpose(bank[4 + j % 2][:, P * p:P * p + P], src[:, 3 * q + p, tokens(ch)])
            m.then_inc(sem("tp_t"), 1)

        w_in(0)
        head_stats("kn0", 2, sq[:, 0:2, :], 6, None, ready=1)
        w_in(1)
        head_spread("kn0", 2, sq[:, 0:2, :], [7])
        head_stats("kn1", 2, sq[:, 2:4, :], 6, None, ready=1)
        pe.wait_ge(sem("mem_v_done"), 2)
        w_in(2)
        pe.wait_ge(*head_count("kn0", "done", 2))
        head_spread("kn1", 2, sq[:, 2:4, :], [7])
        pe.wait_ge(*head_count("kn1", "done", 2))
        loras()
        w_in(3)
        w_in(4)
        w_in(5)
        pe.wait_ge(sem("g_out"), 3)
        head_stats("kkn", NP_, sq, 6, None)
        w_in(6)
        head_spread("kkn", NP_, sq[:, 0:NP_, :], [7, 6])
        for i in range(7, 11):
            w_in(i)
        pe.wait_ge(sem("win_free"), 10)
        pe.wait_ge(sem("a_ready"), NP_)
        for j in range(4):
            to_tokens(j, uv, j // 2, j % 2)
        head_stats("bn", NP_, sq, 6, None)
        head_spread("bn", NP_, sq[:, 0:NP_, :], [7, 6])
        pe.wait_ge(sem("powers_used"), 4)
        for j in range(4):
            to_tokens(4 + j, (ua, uk)[j // 2], 0, j % 2)

        def triangle(g):
            if g >= 2:
                pe.wait_ge(sem("lt_done"), g - 1)
            for q in range(4):
                par, ch, p = INSTANCES[4 * g + q]
                m = nc.tensor.matmul(bank[g % 2][:, P * q:P * q + P], ua[part(par), p, tokens(ch)],
                                     KR[part(par), 2 * p + ch, 0, :], start=True, stop=True)
            m.then_inc(sem("lt_ps"), 1)

        def first_blocks(g):
            pe.wait_ge(sem("z_done"), g + 1)
            if g >= 2:
                pe.wait_ge(sem("x_done"), g - 1)
            for q in range(4):
                m = transpose(bank[2 + g % 2][:, P * q:P * q + P], Zi[:, 4 * g + q, :])
            m.then_inc(sem("x1_t"), 1)

        triangle(0)
        triangle(1)
        for g in range(NG):
            if g + 2 < NG:
                first_blocks(g)
                triangle(g + 2)
            else:
                first_blocks(g)

        def level(lv, last=False):
            for g in range(NG):
                pe.wait_ge(sem("x_done"), NG * lv + g + 1)
                if g >= 2:
                    pe.wait_ge(sem("r_done"), NG * lv + g - 1)
                for q in range(4):
                    i = 4 * g + q
                    m = nc.tensor.matmul(bank[g % 2][:, P * q:P * q + P], LT[:, i, :], Xi[:, i, :], start=True, stop=True)
                m.then_inc(sem("inv_a"), 1)
            pe.wait_ge(sem("z_done"), NG * lv + NG)
            for g in range(NG):
                pe.wait_ge(sem("r_done"), NG * lv + g + 1)
                if not last:
                    if g >= 2:
                        pe.wait_ge(sem("x_done"), NG * lv + NG + g - 1)
                    for q in range(4):
                        i = 4 * g + q
                        m = nc.tensor.matmul(bank[2 + g % 2][:, P * q:P * q + P], Zi[:, i, :], Ri[:, i, :], start=True, stop=True)
                    m.then_inc(sem("inv_b"), 1)
                if g >= 2:
                    pe.wait_ge(sem("z_done"), NG * lv + NG + g - 1)
                for q in range(4):
                    i = 4 * g + q
                    m = nc.tensor.matmul(bank[4 + g % 2][:, P * q:P * q + P], Ri[:, i, :], Zi[:, i, :], start=True, stop=True)
                m.then_inc(sem("inv_c"), 1)

        with pe.Fori(0, 5) as lv:
            level(lv)
        level(5, True)

        def triangles(lo, hi):
            for n in range(lo, hi):
                par, ch, p = TRIANGLES[n]
                if n == 0:
                    pe.wait_ge(*head_count("bn", "done", NP_))
                if n >= 2:
                    pe.wait_ge(sem("nmq_done"), n - 1)
                b = bank[6 + n % 2]
                nc.tensor.matmul(b[:, 0:P], ua[part(par), p, tokens(ch)], KR[part(par), 2 * p + ch, 1, :],
                                 start=True, stop=True)
                nc.tensor.matmul(b[:, P:3 * P], uk[part(par), p, tokens(ch)], KR[part(par), 2 * p + ch, :, :], start=True, stop=True).then_inc(sem("nmq_ps"), 1)

        def rhs(ch, par):
            pe.wait_ge(sem("nmq_done"), NH * ch + NP_ * par + NP_)
            if ch:
                pe.wait_ge(sem("state"), 1)
            for p in range(NP_):
                i, h = inst(par, ch, p), 2 * p + par
                o = bank[par][:, HD * p:HD * p + HD]
                m = nc.tensor.matmul(o, MQ[:, i, 0:P], vt[:, ch, HD * h:HD * h + HD], start=True, stop=(ch == 0))
                if ch:
                    m = nc.tensor.matmul(o, KR[part(par), 2 * p + 1, 0, :], sT[part(par), p, :], start=False, stop=True)
            m.then_inc(sem("rhs_ps"), 1)

        def solve(ch, par):
            pe.wait_ge(sem("rhs_out"), 2 * ch + par + 1)
            if ch == 0 and par == 0:
                pe.wait_ge(sem("z_done"), NG * 7)
            for p in range(NP_):
                m = nc.tensor.matmul(bank[2 + par][:, HD * p:HD * p + HD], Zi[:, inst(par, ch, p), :], rhsb[:, NP_ * par + p, :],
                                     start=True, stop=True)
            m.then_inc(sem("u_ps"), 1)

        def outputs(ch):
            pe.wait_ge(sem("u_out"), 2 * ch + 2)
            if ch:
                pe.wait_ge(sem("y_out"), 2)
            for par in range(2):
                for p in range(NP_):
                    i, h = inst(par, ch, p), 2 * p + par
                    o = bank[4 + p // 3][part(par), P * (p % 3):P * (p % 3) + P]
                    nc.tensor.matmul(o, uneg[:, NP_ * par + p, :], LT[:, i, :], start=True, stop=False)
                    m = nc.tensor.matmul(o, vt[:, ch, HD * h:HD * h + HD], MQ[:, i, P:2 * P], start=False, stop=(ch == 0))
                    if ch:
                        m = nc.tensor.matmul(o, sT[part(par), p, :], KR[part(par), 2 * p + 1, 1, :], start=False, stop=True)
            m.then_inc(sem("y_ps"), 1)

        def state():
            pe.wait_ge(sem("u_out"), 2)
            for par in range(2):
                for p in range(NP_):
                    h = 2 * p + par
                    o = bank[0][part(par), HD * p:HD * p + HD]
                    nc.tensor.matmul(o, bt[:, HD * h:HD * h + HD], uneg[:, NP_ * par + p, :], start=True, stop=False)
                    m = nc.tensor.matmul(o, ktp[:, HD * h:HD * h + HD], vt[:, 0, HD * h:HD * h + HD], start=False, stop=True)
            m.then_inc(sem("s_ps"), 1)

        pe.wait_ge(sem("tp_out"), 8)
        triangles(0, NH)
        rhs(0, 0)
        rhs(0, 1)
        triangles(NH, NH + NP_)
        solve(0, 0)
        solve(0, 1)
        triangles(NH + NP_, 2 * NH)
        state()
        outputs(0)
        rhs(1, 0)
        rhs(1, 1)
        solve(1, 0)
        solve(1, 1)
        outputs(1)
        pe.wait_ge(sem("y_out"), 4)
        for q in range(3):
            for p in (2 * q, 2 * q + 1):
                m = nc.tensor.matmul(bank[q][:, S * (p % 2):S * (p % 2) + S], centre[:, :], yT[:, p, :], start=True, stop=True)
            m.then_inc(sem("centred"), 1)
        head_stats("gn", NP_, sq, 6, None, ready=3)
        head_spread("gn", NP_, sq[:, 0:NP_, :], [7, 6])
        pe.wait_ge(*head_count("gn", "done", NP_))
        head_stats("mq0", 2, sq[:, 0:2, :], 6, None, ready=1)
        head_spread("mq0", 2, sq[:, 0:2, :], [7])
        pe.wait_ge(*head_count("mq0", "done", 2))
        attend("at0")
        w_out(0)
        ffn(1)
        first_slot("kv", n_kv, 0)
        pe.wait_ge(sem("rb_ready"), stat_no["kv"] + 1)
        for t in range(TT):
            m = transpose(bank[7][:, P * t:P * t + P], rb[:, P * t:P * t + P])
        m.then_inc(sem("rb_t"), 1)
        for c in range(1, 6):
            if c >= 4:
                pe.wait_ge(sem("k_out"), c - 3)
            (fp_slot if c < 3 else tp_slot)(n_kv + c, c % 4)
        head_stats("kvn", NP_, sq, 6, None, ready=3)
        head_spread("kvn", NP_, sq[:, 0:NP_, :], [7, 6])
        pe.wait_ge(sem("v_out"), 3)
        ffn(2)
        first_slot("mix1", n_bin, 0)
        for c in range(1, 4):
            fp_slot(n_bin + c, c)
        head_stats("bq", NP_, sq, 6, None, ready=3)
        head_spread("bq", NP_, sq[:, 0:NP_, :], [7, 6])
        pe.wait_ge(*head_count("bq", "done", NP_))
        head_stats("mq1", 2, sq[:, NP_:NP_ + 2, :], 6, None, ready=1)
        head_spread("mq1", 2, sq[:, NP_:NP_ + 2, :], [7])
        pe.wait_ge(*head_count("mq1", "done", 2))
        attend("at1")
        w_out(1)
        ffn(3)
        for t in range(TT):
            for half in range(2):
                b = 4 + 2 * t + half
                if t == 0 and half == 0:
                    pe.wait_ge(sem("x_ready"), UPD_LAST)
                for q in range(4):
                    k = 4 * half + q
                    m = transpose(bank[b][:, P * q:P * q + P], xT[:, k, P * t:P * t + P])
                m.then_inc(sem("out_t"), 1)

    @block.scalar
    def _(act):
        def split(n, half, r=None, rows=False, part=P, tail=False):
            u = 2 * (n % RING) + half
            if r is None:
                r = n // RING
            if tail:
                act.wait_ge(tail_ready, 16 * tail)
            else:
                act.wait_ge(raw_ready[n % RING], 16 * r + 16)
            if not (isinstance(r, int) and r == 0):
                act.wait_ge(unit_used[u], r)
            nc.scalar.activation(unit_dst(whi, n, half, rows)[0:part], unit_src(n, half, rows)[0:part], ACT.Copy)\
                .then_inc(hi_ready[u], 1)

        def split2(n):
            split(n, 0)
            split(n, 1)

        def root(name):
            act.wait_ge(*head_count(name, "var", 1))
            v = STAT[name]
            nc.scalar.activation(v, v, ACT.Sqrt).then_inc(sem("head_std"), 1)

        def split_units(name, later):
            n, units = PHASE[name]
            for c, half in units[later]:
                split(n + c, half, rows=(name[0:3] == "ffn" and c == 2))

        def h_high(name, k):
            nc.scalar.activation(H[name][0][:, k, :], xT[:, k, :], ACT.Copy, scale=col(norm_gain[name] + k)).then_inc(sem("hhi_ready"), 1)

        def root_of_sums(name):
            act.wait_ge(sem("norm_var"), stat_no[name] + 1)
            nc.scalar.activation(rb[:, :], rb[:, :], ACT.Sqrt).then_inc(sem("norm_std"), 1)

        def norm(name):
            i = stat_no[name]
            if name != "ffn0":
                split_units(name, 0)
            for w, v in NORM_WAITS[name]:
                act.wait_ge(sem(w), v)
            for j in range(4):
                act.wait_ge(sem("x_ready"), upd[norm_after[name]] - 4 + j + 1)
                if name != "mix0":
                    h_high(name, 2 * j)
                    h_high(name, 2 * j + 1)
                nc.scalar.activation(sq[:, 2 * j:2 * j + 2, :], xT[:, 2 * j:2 * j + 2, :], ACT.Square)\
                    .then_inc(sem("sq_ready"), 1)
            if name == "ffn0":
                split_units(name, 0)
            split_units(name, 1)
            root_of_sums(name)
            if name == "mix0":
                for k in range(KT):
                    act.wait_ge(sem("hf_ready"), k + 1)
                    nc.scalar.activation(hhi[:, k, :], sq[:, k, :], ACT.Copy).then_inc(sem("hhi_ready"), 1)

        def ffn(f):
            n0, j0 = n_ffn[f], NJ * f
            q = [(n0 + c) // RING for c in range(3)]

            def silu(j, half, rows=P):
                act.wait_ge(sem("pre_ready"), j0 + 1 + j + 1)
                nc.scalar.activation(sg[0:rows, half, :], pre[0:rows, half, 0:S], ACT.Silu).then_inc(sem("silu_done"), 1)

            def g_hi(j, half, rows=P):
                act.wait_ge(sem("g32_done"), j0 + j + 1)
                nc.scalar.activation(ghi[0:rows, half, :], g32[0:rows, half, :], ACT.Copy).then_inc(sem("ghi_done"), 1)

            def double(t, between=None):
                silu(2 * t, 0)
                split(n0, 0, t + 1 + q[0])
                g_hi(2 * t, 0)
                split(n0 + 1, 0, t + 1 + q[1])
                split(n0 + 2, 1, t + q[2], True)
                if between:
                    between(2 * t)
                silu(2 * t + 1, 1)
                split(n0, 1, t + 1 + q[0])
                g_hi(2 * t + 1, 1)
                split(n0 + 1, 1, t + 1 + q[1])
                split(n0 + 2, 0, t + 1 + q[2], True)
                if between:
                    between(2 * t + 1)

            first = PEEL if f == 0 else 0
            for t in range(first):
                double(t, mem_step)
            with act.Fori(first, FULL) as t:
                double(t)
            silu(NJ - 2, 0)
            g_hi(NJ - 2, 0)
            split(n0 + 2, 1, FULL + q[2], True, LASTROWS, tail=f + 1)
            silu(NJ - 1, 1, LASTROWS)
            g_hi(NJ - 1, 1, LASTROWS)

        def mem_step(n):
            if n == 0:
                act.wait_ge(sem("mem_var"), 1)
                nc.scalar.activation(stat[:, 17, 0:2], stat[:, 17, 0:2], ACT.Sqrt).then_inc(sem("mem_std"), 1)
            if n >= 4:
                l, k0 = (n - 4) // 2, 4 * (n % 2)
                act.wait_ge(sem("mt_out"), k0 // 2 + 2)
                for k in range(k0, k0 + 4):
                    nc.scalar.activation(mem_h_at[l, "hi"][:, k, :], mT[:, k, :], ACT.Copy, scale=col(G_MEM + 8 * l + k))\
                        .then_inc(sem("mhi_ready"), 1)

        act.wait_ge(sem("gains_ready"), 1)
        norm("ffn0")
        act.wait_ge(sem("mem_loaded"), 16)
        for t in range(TT):
            m = nc.scalar.activation(sq[:, 4 * t:4 * t + 4, :].rearrange("p a b -> p (a b)"), mrow[:, t, :], ACT.Square,
                                     accum_out=stat[:, 17, t:t + 1])
        m.then_inc(sem("mem_ss"), 1)
        ffn(0)
        def attend(name):
            heads = HEADS[name]

            def exps(n):
                act.wait_ge(*attn_count(name, "max", n + 1))
                for t in range(TT):
                    c = query_cols(heads[n], t)
                    src = bank[n % 3][:, c] if heads[n][3] is None else prb[:, n % 3, c]
                    m = nc.scalar.activation(prb[:, n % 3, c], src, ACT.Exp, bias=sml[:, n % 4, t:t + 1], scale=SCALE,
                                             accum_out=sml[:, n % 4, 2 + t:3 + t])
                m.then_inc(sem("attn_exp"), 1)

            def turned(n):
                act.wait_ge(*attn_count(name, "turn", n + 1))
                if n >= 2:
                    act.wait_ge(*attn_count(name, "values", n - 1))
                c = P * len(blocks(heads[n]))
                nc.scalar.activation(prT[:, n % 2, 0:c], bank[3 + n % 2][:, 0:c], ACT.Copy).then_inc(sem("attn_turned"), 1)

            def pair(p):
                high(int(name[2]), OUT_TILE[name] + p, bank[7][:, 0:S],
                     *attn_count(name, "rows_t", p + 1))

            exps(0)
            for n in range(len(heads)):
                if n + 1 < len(heads):
                    exps(n + 1)
                turned(n)
                if n >= 5 and n % 2:
                    pair(n // 2 - 2)
            pair(len(heads) // 2 - 2)
            pair(len(heads) // 2 - 1)

        def high(l, k, src, w, v):
            act.wait_ge(w, v)
            nc.scalar.activation(hhi[:, k, :], src, ACT.Copy).then_inc(sem(f"mixhi{l}"), 1)

        def split_w_out(l):
            for c in range(3):
                split2(n_wout[l] + c)

        norm("mix0")

        def w_in_out(i):
            slot_done(act, n_win + i)
            b = bank[i % 4]
            for half in range(2):
                c = W_IN_ORDER[i] * 2 + half
                m = nc.scalar.activation(U_TILES[i][half], b[:, S * half:S * half + S], ACT.Copy, scale=omu[:, c:c + 1])
            m.then_inc(sem("shift_a"), 1)
            if i + 3 < 11:
                split2(n_win + i + 3)

        split2(n_mem + 3)
        for c in range(3):
            split2(n_win + c)
        act.wait_ge(sem("mem_k_out"), 2)
        act.wait_ge(sem("h_ready"), 8 * norm_no["mix0"] + 8)
        for l in range(2):
            nc.scalar.activation(sq[:, 2 * l:2 * l + 2, :], kmT[:, l, :, :], ACT.Square).then_inc(sem("head_sq"), 1)
        for l in range(2):
            slot_done(act, n_mem + 2 * l + 1)
            nc.scalar.activation(fl(vm[:, l, :, :]), bank[(5, 2)[l]][:, :], ACT.Copy).then_inc(sem("mem_v_done"), 1)
        root("kn0")
        w_in_out(0)
        root("kn1")
        act.wait_ge(sem("win_free"), 1)
        nc.scalar.activation(wa[0:HD, :], wa[0:HD, :], ACT.Tanh).then_inc(sem("lora_in"), 1)
        nc.scalar.activation(gd[:, :], gd[:, :], ACT.Sigmoid).then_inc(sem("lora_in"), 1)
        w_in_out(1)
        w_in_out(2)
        for p in range(NP_):
            act.wait_ge(sem("lora_wa"), p + 1)
            nc.scalar.activation(pw[:, 2 * p:2 * p + 2, 1:P + 1], bank[4 + p % 2][:, 0:S].rearrange("p (c t) -> p c t", c=2), ACT.Sigmoid,
                                 bias=col(C_W0 + p)).then_inc(sem("lw_ready"), 1)
            nc.scalar.activation(ua[:, p, :], bank[6 + p % 2][:, 0:S], ACT.Sigmoid, bias=col(C_A0 + p)).then_inc(sem("a_ready"), 1)
        for q in range(3):
            act.wait_ge(sem("lora_g"), q + 1)
            nc.scalar.activation(fl(gT[:, 2 * q:2 * q + 2, :]), bank[6 + q % 2][:, :], ACT.Copy).then_inc(sem("g_out"), 1)
        w_in_out(3)
        act.wait_ge(sem("win_free"), 4)
        for p in range(NP_):
            nc.scalar.activation(sq[:, p, :], uk[:, p, :], ACT.Square, scale=col(C_KK + p)).then_inc(sem("head_sq"), 1)
        w_in_out(4)
        w_in_out(5)
        root("kkn")
        w_in_out(6)
        act.wait_ge(sem("cum_ready"), 1)
        nc.scalar.activation(sfin[:, 1, :], c12[:, 1::2, 0], ACT.Exp, scale=-DECAY).then_inc(sem("mid_power"), 1)
        nc.scalar.activation(pr[:, :, :], pw[:, :, :], ACT.Exp, scale=-DECAY).then_inc(sem("powers"), 1)
        nc.scalar.activation(pw[:, :, :], pw[:, :, :], ACT.Exp, scale=DECAY).then_inc(sem("powers"), 1)
        for i in range(7, 10):
            w_in_out(i)
        slot_done(act, n_win + 10)
        nc.scalar.activation(fl(mq[:, :, :]), bank[10 % 4][:, :], ACT.Copy).then_inc(sem("mq_out"), 1)
        for j in range(8):
            act.wait_ge(sem("tp_t"), j + 1)
            if j == 4:
                act.wait_ge(sem("powers_used"), 4)
            q = j % 2
            dst = vt[:, j // 2, 384 * q:384 * q + 384] if j < 4 else (bt, ktp)[j // 2 - 2][:, 384 * q:384 * q + 384]
            nc.scalar.activation(dst, bank[4 + j % 2][:, 0:384], ACT.Copy).then_inc(sem("tp_out"), 1)
        for g in range(NG):
            act.wait_ge(sem("x1_t"), g + 1)
            nc.scalar.activation(fl(Xi[:, 4 * g:4 * g + 4, :]), bank[2 + g % 2][:, :], ACT.Copy).then_inc(sem("x_done"), 1)

        def level(lv, last=False):
            for g in range(NG):
                if not last:
                    act.wait_ge(sem("inv_b"), NG * lv + g + 1)
                    nc.scalar.activation(fl(Xi[:, 4 * g:4 * g + 4, :]), bank[2 + g % 2][:, :], ACT.Copy).then_inc(sem("x_done"), 1)
                act.wait_ge(sem("inv_c"), NG * lv + g + 1)
                nc.scalar.activation(fl(Zi[:, 4 * g:4 * g + 4, :]), bank[4 + g % 2][:, :], ACT.Copy).then_inc(sem("z_done"), 1)

        with act.Fori(0, 5) as lv:
            level(lv)
        level(5, True)
        for ch in range(2):
            for par in range(2):
                act.wait_ge(sem("rhs_ps"), 2 * ch + par + 1)
                nc.scalar.activation(fl(rhsb[:, NP_ * par:NP_ * par + NP_, :]), bank[par][:, 0:384], ACT.Copy)\
                    .then_inc(sem("rhs_out"), 1)
            for par in range(2):
                act.wait_ge(sem("u_ps"), 2 * ch + par + 1)
                if ch:
                    act.wait_ge(sem("y_ps"), 1)
                nc.scalar.activation(fl(uneg[:, NP_ * par:NP_ * par + NP_, :]), bank[2 + par][:, 0:384], ACT.Copy,
                                     scale=-1.0).then_inc(sem("u_out"), 1)
            act.wait_ge(sem("y_ps"), ch + 1)
            for q in range(2):
                nc.scalar.activation(yT[:, 3 * q:3 * q + 3, tokens(ch)], bank[4 + q][:, 0:384].rearrange("p (a t) -> p a t", a=3),
                                     ACT.Copy).then_inc(sem("y_out"), 1)
        split_w_out(0)
        for q in range(3):
            act.wait_ge(sem("d_out"), q + 1)
            nc.scalar.activation(sq[:, 2 * q:2 * q + 2, :], dT[:, 2 * q:2 * q + 2, :], ACT.Square).then_inc(sem("head_sq"), 1)
        root("gn")
        act.wait_ge(*head_count("gn", "done", NP_))
        nc.scalar.activation(sq[:, 0:2, :], mq[:, :, :], ACT.Square).then_inc(sem("head_sq"), 1)
        root("mq0")
        for p in range(NP_):
            high(0, p, dT[:, p, :], sem("mix_f"), p + 1)
        attend("at0")
        split2(n_wout[0] + 3)
        norm("ffn1")
        ffn(1)
        norm("kv")
        for c in range(6):
            if c < 3:
                act.wait_ge(sem("k_out"), c + 1)
                nc.scalar.activation(sq[:, 2 * c:2 * c + 2, :], kT[:, 2 * c:2 * c + 2, :], ACT.Square).then_inc(sem("head_sq"), 1)
                split2(n_kv + c + 3)
            else:
                slot_done(act, n_kv + c)
                act.wait_ge(sem("rcol_ready"), 1)
                for t in range(TT):
                    m = nc.scalar.activation(vt2[:, t, 256 * (c - 3):256 * (c - 3) + 256], bank[c % 4][:, S * t:S * t + S],
                                             ACT.Copy, scale=rcol[:, t:t + 1])
                m.then_inc(sem("v_out"), 1)
            if c == 2:
                root("kvn")
                for k in range(KT):
                    h_high("ffn2", k)
        split_units("ffn2", 0)
        split_units("ffn2", 1)
        ffn(2)
        norm("mix1")
        for c in range(4):
            act.wait_ge(sem("q_out"), c + 1)
            nc.scalar.activation(sq[:, 2 * c:2 * c + 2, :], qT[:, 2 * c:2 * c + 2, :], ACT.Square)\
                .then_inc(sem("head_sq"), 1)
            if c == 0:
                split2(n_bin + 3)
        root("bq")
        root("mq1")
        split_w_out(1)
        attend("at1")
        split2(n_wout[1] + 3)
        norm("ffn3")
        ffn(3)

    @block.vector
    def _(dve):
        TTo = nc.vector.tensor_tensor
        TS = nc.vector.tensor_scalar
        STT = nc.vector.scalar_tensor_tensor
        seq = sem("dve_seq")
        cnt = [0]

        def mark(ins):
            cnt[0] += 1
            ins.then_inc(seq, 1)
            return ins

        def settle():
            dve.wait_ge(seq, cnt[0])

        def split(n, half, r=None, rows=False, part=P):
            u = 2 * (n % RING) + half
            if r is None:
                r = n // RING
            dve.wait_ge(hi_ready[u], r + 1)
            TTo(unit_dst(wlo, n, half, rows)[0:part], unit_src(n, half, rows)[0:part],
                unit_dst(whi, n, half, rows)[0:part].bitcast(F32), ALU.subtract).then_inc(lo_ready[u], 1)

        def split2(n):
            split(n, 0)
            split(n, 1)

        def head_norm(name, nt, b, rb, sqv, src, dst, gain, eps=EPS, mode="rms"):
            flat = stat[:, SLOT[name], 0:4 * nt]
            dve.wait_ge(*head_count(name, "stat", 1))
            if mode == "sum":
                mark(nc.vector.tensor_copy(flat, bank[b][:, 0:4 * nt]))
            else:
                if mode == "rms":
                    TS(flat, bank[b][:, 0:4 * nt], 1.0 / HD, eps, ALU.mult, ALU.add).then_inc(sem("head_var"), 1)
                else:
                    nc.vector.tensor_copy(flat, bank[b][:, 0:4 * nt]).then_inc(sem("head_var"), 1)
                dve.wait_ge(*head_count(name, "std", 1))
                if mode == "l2":
                    mark(nc.vector.tensor_scalar_max(flat, flat, 1e-12))
                    settle()
                mark(nc.vector.reciprocal(flat, flat))
            settle()
            nc.vector.tensor_copy(fl(sqv).rearrange("p (n c) -> p n c", c=HD),
                                  flat.unsqueeze(2).broadcast_to([P, 4 * nt, HD])).then_inc(sem("head_wide"), 1)
            for p in range(nt):
                dve.wait_ge(*head_count(name, "rb", p // 2 + 1))
                r = bank[rb[p // 2 % len(rb)]][:, S * (p % 2):S * (p % 2) + S]
                if gain is None:
                    m = TTo(dst[:, p, :], src[:, p, :], r, ALU.mult)
                else:
                    m = STT(dst[:, p, :], src[:, p, :], gain(p), r, ALU.mult, ALU.mult)
                m.then_inc(sem("head_done"), 1)

        def norm_mix():
            root_of_sums("mix0")
            i = norm_no["mix0"]

            def low(k):
                dve.wait_ge(sem("hhi_ready"), 8 * i + k + 1)
                TTo(hlo[:, k, :], sq[:, k, :], hhi[:, k, :].bitcast(F32), ALU.subtract).then_inc(sem("h_ready"), 1)

            for k in range(KT):
                STT(sq[:, k, :], xT[:, k, :], col(norm_gain["mix0"] + k), rb[:, :], ALU.mult, ALU.mult).then_inc(sem("hf_ready"), 1)
                if k >= 2:
                    low(k - 2)
            low(KT - 2)
            low(KT - 1)

        def split_units(name, later):
            n, units = PHASE[name]
            for c, half in units[later]:
                split(n + c, half, rows=(name[0:3] == "ffn" and c == 2))

        def h_low(name, k):
            dve.wait_ge(sem("hhi_ready"), 8 * norm_no[name] + k + 1)
            hi, lo = H[name]
            STT(lo[:, k, :], xT[:, k, :], col(norm_gain[name] + k), hi[:, k, :].bitcast(F32), ALU.mult, ALU.subtract)\
                .then_inc(sem("h_ready"), 1)

        def root_of_sums(name):
            i = stat_no[name]
            dve.wait_ge(sem("norm_stat"), i + 1)
            TS(rb[:, :], bank[6][:, 0:S], 1.0 / D, EPS, ALU.mult, ALU.add).then_inc(sem("norm_var"), 1)
            dve.wait_ge(sem("norm_std"), i + 1)
            nc.vector.reciprocal(rb[:, :], rb[:, :]).then_inc(sem("rb_ready"), 1)
            dve.wait_ge(sem("rb_ready"), i + 1)

        def new_x(name, update):
            if name is None or name == "mix0":
                for b in range(4):
                    update(b)
                if name:
                    split_units(name, 1)
                return
            update(0)
            for b in range(4):
                if b < 3:
                    update(b + 1)
                h_low(name, 2 * b)
                h_low(name, 2 * b + 1)
            split_units(name, 1)
            root_of_sums(name)

        def by_rb(o, b, n=2):
            return TTo(o.rearrange("p (n s) -> p n s", n=n), b.rearrange("p (n s) -> p n s", n=n),
                       rb[0:o.shape[0], :].unsqueeze(1).broadcast_to([o.shape[0], n, S]), ALU.mult)

        def ffn(f, following):
            n0, j0 = n_ffn[f], NJ * f
            q = [(n0 + c) // RING for c in range(3)]

            def normed(half, r, rows=P):
                dve.wait_ge(unit_used[2 * ((n0 + 1) % RING) + half], r + q[1] + 1)
                by_rb(pre[0:rows, half, :], bank[4 + half][0:rows, :]).then_inc(sem("pre_ready"), 1)

            def gate(j, half, rows=P):
                dve.wait_ge(sem("silu_done"), j0 + j + 1)
                TTo(g32[0:rows, half, :], sg[0:rows, half, :], pre[0:rows, half, S:2 * S], ALU.mult)\
                    .then_inc(sem("g32_done"), 1)

            def g_lo(j, half, rows=P):
                dve.wait_ge(sem("ghi_done"), j0 + j + 1)
                TTo(glo[0:rows, half, :], g32[0:rows, half, :], ghi[0:rows, half, :].bitcast(F32), ALU.subtract)\
                    .then_inc(sem("g_ready"), 1)

            def double(t, between=None):
                normed(0, t)
                split(n0, 0, t + 1 + q[0])
                gate(2 * t, 0)
                g_lo(2 * t, 0)
                split(n0 + 1, 0, t + 1 + q[1])
                split(n0 + 2, 1, t + q[2], True)
                if between:
                    between(2 * t)
                normed(1, t)
                split(n0, 1, t + 1 + q[0])
                gate(2 * t + 1, 1)
                g_lo(2 * t + 1, 1)
                split(n0 + 1, 1, t + 1 + q[1])
                split(n0 + 2, 0, t + 1 + q[2], True)
                if between:
                    between(2 * t + 1)

            first = PEEL if f == 0 else 0
            for t in range(first):
                double(t, mem_step)
            with dve.Fori(first, FULL) as t:
                double(t)
            normed(0, FULL)
            gate(NJ - 2, 0)
            g_lo(NJ - 2, 0)
            split(n0 + 2, 1, FULL + q[2], True, LASTROWS)
            normed(1, FULL, LASTROWS)
            gate(NJ - 1, 1, LASTROWS)
            g_lo(NJ - 1, 1, LASTROWS)
            if following is not None:
                split_units(following, 0)
            slot_done(dve, n0 + 3 * FULL + 2)

            def update(b):
                STT(fl(xT[:, 2 * b:2 * b + 2, :]), bank[b][:, :], 0.5, fl(xT[:, 2 * b:2 * b + 2, :]), ALU.mult, ALU.add)\
                    .then_inc(sem("x_ready"), 1)
            new_x(following, update)

        nc.vector.memset(stat[:, 20, :], 0.0).then_inc(sem("pre_ready"), 1)
        def mem_step(n):
            if n == 0:
                dve.wait_ge(sem("mem_ss"), 1)
                TS(stat[:, 17, 0:2], stat[:, 17, 0:2], 1.0 / D, EPS, ALU.mult, ALU.add).then_inc(sem("mem_var"), 1)
            if n == 1:
                dve.wait_ge(sem("mem_std"), 1)
                mark(nc.vector.reciprocal(stat[:, 17, 0:2], stat[:, 17, 0:2]))
                settle()
                for t in range(TT):
                    TS(mrow[:, t, :], mrow[:, t, :], stat[:, 17, t:t + 1], None, ALU.mult).then_inc(sem("mem_scaled"), 1)
                dve.wait_ge(sem("prm_t"), 1)
                mark(nc.vector.tensor_copy(prm[:, 16:rowsA + rowsB], bank[7][:, 16:rowsA + rowsB]))
                settle()
                mark(TS(omu[:, 0:20], prm[:, C_MU:C_MU + 20], -1.0, 1.0, ALU.mult, ALU.add))
                TS(omu[:, 20:26], prm[:, C_KA:C_KA + 6], -1.0, 1.0, ALU.mult, ALU.add).then_inc(sem("prm_ready"), 1)
            if n in (3, 4):
                for j in (2 * (n - 3), 2 * (n - 3) + 1):
                    dve.wait_ge(sem("m_t"), j + 1)
                    nc.vector.tensor_copy(fl(mT[:, 2 * j:2 * j + 2, :]), bank[6 + j % 2][:, :]).then_inc(sem("mt_out"), 1)
            if n == 4:
                dve.wait_ge(sem("mt_out"), 4)
            if n >= 4:
                l, k0 = (n - 4) // 2, 4 * (n % 2)
                for k in range(k0, k0 + 4):
                    dve.wait_ge(sem("mhi_ready"), 8 * l + k + 1)
                    STT(mem_h_at[l, "lo"][:, k, :], mT[:, k, :], col(G_MEM + 8 * l + k), mem_h_at[l, "hi"][:, k, :].bitcast(F32),
                        ALU.mult, ALU.subtract).then_inc(sem("mem_h"), 1)

        dve.wait_ge(sem("gains_t"), 1)
        nc.vector.tensor_copy(prm[:, 0:16], bank[7][:, 0:16]).then_inc(sem("gains_ready"), 1)
        dve.wait_ge(sem("gains_ready"), 1)
        for j in range(4):
            dve.wait_ge(sem("x_t"), j + 1)
            nc.vector.tensor_copy(fl(xT[:, 2 * j:2 * j + 2, :]), bank[j][:, :]).then_inc(sem("x_ready"), 1)
        for k in range(KT):
            h_low("ffn0", k)
        split_units("ffn0", 0)
        split_units("ffn0", 1)
        root_of_sums("ffn0")
        ffn(0, "mix0")
        def attend(name):
            heads = HEADS[name]

            def maxima(n):
                slope = heads[n][3]
                dve.wait_ge(*attn_count(name, "scores", n + 1))
                if n >= 3:
                    dve.wait_ge(*attn_count(name, "turn", n - 2))
                src = bank[n % 3][:, :]
                if slope is not None:
                    src = prb[:, n % 3, 0:3 * P]
                    mark(STT(src, fl(dist[:, :, :]), -slope / SCALE, bank[n % 3][:, 0:3 * P], ALU.mult, ALU.add))
                    settle()
                for t in range(TT):
                    mark(nc.vector.tensor_reduce(sml[:, n % 4, t:t + 1], src[:, query_cols(heads[n], t)], AX.X, ALU.max))
                settle()
                TS(sml[:, n % 4, 0:TT], sml[:, n % 4, 0:TT], -SCALE, None, ALU.mult).then_inc(sem("attn_max"), 1)

            def rows(n):
                p, e = n // 2, n % 2
                dve.wait_ge(*attn_count(name, "exp", n + 1))
                mark(nc.vector.reciprocal(sml[:, n % 4, 4:4 + TT], sml[:, n % 4, 2:2 + TT]))
                settle()
                dve.wait_ge(*attn_count(name, "values", n + 1))
                if p >= 2:
                    dve.wait_ge(*attn_count(name, "rows_t", p - 1))
                TTo(orow[:, p % 2, :, HD * e:HD * e + HD],
                    bank[5 + e][:, 0:P].rearrange("p (t c) -> p t c", t=TT),
                    sml[:, n % 4, 4:4 + TT].unsqueeze(2).broadcast_to([P, TT, HD]), ALU.mult).then_inc(sem("attn_rows"), 1)

            def pair(p):
                low_mix(int(name[2]), OUT_TILE[name] + p, bank[7][:, 0:S])

            maxima(0)
            for n in range(len(heads)):
                if n + 1 < len(heads):
                    maxima(n + 1)
                if n >= 2:
                    rows(n - 2)
                if n >= 5 and n % 2:
                    pair(n // 2 - 2)
            rows(len(heads) - 2)
            rows(len(heads) - 1)
            pair(len(heads) // 2 - 2)
            pair(len(heads) // 2 - 1)

        def low_mix(l, k, src):
            dve.wait_ge(sem(f"mixhi{l}"), k + 1)
            TTo(hlo[:, k, :], src, hhi[:, k, :].bitcast(F32), ALU.subtract).then_inc(sem(f"mixed{l}"), 1)

        def split_w_out(l):
            for c in range(3):
                split2(n_wout[l] + c)

        def w_out(l, following):
            split2(n_wout[l] + 3)
            if following is not None:
                split_units(following, 0)

            def update(c):
                slot_done(dve, n_wout[l] + c)
                x = fl(xT[:, 2 * c:2 * c + 2, :])
                TTo(x, bank[c][:, :], x, ALU.add).then_inc(sem("x_ready"), 1)
            new_x(following, update)

        dve.wait_ge(sem("all_consts"), 1)
        norm_mix()

        def shift(i):
            dve.wait_ge(sem("shift_a"), i + 1)
            for half in range(2):
                c = W_IN_ORDER[i] * 2 + half
                u = U_TILES[i][half]
                m = STT(u[:, 1:S], bank[i % 4][:, S * half:S * half + S - 1], col(C_MU + c), u[:, 1:S], ALU.mult, ALU.add)
            m.then_inc(sem("win_free"), 1)
            if i + 3 < 11:
                split2(n_win + i + 3)

        split2(n_mem + 3)
        for c in range(3):
            split2(n_win + c)
        for l in range(2):
            slot_done(dve, n_mem + 2 * l)
            nc.vector.tensor_copy(fl(kmT[:, l, :, :]), bank[(4, 3)[l]][:, :]).then_inc(sem("mem_k_out"), 1)
        dve.wait_ge(sem("mem_k_out"), 2)

        def key_norm(l):
            head_norm(f"kn{l}", 2, 6, [7], sq[:, 2 * l:2 * l + 2, :], kmT[:, l, :, :], kmT[:, l, :, :], lambda p: col(C_MK + l))

        key_norm(0)
        shift(0)
        mark(nc.vector.memset(pw[:, :, 0:1], 0.0))
        key_norm(1)
        for i in range(1, 4):
            shift(i)
        for p in range(NP_):
            dve.wait_ge(sem("lw_ready"), p + 1)
            for j in (2 * p, 2 * p + 1):
                mark(nc.vector.tensor_tensor_scan(pw[:, j, 1:P + 1], ones[:, :], pw[:, j, 1:P + 1], 0.0, ALU.mult, ALU.add))
        settle()
        mark(nc.vector.tensor_copy(c12[:, :, :], pw[:, :, HD:HD + 1]))
        settle()
        TTo(pw[:, :, :], pw[:, :, :], c12[:, :, :].broadcast_to([P, 2 * NP_, P + 1]), ALU.subtract).then_inc(sem("cum_ready"), 1)
        shift(4)
        shift(5)
        head_norm("kkn", NP_, 6, [7, 6], sq[:, 0:NP_, :], uk, kk, lambda p: col(C_KK + p), mode="l2")
        shift(6)
        dve.wait_ge(sem("a_ready"), NP_)
        tmp = KR[:, :, :, :].rearrange("p a b c -> p (a b c)")[:, 0:NP_ * S].rearrange("p (a s) -> p a s", a=NP_)
        for p in range(NP_):
            mark(TS(tmp[:, p, :], ua[:, p, :], col(C_KA + p), omu[:, 20 + p:21 + p], ALU.mult, ALU.add))
        settle()
        mark(TTo(fl(uk[:, :, :]), fl(uk[:, :, :]), fl(tmp), ALU.mult))
        mark(TTo(fl(ua[:, :, :]), fl(kk[:, :, :]), fl(ua[:, :, :]), ALU.mult))
        settle()
        shift(7)
        dve.wait_ge(*head_count("kkn", "done", NP_))
        for p in range(NP_):
            STT(sq[:, p, :], ur[:, p, :], col(C_RK + p), uk[:, p, :], ALU.mult, ALU.mult).then_inc(sem("head_sq"), 1)
        shift(8)
        shift(9)
        dve.wait_ge(sem("powers"), 2)
        dve.wait_ge(sem("mid_power"), 1)
        dve.wait_ge(*head_count("bn", "sq", NP_))

        def per_chunk(t):
            return t[:, :, :].rearrange("p a (c t) -> p (a c) t", c=2)

        TTo(KR[:, :, 0, :], per_chunk(kk), pr[:, :, 0:P], ALU.mult).then_inc(sem("powers_used"), 1)
        TTo(KR[:, :, 1, :], per_chunk(ur), pr[:, :, 1:P + 1], ALU.mult).then_inc(sem("powers_used"), 1)
        TTo(sfin[:, 0, :], sfin[:, 1, :], pr[:, 0::2, P], ALU.mult).then_inc(sem("powers_used"), 1)
        mark(TTo(per_chunk(ua), per_chunk(ua), pw[:, :, 1:P + 1], ALU.mult))
        TTo(per_chunk(uk), per_chunk(uk), pw[:, :, 1:P + 1], ALU.mult).then_inc(sem("powers_used"), 1)
        dve.wait_ge(sem("tp_t"), 4)
        head_norm("bn", NP_, 6, [7, 6], sq[:, 0:NP_, :], uv, uv, None, mode="sum")
        dve.wait_ge(sem("lt_unit"), 1)

        def strict(n):
            return tri[:, 1:2, :].broadcast_to([P, n, P]).bitcast(I32)

        def lt(g):
            dve.wait_ge(sem("lt_ps"), g + 1)
            nc.vector.copy_predicated(LT[:, 4 * g:4 * g + 4, :], tri4[:, :, :].bitcast(I32),
                                      bank[g % 2][:, :].rearrange("p (a t) -> p a t", a=4)).then_inc(sem("lt_done"), 1)

        def z1(g):
            dve.wait_ge(sem("lt_done"), g + 1)
            TTo(Zi[:, 4 * g:4 * g + 4, :], LT[:, 4 * g:4 * g + 4, :], z1mask[:, :].unsqueeze(1).broadcast_to([P, 4, P]), ALU.mult)\
                .then_inc(sem("z_done"), 1)

        lt(0)
        for g in range(NG):
            if g + 1 < NG:
                lt(g + 1)
            z1(g)

        def level(lv):
            q = bass.ds(lv + 1, 1)
            for g in range(NG):
                dve.wait_ge(sem("inv_a"), NG * lv + g + 1)
                TTo(Ri[:, 4 * g:4 * g + 4, :], bank[g % 2][:, :].rearrange("p (a t) -> p a t", a=4),
                    invmask[:, q, :].broadcast_to([P, 4, P]), ALU.mult).then_inc(sem("r_done"), 1)

        with dve.Fori(0, 5) as lv:
            level(lv)
        level(5)
        dve.wait_ge(sem("mq_zero"), 1)
        for n in range(2 * NH):
            par, ch, p = TRIANGLES[n]
            i = inst(par, ch, p)
            dve.wait_ge(sem("nmq_ps"), n + 1)
            nc.vector.copy_predicated(LT[:, i, :], tri[:, 0, :].bitcast(I32), bank[6 + n % 2][:, 0:P])
            nc.vector.copy_predicated(MQ[:, i, :], fl(tri[:, 1:3, :]).bitcast(I32), bank[6 + n % 2][:, P:3 * P])\
                .then_inc(sem("nmq_done"), 1)
        dve.wait_ge(sem("s_ps"), 1)
        TTo(sT[:, :, :], bank[0][:, 0:384].rearrange("p (a v) -> p a v", a=NP_),
            sfin[:, 0, :].unsqueeze(2).broadcast_to([P, NP_, HD]), ALU.mult).then_inc(sem("state"), 1)
        split_w_out(0)
        for q in range(3):
            dve.wait_ge(sem("centred"), q + 1)
            nc.vector.tensor_copy(fl(dT[:, 2 * q:2 * q + 2, :]), bank[q][:, :]).then_inc(sem("d_out"), 1)
        dve.wait_ge(sem("d_out"), 3)
        head_norm("gn", NP_, 6, [7, 6], sq[:, 0:NP_, :], dT, dT, lambda p: col(C_LNW + p), eps=GN_EPS)
        dve.wait_ge(*head_count("gn", "done", NP_))
        for p in range(NP_):
            mark(STT(dT[:, p, :], dT[:, p, :], col(C_LNB + p), uv[:, p, :], ALU.add, ALU.add))
        settle()
        for p in range(NP_):
            TTo(dT[:, p, :], dT[:, p, :], gT[:, p, :], ALU.mult).then_inc(sem("mix_f"), 1)
        dve.wait_ge(sem("mq_out"), 1)
        head_norm("mq0", 2, 6, [7], sq[:, 0:2, :], mq, mq, lambda p: col(C_MQ))
        for p in range(NP_):
            low_mix(0, p, dT[:, p, :])
        attend("at0")
        w_out(0, "ffn1")
        ffn(1, "kv")
        for c in range(3):
            slot_done(dve, n_kv + c)
            by_rb(fl(kT[:, 2 * c:2 * c + 2, :]), bank[c][:, :]).then_inc(sem("k_out"), 1)
            if c == 0:
                dve.wait_ge(sem("rb_t"), 1)
                nc.vector.tensor_copy(rcol[:, :], bank[7][:, 0:S:P]).then_inc(sem("rcol_ready"), 1)
            split2(n_kv + c + 3)
        dve.wait_ge(sem("k_out"), 3)
        head_norm("kvn", NP_, 6, [7, 6], sq[:, 0:NP_, :], kT, kT, lambda p: col(C_KVK))
        for k in range(KT):
            h_low("ffn2", k)
        split_units("ffn2", 0)
        split_units("ffn2", 1)
        ffn(2, "mix1")
        for c in range(4):
            slot_done(dve, n_bin + c)
            by_rb(fl(qT[:, 2 * c:2 * c + 2, :]), bank[c][:, :]).then_inc(sem("q_out"), 1)
            if c == 0:
                split2(n_bin + 3)
        dve.wait_ge(sem("q_out"), 4)
        head_norm("bq", NP_, 6, [7, 6], sq[:, 0:NP_, :], qT, qT, lambda p: col(C_BQ))
        head_norm("mq1", 2, 6, [7], sq[:, NP_:NP_ + 2, :], qT[:, NP_:NP_ + 2, :], qT[:, NP_:NP_ + 2, :],
                  lambda p: col(C_MQ + 1))
        split_w_out(1)
        attend("at1")
        w_out(1, "ffn3")
        ffn(3, None)
        for t in range(TT):
            for half in range(2):
                dve.wait_ge(sem("out_t"), 2 * t + half + 1)
                nc.vector.tensor_copy(xrow[:, t, 512 * half:512 * half + 512], bank[4 + 2 * t + half][:, :])\
                    .then_inc(sem("out_rows_ready"), 1)

    ctx.close()


_INS = ["x", "mem", "ffn1_norm", "ffn1_w1", "ffn1_w3", "ffn1_w2", "mix_norm", "w_out", "mem_norm", "w_mem_kv",
        "mem_q_norm", "mem_k_norm", "ffn2_norm", "ffn2_w1", "ffn2_w3", "ffn2_w2", "rwkv_w_in", "rwkv_mu", "rwkv_w0",
        "rwkv_w2", "rwkv_a0", "rwkv_a2", "rwkv_g2", "rwkv_k_k", "rwkv_k_a", "rwkv_r_k", "rwkv_ln_w", "rwkv_ln_b",
        "kv_norm", "w_kv", "kv_k_norm", "moba_w_in", "moba_q_norm"]


def kernel(**inputs):
    import numpy as np
    import concourse.bacc as bacc
    from concourse.bass_utils import run_bass_kernel_spmd

    nc = bacc.Bacc("TRN2", target_bir_lowering=False, num_devices=1)
    arrays, T = {}, {}
    for name in _INS:
        arrays[name] = np.ascontiguousarray(inputs[name])
        T[name] = nc.dram_tensor(name, arrays[name].shape, F32, kind="ExternalInput").ap()
    out = nc.dram_tensor("out", (1, S, D), F32, kind="ExternalOutput").ap()
    build(nc, T, out)
    return run_bass_kernel_spmd(nc, [arrays], core_ids=[0]).results[0]["out"]
```

```python
from contextlib import ExitStack

import concourse.bass as bass
from concourse import mybir

F32 = mybir.dt.float32
F32R = mybir.dt.float32r
BF16 = mybir.dt.bfloat16
I32 = mybir.dt.int32
ALU = mybir.AluOpType
ACT = mybir.ActivationFunctionType
AX = mybir.AxisListType

P = 128
D = 1024
S = 256
DFF = 2752
KT = D // P
TT = S // P
HD = 64
NH = 12
MIX = NH * HD
MEMW = 4 * HD
NP_ = NH // 2
SHIFTW = 3 * MIX + 256
FULL = DFF // 256
TAIL = DFF - 256 * FULL
NJ = -(-DFF // P)
LASTROWS = DFF - P * (NJ - 1)
RING = 3
EPS = 1e-6
GN_EPS = 64e-5
DECAY = float.fromhex("0x1.368b2fc6f9609p-1")
SCALE = HD ** -0.5
FAR = 1e30


def build(nc, T, out):
    ctx = ExitStack()
    sems = {}

    def sem(name):
        if name not in sems:
            sems[name] = ctx.enter_context(nc.semaphore(name))
        return sems[name]

    base = [-(-nc.sbuf_base // 64) * 64]

    def place(name, shape, dt, at=None):
        size = (2 if dt == BF16 else 4)
        for n in shape[1:]:
            size *= n
        size = -(-size // 64) * 64
        off = base[0] if at is None else at
        if at is None:
            base[0] += size
        assert off + size <= 229368, (name, off, size)
        return nc.alloc_sbuf_tensor_at(name, shape, dt, offset=off), off + size

    def sb(name, shape, dt=F32):
        return place(name, shape, dt)[0]

    raw = sb("raw", [P, RING, 2048])
    rings_at = base[0]
    whi = sb("whi", [P, 2 * RING, 1024], F32R)
    wlo = sb("wlo", [P, 2 * RING, 1024], F32R)
    rings_end = base[0]
    xT = sb("xT", [P, KT, S])
    h_at = base[0]
    hhi = sb("hhi", [P, KT, S], F32R)
    hlo = sb("hlo", [P, KT, S], F32R)
    sq = sb("sq", [P, KT, S])
    sq_end = base[0]
    kmT = sb("kmT", [P, 2, 2, S])
    vm = sb("vm", [P, 2, 2, MEMW])
    ident = sb("ident", [P, P])
    ones = sb("ones", [P, P])
    rb = sb("rb", [P, S])
    rcol = sb("rcol", [P, TT])
    head_sel = sb("head_sel", [P, 2])
    eps_col = sb("eps_col", [P, 2])
    centre = sb("centre", [P, P])
    invmask = sb("invmask", [P, 7, P])
    z1mask = sb("z1mask", [P, P])
    upper4 = sb("upper4", [P, 4, P])
    tri_mq = sb("tri_mq", [P, 4, P])
    tri4 = sb("tri4", [P, 4, P])
    dist = sb("dist", [P, 3, P])
    prm = sb("prm", [P, 144])
    omu = sb("omu", [P, 32])
    stat = sb("stat", [P, 11, 24])
    zw = sb("zw", [P, P], BF16)
    zm = sb("zm", [P, 512], BF16)
    region = base[0]

    bank = [ctx.enter_context(nc.psum_tensor(f"bank{i}", [P, 512], F32)) for i in range(8)]

    ksq, at = place("ksq", [P, NP_, S], F32, region)
    at = region
    pre, at = place("pre", [P, 2, 2 * S], F32, at)
    sg, at = place("sg", [P, 2, S], F32, at)
    g32, at = place("g32", [P, 2, S], F32, at)
    ghi, at = place("ghi", [P, 2, S], F32R, at)
    glo, at = place("glo", [P, 2, S], F32R, at)
    ffn_end = at
    kT, at = place("kT", [P, NP_, S], F32, at)
    vt2, at = place("vt2", [P, TT, MIX], F32, at)
    attn_at = at
    h2hi, at = place("h2hi", [P, KT, S], F32R, at)
    h2lo, h2_end = place("h2lo", [P, KT, S], F32R, at)
    assert h2_end <= 229368
    at = ffn_end
    xrow, at = place("xrow", [P, TT, D], F32, at)
    mrow, at = place("mrow", [P, TT, D], F32, at)
    prow, at = place("prow", [P, 2, P], F32, at)
    mT, at = place("mT", [P, KT, S], F32, at)
    mem_h_at = {}
    for l in range(2):
        for what in ("hi", "lo"):
            mem_h_at[l, what], at = place(f"m{l}{what}", [P, KT, S], F32R, at)
    start_end = at
    at = region
    uk, at = place("uk", [P, NP_, S], F32, at)
    uv, at = place("uv", [P, NP_, S], F32, at)
    ua, at = place("ua", [P, NP_, S], F32, at)
    gT, at = place("gT", [P, NP_, S], F32, at)
    KR, at = place("KR", [P, 2 * NP_, 2, P], F32, at)
    vt, at = place("vt", [P, TT, MIX], F32, at)
    mq, at = place("mq", [P, 2, S], F32, at)
    wa, at = place("wa", [P, S], F32, at)
    gd, at = place("gd", [P, S], F32, at)
    la_at = at
    la, at = place("la", [P, MIX], F32, at)
    lg, at = place("lg", [P, MIX], F32, at)
    c12, at = place("c12", [P, 2 * NP_, 1], F32, at)
    sfin, at = place("sfin", [P, 2, NP_], F32, at)
    sT, at = place("sT", [P, NP_, HD], F32, at)
    pw_at = at
    pw, at = place("pw", [P, 2 * NP_, P + 1], F32, at)
    pr_at = at
    pr, at = place("pr", [P, 2 * NP_, P + 1], F32, at)
    kk_at = at
    kk, at = place("kk", [P, NP_, S], F32, at)
    ur_at = at
    ur, at = place("ur", [P, NP_, S], F32, at)
    rwkv_end = at
    bt, _e = place("bt", [P, MIX], F32, pr_at)
    ktp, _e = place("ktp", [P, MIX], F32, _e)
    assert _e <= kk_at
    rhsb, _e = place("rhsb", [P, NH, HD], F32, kk_at)
    uneg, _e = place("uneg", [P, NH, HD], F32, _e)
    assert _e <= ur_at
    yT, _e = place("yT", [P, NP_, S], F32, ur_at)
    dT, _e = place("dT", [P, NP_, S], F32, la_at)
    LT, _e = place("LT", [P, 2 * NH, P], F32, rings_at)
    Zi, _e = place("Zi", [P, 2 * NH, P], F32, _e)
    Xi, _e = place("Xi", [P, 2 * NH, P], F32, _e)
    Ri, _e = place("Ri", [P, 2 * NH, P], F32, _e)
    assert _e <= rings_end
    MQ, _e = place("MQ", [P, 2 * NH, 2 * P], F32, h_at)
    assert _e <= sq_end
    at = attn_at
    qT, at = place("qT", [P, 4 * 2, S], F32, at)
    attn_end = at
    prb, _e = place("prb", [P, 3, 4 * P], F32, pw_at)
    prT, _e = place("prT", [P, 2, 4 * P], F32, _e)
    sml, _e = place("sml", [P, 4, 8], F32, _e)
    assert attn_end <= pw_at and _e <= ur_at, (attn_end, pw_at, _e)
    assert max(start_end, attn_at, rwkv_end) <= 229368, (start_end, attn_at, rwkv_end)

    rowsA, rowsB = 72, 68
    G_FFN1, G_MIX, G_MEM, G_FFN2, G_KV = 0, 16, 32, 48, 64
    C_MU = rowsA
    C_W0, C_A0, C_KK, C_KA, C_RK, C_LNW, C_LNB = (rowsA + 20 + 6 * i for i in range(7))
    C_MQ, C_MK, C_KVK, C_BQ = rowsA + 62, rowsA + 64, rowsA + 66, rowsA + 67

    def col(c):
        return prm[:, c:c + 1]

    def fl(ap):
        return ap.rearrange("p a b -> p (a b)")

    def cols_of(w, c):
        return w.rearrange("(k p) c -> p k c", p=P)[:, :, 256 * c:256 * c + 256]

    W_IN_ORDER = [9, 3, 4, 5, 0, 1, 2, 6, 7, 8, 10]

    n_slot = [0]

    def take(n):
        n_slot[0] += n
        return n_slot[0] - n

    n_ffn = {}
    n_ffn[0] = take(3 * (FULL + 1))
    n_mem = take(4)
    n_win = take(11)
    n_wout = {0: take(4)}
    n_ffn[1] = take(3 * (FULL + 1))
    n_kv = take(6)
    n_ffn[2] = take(3 * (FULL + 1))
    n_bin = take(4)
    n_wout[1] = take(4)
    n_ffn[3] = take(3 * (FULL + 1))

    static = {}
    for l in range(2):
        for c in range(2):
            static[n_mem + 2 * l + c] = cols_of(T["w_mem_kv"][l], c)
        for c in range(4):
            static[n_wout[l] + c] = cols_of(T["w_out"][l], c)
    for i, c in enumerate(W_IN_ORDER):
        static[n_win + i] = cols_of(T["rwkv_w_in"][0], c)
    for c in range(6):
        static[n_kv + c] = cols_of(T["w_kv"], c)
    for c in range(4):
        static[n_bin + c] = cols_of(T["moba_w_in"][0], c)

    ffn_w = [(T[f"ffn{1 + i % 2}_w1"][i // 2], T[f"ffn{1 + i % 2}_w3"][i // 2], T[f"ffn{1 + i % 2}_w2"][i // 2])
             for i in range(4)]
    raw_ready = [sem(f"raw_ready{c}") for c in range(RING)]
    tail_ready = sem("tail_ready")
    hi_ready = [sem(f"hi_ready{u}") for u in range(2 * RING)]
    lo_ready = [sem(f"lo_ready{u}") for u in range(2 * RING)]
    unit_used = [sem(f"unit_used{u}") for u in range(2 * RING)]

    def raw8(n):
        return raw[:, n % RING, :].rearrange("p (k c) -> p k c", k=KT)

    def unit_src(n, half, rows):
        if rows:
            return raw[:, n % RING, 1024 * half:1024 * half + 1024]
        return raw8(n)[:, :, P * half:P * half + P]

    def unit_dst(ring, n, half, rows):
        u = ring[:, 2 * (n % RING) + half, :]
        return u if rows else u.rearrange("p (k c) -> p k c", k=KT)

    N_ROW_LOADS = 20
    UPD_LAST = 28
    NORM_WAITS = {"ffn0": []}
    NORM_WAITS.update({n: [] for n in ("mix0", "ffn1", "kv", "mix1", "ffn3")})
    H = {n: (h2hi, h2lo) if n in ("ffn1", "ffn2", "ffn3") else (hhi, hlo)
         for n in ("ffn0", "mix0", "ffn1", "kv", "ffn2", "mix1", "ffn3")}
    PEEL = 4
    FFN_UNITS = ([(0, 0), (1, 0)], [(0, 1), (1, 1), (2, 0)])
    SLOT_UNITS = ([(0, 0), (0, 1)], [(1, 0), (1, 1), (2, 0), (2, 1)])
    PHASE = {"ffn0": (n_ffn[0], FFN_UNITS), "mix0": (n_mem, SLOT_UNITS), "ffn1": (n_ffn[1], FFN_UNITS), "kv": (n_kv, SLOT_UNITS),
             "ffn2": (n_ffn[2], ([(0, 0), (0, 1), (1, 0), (1, 1)], [(2, 0)])), "mix1": (n_bin, SLOT_UNITS), "ffn3": (n_ffn[3], FFN_UNITS)}

    def inst(par, ch, p):
        return NH * par + NP_ * ch + p

    INSTANCES = [(par, ch, p) for par in range(2) for ch in range(2) for p in range(NP_)]
    NG = 2 * NH // 4
    def part(par):
        return slice(HD * par, HD * par + HD)

    def tokens(ch):
        return slice(P * ch, P * ch + P)

    def mem_heads(l, q):
        return [(q[part(e), p, :], kmT[part(e), l, p, :], lambda kt, h=2 * p + e: vm[:, l, kt, HD * h:HD * h + HD], None)
                for p in range(2) for e in range(2)]

    HEADS = {
        "at0": mem_heads(0, mq),
        "at1": [(qT[part(e), p, :], kT[part(e), p, :], lambda kt, h=2 * p + e: vt2[:, kt, HD * h:HD * h + HD],
                 2.0 ** (-8.0 * (2 * p + e + 1) / NH)) for p in range(NP_) for e in range(2)]
        + mem_heads(1, qT[:, NP_:NP_ + 2, :]),
    }
    OUT_TILE = {"at0": NP_, "at1": 0}

    def blocks(head):
        return [(t, kt) for t in range(TT) for kt in range(TT) if head[3] is None or kt <= t]

    def turned_at(head, i):
        order = sorted(blocks(head), key=lambda b: (b[1], b[0]))
        return P * order.index(blocks(head)[i])

    def query_cols(head, t):
        mine = [i for i, (bt_, _) in enumerate(blocks(head)) if bt_ == t]
        return slice(P * mine[0], P * mine[-1] + P)

    U_TILES = []
    for c in W_IN_ORDER:
        U_TILES.append((wa[:, :], gd[:, :]) if c == 9 else
                       None if c == 10 else
                       tuple((ur, uk, uv)[c // 3][:, 2 * (c % 3) + half, :] for half in range(2)))

    HEAD_PAIRS = {"kn0": 1, "kn1": 1, "kkn": 3, "bn": 3, "mq0": 1, "gn": 3, "kvn": 3, "bq": 3, "mq1": 1}
    HEAD_BANKS = {"kn0": [6], "kn1": [7], "kkn": [6, 7, 4], "bn": [6, 7, 3], "mq0": [4], "gn": [6, 7, 3], "kvn": [7, 5, 4],
                  "bq": [6, 7, 5], "mq1": [4]}
    HEAD_SRC = {"kn0": sq[:, 0:2, :], "kn1": sq[:, 2:4, :], "kkn": sq, "bn": sq, "mq0": sq[:, NP_:NP_ + 2, :], "gn": sq,
                "kvn": ksq, "bq": sq, "mq1": sq[:, NP_:NP_ + 2, :]}
    START, total = {}, {}
    for name, pairs in HEAD_PAIRS.items():
        for what in ("sq", "sum", "var", "std", "rec", "wide", "rb", "done"):
            START[name, what] = total.get(what, 0)
            if not (what == "var" and name != "kkn" or what == "std" and name == "bn"):
                total[what] = total.get(what, 0) + pairs

    def head_count(name, what, n):
        return sem(f"head_{what}"), START[name, what] + n

    def head_pair(name, q):
        return HEAD_SRC[name][:, 2 * q:2 * q + 2, :]

    def head_stat(name, q):
        return stat[:, list(HEAD_PAIRS).index(name), 8 * q:8 * q + 8]

    def attn_count(name, what, n):
        heads0 = len(HEADS["at0"])
        return sem(f"attn_{what}"), n + (0 if name == "at0" else heads0)

    def mixed(name, p):
        return sem(f"mixed{name[2]}"), OUT_TILE[name] + p + 1

    block = ctx.enter_context(nc.Block())

    upd = {"load": 4, "ffn0": 8, "mix0": 12, "ffn1": 16, "ffn2": 20, "mix1": 24, "ffn3": 28}
    norm_no = {"ffn0": 0, "mix0": 1, "ffn1": 2, "kv": 3, "ffn2": 4, "mix1": 5, "ffn3": 6}
    stat_no = {"ffn0": 0, "mix0": 1, "ffn1": 2, "kv": 3, "mix1": 4, "ffn3": 5}
    norm_after = {"ffn0": "load", "mix0": "ffn0", "ffn1": "mix0", "kv": "ffn1", "mix1": "ffn2", "ffn3": "mix1"}
    norm_gain = {"ffn0": G_FFN1, "mix0": G_MIX, "ffn1": G_FFN2, "kv": G_KV, "ffn2": G_FFN1 + 8,
                 "mix1": G_MIX + 8, "ffn3": G_FFN2 + 8}

    def slot_done(eng, n):
        eng.wait_ge(unit_used[2 * (n % RING) + 1], n // RING + 1)

    @block.sync
    def _(sp):
        x2 = T["x"][0].rearrange("(t p) d -> p t d", p=P)
        m2 = T["mem"][0].rearrange("(t p) d -> p t d", p=P)
        sp.dma_start(xrow[:, :, :], x2).then_inc(sem("x_loaded"), 16)
        sp.dma_start(prow[0:16, 0, :], T["ffn1_norm"].rearrange("l (r c) -> (l r) c", c=P)).then_inc(sem("first_rows"), 16)
        for c in range(2):
            sp.dma_start(raw8(c), cols_of(ffn_w[0][c], 0)).then_inc(raw_ready[c], 16)
        sp.dma_start(raw[:, 2, :].rearrange("p (j d) -> p j d", j=2), ffn_w[0][2][0:256, :].rearrange("(j p) d -> p j d", p=P))\
            .then_inc(raw_ready[2], 16)
        sp.dma_start(mrow[:, :, :], m2).then_inc(sem("mem_loaded"), 16)
        r = 16
        for name, rows in (("mix_norm", 16), ("mem_norm", 16), ("ffn2_norm", 16), ("kv_norm", 8)):
            src = T[name].rearrange("l (r c) -> (l r) c", c=P) if name != "kv_norm" else T[name].rearrange("(r c) -> r c", c=P)
            sp.dma_start(prow[r:r + rows, 0, :], src).then_inc(sem("rows_loaded"), 16)
            r += rows
        r = 0
        for name in ("rwkv_mu", "rwkv_w0", "rwkv_a0", "rwkv_k_k", "rwkv_k_a"):
            src = T[name][0].rearrange("(r c) -> r c", c=P)
            sp.dma_start(prow[r:r + src.shape[0], 1, :], src).then_inc(sem("rows_loaded"), 16)
            r += src.shape[0]
        sp.dma_start(prow[r:r + 6, 1, :], T["rwkv_r_k"][0].rearrange("(r e) c -> r (e c)", e=2)).then_inc(sem("rows_loaded"), 16)
        r += 6
        for name in ("rwkv_ln_w", "rwkv_ln_b"):
            sp.dma_start(prow[r:r + 6, 1, :], T[name][0].rearrange("(r c) -> r c", c=P)).then_inc(sem("rows_loaded"), 16)
            r += 6
        for name in ("mem_q_norm", "mem_k_norm"):
            for e in range(2):
                sp.dma_start(prow[r:r + 2, 1, HD * e:HD * e + HD], T[name]).then_inc(sem("rows_loaded"), 16)
            r += 2
        for e in range(2):
            sp.dma_start(prow[r:r + 1, 1, HD * e:HD * e + HD], T["kv_k_norm"].rearrange("(a c) -> a c", a=1)).then_inc(sem("rows_loaded"), 16)
            sp.dma_start(prow[r + 1:r + 2, 1, HD * e:HD * e + HD], T["moba_q_norm"]).then_inc(sem("rows_loaded"), 16)

        def load_slot(n, src, dst=None):
            if n >= RING:
                sp.wait_ge(lo_ready[2 * (n % RING) + 1], n // RING)
            sp.dma_start(raw8(n) if dst is None else dst, src).then_inc(raw_ready[n % RING], 16)

        def load_ffn(f):
            w1, w3, w2 = ffn_w[f]
            n0 = n_ffn[f]
            w1v = w1.rearrange("(k p) c -> p k c", p=P)
            w3v = w3.rearrange("(k p) c -> p k c", p=P)
            rows2 = [raw[:, (n0 + 2) % RING, :].rearrange("p (j d) -> p j d", j=2)]
            with sp.Fori(1 if f == 0 else 0, FULL) as t:
                for c, wv in ((0, w1v), (1, w3v)):
                    n = n0 + c
                    sp.wait_ge(lo_ready[2 * (n % RING) + 1], t + n // RING)
                    sp.dma_start(raw8(n), wv[:, :, bass.ds(t * 256, 256)]).then_inc(raw_ready[n % RING], 16)
                n = n0 + 2
                sp.wait_ge(lo_ready[2 * (n % RING) + 1], t + n // RING)
                sp.dma_start(rows2[0], w2[bass.ds(t * 256, 256), :].rearrange("(j p) d -> p j d", p=P))\
                    .then_inc(raw_ready[n % RING], 16)
            n = n0 + 3 * FULL
            load_slot(n, w1v[:, :, 256 * FULL:DFF], raw8(n)[:, :, 0:TAIL])
            load_slot(n + 1, w3v[:, :, 256 * FULL:DFF], raw8(n + 1)[:, :, 0:TAIL])
            load_slot(n + 2, w2[256 * FULL:256 * FULL + P, :], raw[:, (n + 2) % RING, 0:1024])
            sp.dma_start(raw[0:LASTROWS, (n + 2) % RING, 1024:2048], w2[DFF - LASTROWS:DFF, :]).then_inc(tail_ready, 16)

        load_ffn(0)
        for n in range(n_mem, n_mem + 4):
            load_slot(n, static[n])
        for n in range(n_win, n_win + 11):
            load_slot(n, static[n])
            if n == n_win + 3:
                slot_done(sp, n_mem + 3)
                sp.dma_start(la[0:HD, :], T["rwkv_w2"][0]).then_inc(sem("lora_loaded"), 16)
                sp.dma_start(la[HD:P, :], T["rwkv_a2"][0]).then_inc(sem("lora_loaded"), 16)
                sp.dma_start(lg[:, :], T["rwkv_g2"][0]).then_inc(sem("lora_loaded"), 16)
        for n in range(n_wout[0], n_wout[0] + 4):
            load_slot(n, static[n])
        load_ffn(1)
        for n in range(n_kv, n_kv + 6):
            load_slot(n, static[n])
        load_ffn(2)
        for n in range(n_bin, n_bin + 4):
            load_slot(n, static[n])
        for n in range(n_wout[1], n_wout[1] + 4):
            load_slot(n, static[n])
        load_ffn(3)
        for t in range(TT):
            sp.wait_ge(sem("out_rows_ready"), 2 * t + 2)
            sp.dma_start(out[0, P * t:P * t + P, :], xrow[:, t, :]).then_inc(sem("stored"), 16)
        sp.wait_ge(sem("stored"), 16 * TT)


    def head_wide(pool, name, q):
        pool.wait_ge(*head_count(name, "rec", q + 1))
        nc.gpsimd.tensor_copy(fl(head_pair(name, q)).rearrange("p (n c) -> p n c", c=HD),
                              head_stat(name, q).unsqueeze(2).broadcast_to([P, 8, HD])).then_inc(sem("head_wide"), 1)

    def pool_rwkv(pool):
        for name in ("kn0", "kn1"):
            head_wide(pool, name, 0)
        for q in range(3):
            head_wide(pool, "bn", q)
        slot_done(pool, n_win + 10)
        nc.gpsimd.memset(fl(LT[:, :, :]), 0.0).then_inc(sem("lt_step"), 1)
        pool.wait_ge(sem("lt_step"), 1)
        nc.gpsimd.affine_select(out=LT[:, :, :], in_=LT[:, :, :], compare_op=ALU.not_equal, fill=1.0, base=0,
                                pattern=[[0, 2 * NH], [-1, P]], channel_multiplier=1).then_inc(sem("lt_unit"), 1)
        pool.wait_ge(*head_count("bn", "done", 3))
        nc.gpsimd.memset(MQ[:, :, :], 0.0).then_inc(sem("mq_zero"), 1)

    def pool_attention(pool):
        for name, pairs in (("kvn", 3), ("bq", 2)):
            for q in range(pairs):
                head_wide(pool, name, q)

    @block.gpsimd
    def _(pool):
        made = sem("const_step")
        n = [0]

        def step(ins):
            n[0] += 1
            ins.then_inc(made, 1)

        def done():
            pool.wait_ge(made, n[0])

        def diag(ap, pattern, fill, keep=ALU.not_equal, cbase=0, mult=1):
            step(nc.gpsimd.affine_select(out=ap, in_=ap, compare_op=keep, fill=fill, base=cbase, pattern=pattern,
                                         channel_multiplier=mult))

        step(nc.gpsimd.memset(ident[:, :], 0.0))
        step(nc.gpsimd.memset(ones[:, :], 1.0))
        done()
        diag(ident[:, :], [[-1, P]], 1.0)
        done()
        nc.gpsimd.memset(zw[:, :], 0.0).then_inc(sem("base_consts"), 1)
        nc.gpsimd.memset(zm[:, :], 0.0).then_inc(sem("base_consts"), 1)
        step(nc.gpsimd.memset(centre[:, :], -1.0 / HD))
        step(nc.gpsimd.memset(head_sel[:, :], 1.0))
        step(nc.gpsimd.memset(eps_col[:, 0:1], EPS))
        step(nc.gpsimd.memset(eps_col[:, 1:2], GN_EPS))
        step(nc.gpsimd.memset(invmask[:, :, :], 0.0))
        step(nc.gpsimd.memset(z1mask[:, :], 0.0))
        step(nc.gpsimd.memset(upper4[:, :, :], 1.0))
        step(nc.gpsimd.memset(tri_mq[:, :, :], 1.0))
        step(nc.gpsimd.memset(tri4[:, :, :], 1.0))
        step(nc.gpsimd.iota(dist[:, 0:2, :], pattern=[[P, 2], [-1, P]], base=0, channel_multiplier=1,
                            allow_small_or_imprecise_dtypes=True))
        step(nc.gpsimd.iota(dist[:, 2:3, :], pattern=[[0, 1], [-1, P]], base=0, channel_multiplier=1,
                            allow_small_or_imprecise_dtypes=True))
        done()
        for v in (centre[:, :].rearrange("p (e c) -> p e c", e=2), head_sel[:, :].unsqueeze(2)):
            diag(v, [[-HD, 2], [0, v.shape[2]]], 0.0, ALU.is_ge)
            done()
            step(nc.gpsimd.affine_select(out=v, in_=v, compare_op=ALU.is_ge, fill=0.0, base=HD - 1,
                                         pattern=[[HD, 2], [0, v.shape[2]]], channel_multiplier=-1))
            done()
        diag(centre[:, :], [[-1, P]], 1.0 - 1.0 / HD)
        for q in range(7):
            s = 1 << q
            nb = P // (2 * s)
            left = invmask[:, q, :].rearrange("p (b e c) -> p b e c", e=2, c=s)[:, :, 0, :]
            step(nc.gpsimd.memset(left, -1.0))
            done()
            step(nc.gpsimd.affine_select(out=left, in_=left, compare_op=ALU.is_ge, fill=0.0, base=-s,
                                         pattern=[[-2 * s, nb], [0, s]], channel_multiplier=1))
            done()
            step(nc.gpsimd.affine_select(out=left, in_=left, compare_op=ALU.is_ge, fill=0.0, base=2 * s - 1,
                                         pattern=[[2 * s, nb], [0, s]], channel_multiplier=-1))
            done()
            diag(invmask[:, q, :], [[-1, P]], 1.0)
        odd = z1mask[:, :].rearrange("p (b e) -> p b e", e=2)[:, :, 1]
        step(nc.gpsimd.affine_select(out=odd, in_=odd, compare_op=ALU.not_equal, fill=-1.0, base=0,
                                     pattern=[[-2, P // 2]], channel_multiplier=1))
        done()
        diag(z1mask[:, :], [[-1, P]], 1.0)
        for v, op in ((upper4[:, :, :], ALU.is_ge), (tri_mq[:, 0::2, :], ALU.is_gt), (tri_mq[:, 1::2, :], ALU.is_ge)):
            step(nc.gpsimd.affine_select(out=v, in_=v, compare_op=op, fill=0.0, base=0, pattern=[[0, v.shape[1]], [1, P]],
                                         channel_multiplier=-1))
        step(nc.gpsimd.affine_select(out=tri4[:, :, :], in_=tri4[:, :, :], compare_op=ALU.is_gt, fill=0.0, base=0,
                                     pattern=[[0, 4], [1, P]], channel_multiplier=-1))
        for b in (0, 2):
            step(nc.gpsimd.affine_select(out=dist[:, b, :], in_=dist[:, b, :], compare_op=ALU.is_ge, fill=FAR, base=0,
                                         pattern=[[-1, P]], channel_multiplier=1))
        done()
        nc.gpsimd.memset(rcol[:, :], 0.0).then_inc(sem("all_consts"), 1)
        pool_rwkv(pool)
        pool_attention(pool)


    @block.tensor
    def _(pe):
        def transpose(o, i, n=P):
            return nc.tensor.transpose(o, i, ident[0:n, 0:n])

        def product(o, a_hi, a_lo, b_hi, b_lo, first, last, open_=False):
            nc.tensor.matmul(o, a_hi, b_hi, start=first, stop=False, skip_group_check=open_)
            nc.tensor.matmul(o, a_hi, b_lo, start=False, stop=False, skip_group_check=open_)
            return nc.tensor.matmul(o, a_lo, b_hi, start=False, stop=last, skip_group_check=open_)

        def fp_unit(o, u, width=P, h=(hhi, hlo)):
            for k in range(KT):
                m = product(o, whi[:, u, P * k:P * k + width], wlo[:, u, P * k:P * k + width],
                            h[0][:, k, :], h[1][:, k, :], k == 0, k == KT - 1)
            return m

        def fp_slot(n, b, h=(hhi, hlo)):
            for half in range(2):
                u = 2 * (n % RING) + half
                pe.wait_ge(lo_ready[u], n // RING + 1)
                m = fp_unit(bank[b][:, S * half:S * half + S], u, h=h)
                m.then_inc(unit_used[u], 1)

        def tp_slot(n, b, h=(hhi, hlo)):
            u = 2 * (n % RING)
            pe.wait_ge(lo_ready[u + 1], n // RING + 1)
            for t in range(TT):
                for k in range(KT if t < TT - 1 else KT - 1):
                    product(bank[b][:, 256 * t:256 * t + 256], h[0][:, k, P * t:P * t + P],
                            h[1][:, k, P * t:P * t + P], whi[:, u:u + 2, P * k:P * k + P],
                            wlo[:, u:u + 2, P * k:P * k + P], k == 0, k == KT - 1, t == TT - 1)
            for half in range(2):
                k, c = KT - 1, 256 * (TT - 1) + P * half
                product(bank[b][:, c:c + P], h[0][:, k, P * t:P * t + P], h[1][:, k, P * t:P * t + P],
                        whi[:, u + half, P * k:P * k + P], wlo[:, u + half, P * k:P * k + P], False, True, True)\
                    .then_inc(unit_used[u + half], 1)

        def head_sums(name, q):
            pe.wait_ge(*head_count(name, "sq", q + 1))
            for t in range(TT):
                for e in range(2):
                    m = nc.tensor.matmul(bank[HEAD_BANKS[name][q]][:, 4 * t + 2 * e:4 * t + 2 * e + 2],
                                         head_pair(name, q)[:, e, tokens(t)], head_sel[:, :], start=True, stop=True)
            m.then_inc(sem("head_sum"), 1)

        def head_spread(name, q):
            pe.wait_ge(*head_count(name, "wide", q + 1))
            for e in range(2):
                for t in range(TT):
                    c = S * e + P * t
                    m = transpose(bank[HEAD_BANKS[name][q]][:, c:c + P], fl(head_pair(name, q))[:, S * t + P * e:S * t + P * e + P])
            m.then_inc(sem("head_rb"), 1)

        def square_sums(name, j):
            i = stat_no[name]
            pe.wait_ge(sem("sq_ready"), 4 * i + j + 1)
            for k in (2 * j, 2 * j + 1):
                m = nc.tensor.matmul(bank[6][:, 0:S], ones[:, :], sq[:, k, :], start=(k == 0), stop=(k == KT - 1),
                                     skip_group_check=True)
            if j == 3:
                m.then_inc(sem("norm_stat"), 1)

        def keep_clock(b, n):
            for _ in range(n):
                nc.tensor.matmul(bank[b][:, :], zw[:, :], zm[:, :], start=True, stop=True)

        def first_pair(name, u0, o0, u1, o1, n0, n1):
            pe.wait_ge(lo_ready[u0], n0 // RING + 1)
            pe.wait_ge(lo_ready[u1], n1 // RING + 1)
            for k in range(KT):
                pe.wait_ge(sem("h_ready"), 8 * norm_no[name] + k + 1)
                for o, u in ((o0, u0), (o1, u1)):
                    m = product(o, whi[:, u, P * k:P * k + P], wlo[:, u, P * k:P * k + P], H[name][0][:, k, :], H[name][1][:, k, :],
                                k == 0 and u == u0, k == KT - 1, True)
                    if k == KT - 1:
                        m.then_inc(unit_used[u], 1)
                if name in stat_no and k % 2:
                    square_sums(name, k // 2)

        def first_slot(name, n, b):
            u = 2 * (n % RING)
            first_pair(name, u, bank[b][:, 0:S], u + 1, bank[b][:, S:2 * S], n, n)

        def ffn(f):
            n0, j0 = n_ffn[f], NJ * f
            u1, u3, u2 = (2 * ((n0 + c) % RING) for c in range(3))
            r1, r3, r2 = ((n0 + c) // RING for c in range(3))

            def h(j, half, r, width=P):
                pe.wait_ge(sem("pre_ready"), j0 + j)
                b = bank[4 + half]
                pe.wait_ge(lo_ready[u1 + half], r + r1 + 1)
                fp_unit(b[0:width, 0:S], u1 + half, width, H[f"ffn{f}"]).then_inc(unit_used[u1 + half], 1)
                pe.wait_ge(lo_ready[u3 + half], r + r3 + 1)
                fp_unit(b[0:width, S:2 * S], u3 + half, width, H[f"ffn{f}"]).then_inc(unit_used[u3 + half], 1)

            def o(j, half, r, rows=P, last=False):
                u = u2 + half
                pe.wait_ge(sem("g_ready"), j0 + j + 1)
                pe.wait_ge(lo_ready[u], r + r2 + 1)
                for d in range(KT):
                    m = product(bank[d // 2][:, S * (d % 2):S * (d % 2) + S], whi[0:rows, u, P * d:P * d + P],
                                wlo[0:rows, u, P * d:P * d + P], ghi[0:rows, half, :], glo[0:rows, half, :],
                                False, last, True)
                m.then_inc(unit_used[u], 1)

            first_pair(f"ffn{f}", u1, bank[4][:, 0:S], u3, bank[4][:, S:2 * S], n0, n0 + 1)
            for b in range(4):
                if f == 2 and b == 0:
                    pe.wait_ge(sem("v_out"), 3)
                nc.tensor.matmul(bank[b][:, :], zw[:, :], zm[:, :], start=True, stop=False, skip_group_check=True)
            def double(t, between=None):
                h(2 * t + 1, 1, t)
                o(2 * t, 0, t)
                if between:
                    between(2 * t)
                h(2 * t + 2, 0, t + 1)
                o(2 * t + 1, 1, t)
                if between:
                    between(2 * t + 1)

            first = PEEL if f == 0 else 0
            for t in range(first):
                double(t, mem_step)
            with pe.Fori(first, FULL) as t:
                double(t)
            h(NJ - 1, 1, FULL, LASTROWS)
            o(NJ - 2, 0, FULL)
            o(NJ - 1, 1, FULL, LASTROWS, True)

        def mem_step(n):
            if n == 0:
                pe.wait_ge(sem("rows_loaded"), 16 * N_ROW_LOADS)
                transpose(bank[7][:, 0:rowsA], prow[0:rowsA, 0, :], rowsA)
                transpose(bank[7][:, rowsA:rowsA + rowsB], prow[0:rowsB, 1, :], rowsB).then_inc(sem("prm_t"), 1)
            if n in (2, 3):
                pe.wait_ge(sem("mem_scaled"), 2)
                if n == 2:
                    pe.wait_ge(sem("prm_ready"), 1)
                for j in (2 * (n - 2), 2 * (n - 2) + 1):
                    if j >= 2:
                        pe.wait_ge(sem("mt_out"), j - 1)
                    for k in (2 * j, 2 * j + 1):
                        for t in range(TT):
                            c = S * (k % 2) + P * t
                            m = transpose(bank[6 + j % 2][:, c:c + P], mrow[:, t, P * k:P * k + P])
                    m.then_inc(sem("m_t"), 1)

        pe.wait_ge(sem("base_consts"), 2)
        pe.wait_ge(sem("first_rows"), 16)
        transpose(bank[7][:, 0:16], prow[0:16, 0, :], 16).then_inc(sem("gains_t"), 1)
        pe.wait_ge(sem("x_loaded"), 16)
        for j in range(4):
            for k in (2 * j, 2 * j + 1):
                for t in range(TT):
                    c = S * (k % 2) + P * t
                    m = transpose(bank[j][:, c:c + P], xrow[:, t, P * k:P * k + P])
            m.then_inc(sem("x_t"), 1)
        ffn(0)
        def attend(name):
            heads = HEADS[name]

            def scores(n):
                q, k, _, _ = heads[n]
                if name == "at1" and n == 0:
                    pe.wait_ge(*head_count("bq", "done", 1))
                if n >= 3:
                    pe.wait_ge(*attn_count(name, "exp", n - 2))
                for t in range(TT):
                    c = query_cols(heads[n], t)
                    m = nc.tensor.matmul(bank[n % 3][:, c], q[:, tokens(t)], k[:, 0:c.stop - c.start], start=True, stop=True)
                m.then_inc(sem("attn_scores"), 1)

            def turn(n):
                pe.wait_ge(*attn_count(name, "probs", n + 1))
                if n >= 2:
                    pe.wait_ge(*attn_count(name, "turned", n - 1))
                for i in range(len(blocks(heads[n]))):
                    c = turned_at(heads[n], i)
                    m = transpose(bank[3 + n % 2][:, c:c + P], prb[:, n % 3, P * i:P * i + P])
                m.then_inc(sem("attn_turn"), 1)

            def values(n):
                pe.wait_ge(*attn_count(name, "turned", n + 1))
                if n >= 4 and n % 2 == 0:
                    pe.wait_ge(*mixed(name, n // 2 - 2))
                for kt in range(TT):
                    mine = [(i, t) for i, (t, k) in enumerate(blocks(heads[n])) if k == kt]
                    t0 = mine[0][1]
                    c = turned_at(heads[n], mine[0][0])
                    m = nc.tensor.matmul(bank[5 + n // 2 % 2][part(n % 2), P * t0:S], heads[n][2](kt),
                                         prT[:, n % 2, c:c + S - P * t0], start=(kt == 0), stop=(kt == TT - 1),
                                         skip_group_check=True)
                m.then_inc(sem("attn_values"), 1)

            scores(0)
            scores(1)
            if name == "at1":
                pe.wait_ge(*head_count("mq1", "done", 1))
            for n in range(len(heads)):
                if n + 2 < len(heads):
                    scores(n + 2)
                turn(n)
                if n >= 1:
                    values(n - 1)
            values(len(heads) - 1)

        def w_out(l):
            pe.wait_ge(sem(f"mixed{l}"), KT)
            for c in range(4):
                fp_slot(n_wout[l] + c, c)

        pe.wait_ge(sem("all_consts"), 1)
        def mem_h(l):
            pe.wait_ge(sem("mem_h"), 8 * l + 8)
            return mem_h_at[l, "hi"], mem_h_at[l, "lo"]

        fp_slot(n_mem, 4, mem_h(0))
        for j in range(4):
            square_sums("mix0", j)
        tp_slot(n_mem + 1, 5, mem_h(0))
        fp_slot(n_mem + 2, 3, mem_h(1))
        tp_slot(n_mem + 3, 2, mem_h(1))
        pe.wait_ge(sem("h_ready"), 8 * norm_no["mix0"] + 8)

        def w_in(i):
            if i >= 4:
                pe.wait_ge(sem("win_free"), i - 3)
            fp_slot(n_win + i, i % 4)

        def loras():
            pe.wait_ge(sem("lora_loaded"), 48)
            pe.wait_ge(sem("lora_in"), 2)
            for p in range(NP_):
                if p >= 2:
                    pe.wait_ge(sem("a_ready"), p - 1)
                nc.tensor.matmul(bank[4 + p % 2][:, 0:S], la[0:HD, P * p:P * p + P], wa[0:HD, :], start=True, stop=True)
                nc.tensor.matmul(bank[6 + p % 2][:, 0:S], la[HD:P, P * p:P * p + P], wa[HD:P, :], start=True, stop=True)\
                    .then_inc(sem("lora_wa"), 1)
            pe.wait_ge(sem("a_ready"), NP_)
            for q in range(3):
                if q == 2:
                    pe.wait_ge(sem("g_out"), 1)
                for p in (2 * q, 2 * q + 1):
                    m = nc.tensor.matmul(bank[6 + q % 2][:, S * (p % 2):S * (p % 2) + S], lg[:, P * p:P * p + P], gd[:, :],
                                         start=True, stop=True)
                m.then_inc(sem("lora_g"), 1)

        def to_tokens(j, src, ch, q):
            if j >= 2:
                pe.wait_ge(sem("tp_out"), j - 1)
            for p in range(3):
                m = transpose(bank[4 + j % 2][:, P * p:P * p + P], src[:, 3 * q + p, tokens(ch)])
            m.then_inc(sem("tp_t"), 1)

        w_in(0)
        head_sums("kn0", 0)
        head_sums("kn1", 0)
        w_in(1)
        pe.wait_ge(sem("mem_v_done"), 2)
        head_spread("kn0", 0)
        head_spread("kn1", 0)
        w_in(2)
        pe.wait_ge(*head_count("kn1", "done", 1))
        loras()
        w_in(3)
        w_in(4)
        w_in(5)
        pe.wait_ge(sem("g_out"), 3)
        for q in range(3):
            head_sums("kkn", q)
        w_in(6)
        for q in range(3):
            head_spread("kkn", q)
        for i in range(7, 11):
            w_in(i)
        pe.wait_ge(sem("win_free"), 10)
        pe.wait_ge(sem("a_ready"), NP_)
        pe.wait_ge(*head_count("kkn", "done", 3))
        for q in range(3):
            head_sums("bn", q)
        for j in range(4):
            to_tokens(j, uv, j // 2, j % 2)
        for q in range(3):
            head_spread("bn", q)
        keep_clock(1, 12)
        pe.wait_ge(sem("powers_used"), 4)
        for j in range(4):
            to_tokens(4 + j, (ua, uk)[j // 2], 0, j % 2)

        def triangle(g):
            if g >= 2:
                pe.wait_ge(sem("lt_done"), g - 1)
            for q in range(4):
                par, ch, p = INSTANCES[4 * g + q]
                m = nc.tensor.matmul(bank[g % 2][:, P * q:P * q + P], ua[part(par), p, tokens(ch)],
                                     KR[part(par), 2 * p + ch, 0, :], start=True, stop=True)
            m.then_inc(sem("lt_ps"), 1)

        def first_blocks(g):
            pe.wait_ge(sem("z_done"), g + 1)
            if g == 1:
                pe.wait_ge(*head_count("bn", "done", 3))
            if g >= 2:
                pe.wait_ge(sem("x_done"), g - 1)
            for q in range(4):
                m = transpose(bank[2 + g % 2][:, P * q:P * q + P], Zi[:, 4 * g + q, :])
            m.then_inc(sem("x1_t"), 1)

        triangle(0)
        triangle(1)
        for g in range(NG):
            if g + 2 < NG:
                first_blocks(g)
                triangle(g + 2)
            else:
                first_blocks(g)

        def triangles(g):
            if g == 0:
                pe.wait_ge(*head_count("bn", "done", 3))
                pe.wait_ge(sem("x_done"), NG * 6)
            for b in range(3):
                if g:
                    pe.wait_ge(sem("nmq_done"), 3 * (g - 1) + b + 1)
                mine = INSTANCES[4 * g:4 * g + 4] if b == 0 else INSTANCES[4 * g + 2 * b - 2:4 * g + 2 * b]
                for e, (par, ch, p) in enumerate(mine):
                    kr = KR[part(par), 2 * p + ch, :, :]
                    if b == 0:
                        m = nc.tensor.matmul(bank[6][:, P * e:P * e + P], ua[part(par), p, tokens(ch)], kr[:, 1, :],
                                             start=True, stop=True)
                    else:
                        m = nc.tensor.matmul(bank[(7, 3)[b - 1]][:, 2 * P * e:2 * P * e + 2 * P], uk[part(par), p, tokens(ch)],
                                             kr, start=True, stop=True)
                m.then_inc(sem("nmq_ps"), 1)

        def level(lv, last=False):
            for g in range(NG):
                pe.wait_ge(sem("x_done"), NG * lv + g + 1)
                if g >= 2:
                    pe.wait_ge(sem("r_done"), NG * lv + g - 1)
                for q in range(4):
                    i = 4 * g + q
                    m = nc.tensor.matmul(bank[g % 2][:, P * q:P * q + P], LT[:, i, :], Xi[:, i, :], start=True, stop=True)
                m.then_inc(sem("inv_a"), 1)
                if last:
                    triangles(g)
            pe.wait_ge(sem("z_done"), NG * lv + NG)
            for g in range(NG):
                pe.wait_ge(sem("r_done"), NG * lv + g + 1)
                if not last:
                    if g >= 2:
                        pe.wait_ge(sem("x_done"), NG * lv + NG + g - 1)
                    for q in range(4):
                        i = 4 * g + q
                        m = nc.tensor.matmul(bank[2 + g % 2][:, P * q:P * q + P], Zi[:, i, :], Ri[:, i, :], start=True, stop=True)
                    m.then_inc(sem("inv_b"), 1)
                if g >= 2:
                    pe.wait_ge(sem("z_done"), NG * lv + NG + g - 1)
                for q in range(4):
                    i = 4 * g + q
                    m = nc.tensor.matmul(bank[4 + g % 2][:, P * q:P * q + P], Ri[:, i, :], Zi[:, i, :], start=True, stop=True)
                m.then_inc(sem("inv_c"), 1)

        with pe.Fori(0, 5) as lv:
            level(lv)
        level(5, True)

        def rhs(ch, par):
            pe.wait_ge(sem("nmq_done"), 3 * NG)
            if ch:
                pe.wait_ge(sem("state"), 1)
            for p in range(NP_):
                i, h = inst(par, ch, p), 2 * p + par
                o = bank[par][:, HD * p:HD * p + HD]
                m = nc.tensor.matmul(o, MQ[:, i, 0:P], vt[:, ch, HD * h:HD * h + HD], start=True, stop=(ch == 0))
                if ch:
                    m = nc.tensor.matmul(o, KR[part(par), 2 * p + 1, 0, :], sT[part(par), p, :], start=False, stop=True)
            m.then_inc(sem("rhs_ps"), 1)

        def solve(ch, par):
            pe.wait_ge(sem("rhs_out"), 2 * ch + par + 1)
            if ch == 0 and par == 0:
                pe.wait_ge(sem("z_done"), NG * 7)
            for p in range(NP_):
                m = nc.tensor.matmul(bank[2 + par][:, HD * p:HD * p + HD], Zi[:, inst(par, ch, p), :], rhsb[:, NP_ * par + p, :],
                                     start=True, stop=True)
            m.then_inc(sem("u_ps"), 1)

        def outputs(ch):
            pe.wait_ge(sem("u_out"), 2 * ch + 2)
            if ch:
                pe.wait_ge(sem("y_out"), 2)
            for par in range(2):
                for p in range(NP_):
                    i, h = inst(par, ch, p), 2 * p + par
                    o = bank[4 + p // 3][part(par), P * (p % 3):P * (p % 3) + P]
                    nc.tensor.matmul(o, uneg[:, NP_ * par + p, :], LT[:, i, :], start=True, stop=False)
                    m = nc.tensor.matmul(o, vt[:, ch, HD * h:HD * h + HD], MQ[:, i, P:2 * P], start=False, stop=(ch == 0))
                    if ch:
                        m = nc.tensor.matmul(o, sT[part(par), p, :], KR[part(par), 2 * p + 1, 1, :], start=False, stop=True)
            m.then_inc(sem("y_ps"), 1)

        def state():
            pe.wait_ge(sem("u_out"), 2)
            for par in range(2):
                for p in range(NP_):
                    h = 2 * p + par
                    o = bank[0][part(par), HD * p:HD * p + HD]
                    nc.tensor.matmul(o, bt[:, HD * h:HD * h + HD], uneg[:, NP_ * par + p, :], start=True, stop=False)
                    m = nc.tensor.matmul(o, ktp[:, HD * h:HD * h + HD], vt[:, 0, HD * h:HD * h + HD], start=False, stop=True)
            m.then_inc(sem("s_ps"), 1)

        pe.wait_ge(sem("tp_out"), 8)
        rhs(0, 0)
        rhs(0, 1)
        solve(0, 0)
        solve(0, 1)
        state()
        outputs(0)
        rhs(1, 0)
        rhs(1, 1)
        solve(1, 0)
        solve(1, 1)
        outputs(1)
        keep_clock(2, 6)
        pe.wait_ge(sem("y_out"), 4)
        for q in range(3):
            for p in (2 * q, 2 * q + 1):
                m = nc.tensor.matmul(bank[q][:, S * (p % 2):S * (p % 2) + S], centre[:, :], yT[:, p, :], start=True, stop=True)
            m.then_inc(sem("centred"), 1)
        head_sums("mq0", 0)
        for q in range(3):
            head_sums("gn", q)
        head_spread("mq0", 0)
        for q in range(3):
            head_spread("gn", q)
        pe.wait_ge(*head_count("gn", "done", 3))
        attend("at0")
        w_out(0)
        ffn(1)
        first_slot("kv", n_kv, 0)
        fp_slot(n_kv + 1, 1)
        pe.wait_ge(sem("rb_ready"), stat_no["kv"] + 1)
        for t in range(TT):
            m = transpose(bank[7][:, P * t:P * t + P], rb[:, P * t:P * t + P])
        m.then_inc(sem("rb_t"), 1)
        for c in range(2, 6):
            if c >= 4:
                pe.wait_ge(sem("k_out"), c - 3)
            (fp_slot if c < 3 else tp_slot)(n_kv + c, c % 4)
        ffn(2)
        first_slot("mix1", n_bin, 0)
        for q in range(3):
            head_sums("kvn", q)
        fp_slot(n_bin + 1, 1)
        for q in range(3):
            head_spread("kvn", q)
        head_sums("bq", 0)
        fp_slot(n_bin + 2, 2)
        head_spread("bq", 0)
        pe.wait_ge(*head_count("kvn", "done", 1))
        head_sums("bq", 1)
        fp_slot(n_bin + 3, 3)
        head_spread("bq", 1)
        pe.wait_ge(*head_count("kvn", "done", 3))
        head_sums("bq", 2)
        head_sums("mq1", 0)
        head_spread("bq", 2)
        head_spread("mq1", 0)
        attend("at1")
        w_out(1)
        ffn(3)
        for t in range(TT):
            for half in range(2):
                b = 4 + 2 * t + half
                if t == 0 and half == 0:
                    pe.wait_ge(sem("x_ready"), UPD_LAST)
                for q in range(4):
                    k = 4 * half + q
                    m = transpose(bank[b][:, P * q:P * q + P], xT[:, k, P * t:P * t + P])
                m.then_inc(sem("out_t"), 1)

    @block.scalar
    def _(act):
        def split(n, half, r=None, rows=False, part=P, tail=False):
            u = 2 * (n % RING) + half
            if r is None:
                r = n // RING
            if tail:
                act.wait_ge(tail_ready, 16 * tail)
            else:
                act.wait_ge(raw_ready[n % RING], 16 * r + 16)
            if not (isinstance(r, int) and r == 0):
                act.wait_ge(unit_used[u], r)
            nc.scalar.activation(unit_dst(whi, n, half, rows)[0:part], unit_src(n, half, rows)[0:part], ACT.Copy)\
                .then_inc(hi_ready[u], 1)

        def split2(n):
            split(n, 0)
            split(n, 1)

        def root(name, q):
            v = head_stat(name, q)
            if name == "kkn":
                act.wait_ge(*head_count(name, "var", q + 1))
                nc.scalar.activation(v, v, ACT.Sqrt).then_inc(sem("head_std"), 1)
            else:
                act.wait_ge(*head_count(name, "sum", q + 1))
                nc.scalar.activation(v, bank[HEAD_BANKS[name][q]][:, 0:8], ACT.Sqrt, scale=1.0 / HD,
                                     bias=eps_col[:, 1:2] if name == "gn" else eps_col[:, 0:1]).then_inc(sem("head_std"), 1)

        def head_wide(name, q):
            act.wait_ge(*head_count(name, "rec", q + 1))
            nc.scalar.activation(fl(head_pair(name, q)).rearrange("p (n c) -> p n c", c=HD),
                                 head_stat(name, q).unsqueeze(2).broadcast_to([P, 8, HD]), ACT.Copy).then_inc(sem("head_wide"), 1)

        def split_units(name, later):
            n, units = PHASE[name]
            for c, half in units[later]:
                split(n + c, half, rows=(name[0:3] == "ffn" and c == 2))

        def h_high(name, k):
            nc.scalar.activation(H[name][0][:, k, :], xT[:, k, :], ACT.Copy, scale=col(norm_gain[name] + k)).then_inc(sem("hhi_ready"), 1)

        def root_of_sums(name):
            act.wait_ge(sem("norm_var"), stat_no[name] + 1)
            nc.scalar.activation(rb[:, :], rb[:, :], ACT.Sqrt).then_inc(sem("norm_std"), 1)

        def norm(name):
            i = stat_no[name]
            if name != "ffn0":
                split_units(name, 0)
            for w, v in NORM_WAITS[name]:
                act.wait_ge(sem(w), v)
            for j in range(4):
                if name == "ffn0" and j < 2:
                    split(j, 0)
                act.wait_ge(sem("x_ready"), upd[norm_after[name]] - 4 + j + 1)
                if name != "mix0":
                    h_high(name, 2 * j)
                    h_high(name, 2 * j + 1)
                nc.scalar.activation(sq[:, 2 * j:2 * j + 2, :], xT[:, 2 * j:2 * j + 2, :], ACT.Square)\
                    .then_inc(sem("sq_ready"), 1)
            split_units(name, 1)
            root_of_sums(name)
            if name == "mix0":
                for k in range(KT):
                    act.wait_ge(sem("hf_ready"), k + 1)
                    nc.scalar.activation(hhi[:, k, :], sq[:, k, :], ACT.Copy).then_inc(sem("hhi_ready"), 1)

        def ffn(f):
            n0, j0 = n_ffn[f], NJ * f
            q = [(n0 + c) // RING for c in range(3)]

            def silu(j, half, rows=P):
                act.wait_ge(sem("pre_ready"), j0 + 1 + j + 1)
                nc.scalar.activation(sg[0:rows, half, :], pre[0:rows, half, 0:S], ACT.Silu).then_inc(sem("silu_done"), 1)

            def g_hi(j, half, rows=P):
                act.wait_ge(sem("g32_done"), j0 + j + 1)
                nc.scalar.activation(ghi[0:rows, half, :], g32[0:rows, half, :], ACT.Copy).then_inc(sem("ghi_done"), 1)

            def double(t, between=None):
                silu(2 * t, 0)
                split(n0, 0, t + 1 + q[0])
                g_hi(2 * t, 0)
                split(n0 + 1, 0, t + 1 + q[1])
                split(n0 + 2, 1, t + q[2], True)
                if between:
                    between(2 * t)
                silu(2 * t + 1, 1)
                split(n0, 1, t + 1 + q[0])
                g_hi(2 * t + 1, 1)
                split(n0 + 1, 1, t + 1 + q[1])
                split(n0 + 2, 0, t + 1 + q[2], True)
                if between:
                    between(2 * t + 1)

            first = PEEL if f == 0 else 0
            for t in range(first):
                double(t, mem_step)
            with act.Fori(first, FULL) as t:
                double(t)
            silu(NJ - 2, 0)
            g_hi(NJ - 2, 0)
            split(n0 + 2, 1, FULL + q[2], True, LASTROWS, tail=f + 1)
            silu(NJ - 1, 1, LASTROWS)
            g_hi(NJ - 1, 1, LASTROWS)

        def mem_step(n):
            if n == 0:
                act.wait_ge(sem("mem_var"), 1)
                nc.scalar.activation(stat[:, 9, 0:2], stat[:, 9, 0:2], ACT.Sqrt).then_inc(sem("mem_std"), 1)
            if n >= 4:
                l, k0 = (n - 4) // 2, 4 * (n % 2)
                act.wait_ge(sem("mt_out"), k0 // 2 + 2)
                for k in range(k0, k0 + 4):
                    nc.scalar.activation(mem_h_at[l, "hi"][:, k, :], mT[:, k, :], ACT.Copy, scale=col(G_MEM + 8 * l + k))\
                        .then_inc(sem("mhi_ready"), 1)

        act.wait_ge(sem("gains_ready"), 1)
        norm("ffn0")
        act.wait_ge(sem("mem_loaded"), 16)
        for t in range(TT):
            m = nc.scalar.activation(sq[:, 4 * t:4 * t + 4, :].rearrange("p a b -> p (a b)"), mrow[:, t, :], ACT.Square,
                                     accum_out=stat[:, 9, t:t + 1])
        m.then_inc(sem("mem_ss"), 1)
        ffn(0)
        def attend(name, meanwhile=None):
            heads = HEADS[name]

            def exps(n):
                act.wait_ge(*attn_count(name, "max", n + 1))
                for t in range(TT):
                    c = query_cols(heads[n], t)
                    src = bank[n % 3][:, c] if heads[n][3] is None else prb[:, n % 3, c]
                    m = nc.scalar.activation(prb[:, n % 3, c], src, ACT.Exp, bias=sml[:, n % 4, t:t + 1], scale=SCALE,
                                             accum_out=sml[:, n % 4, 2 + t:3 + t])
                m.then_inc(sem("attn_exp"), 1)

            def turned(n):
                act.wait_ge(*attn_count(name, "turn", n + 1))
                if n >= 2:
                    act.wait_ge(*attn_count(name, "values", n - 1))
                c = P * len(blocks(heads[n]))
                nc.scalar.activation(prT[:, n % 2, 0:c], bank[3 + n % 2][:, 0:c], ACT.Copy).then_inc(sem("attn_turned"), 1)

            def pair(p):
                high(int(name[2]), OUT_TILE[name] + p, bank[5 + p % 2][:, 0:S],
                     *attn_count(name, "values", 2 * p + 2))

            exps(0)
            for n in range(len(heads)):
                if n >= 4 and n % 2 == 0:
                    pair(n // 2 - 2)
                if n + 1 < len(heads):
                    exps(n + 1)
                turned(n)
                if meanwhile:
                    meanwhile(n)
            pair(len(heads) // 2 - 2)
            pair(len(heads) // 2 - 1)

        def high(l, k, src, w, v):
            act.wait_ge(w, v)
            nc.scalar.activation(hhi[:, k, :], src, ACT.Copy).then_inc(sem(f"mixhi{l}"), 1)

        norm("mix0")

        def w_in_out(i):
            slot_done(act, n_win + i)
            b = bank[i % 4]
            for half in range(2):
                c = W_IN_ORDER[i] * 2 + half
                m = nc.scalar.activation(U_TILES[i][half], b[:, S * half:S * half + S], ACT.Copy, scale=omu[:, c:c + 1])
            m.then_inc(sem("shift_a"), 1)
            if i + 3 < 11:
                split2(n_win + i + 3)

        split2(n_mem + 3)
        for c in range(3):
            split2(n_win + c)
        act.wait_ge(sem("mem_k_out"), 2)
        act.wait_ge(sem("h_ready"), 8 * norm_no["mix0"] + 8)
        for l in range(2):
            nc.scalar.activation(sq[:, 2 * l:2 * l + 2, :], kmT[:, l, :, :], ACT.Square).then_inc(sem("head_sq"), 1)
        for l in range(2):
            slot_done(act, n_mem + 2 * l + 1)
            nc.scalar.activation(fl(vm[:, l, :, :]), bank[(5, 2)[l]][:, :], ACT.Copy).then_inc(sem("mem_v_done"), 1)
        w_in_out(0)
        root("kn0", 0)
        root("kn1", 0)
        act.wait_ge(sem("win_free"), 1)
        nc.scalar.activation(wa[0:HD, :], wa[0:HD, :], ACT.Tanh).then_inc(sem("lora_in"), 1)
        nc.scalar.activation(gd[:, :], gd[:, :], ACT.Sigmoid).then_inc(sem("lora_in"), 1)
        w_in_out(1)
        w_in_out(2)
        for p in range(NP_):
            act.wait_ge(sem("lora_wa"), p + 1)
            nc.scalar.activation(pw[:, 2 * p:2 * p + 2, 1:P + 1], bank[4 + p % 2][:, 0:S].rearrange("p (c t) -> p c t", c=2), ACT.Sigmoid,
                                 bias=col(C_W0 + p)).then_inc(sem("lw_ready"), 1)
            nc.scalar.activation(ua[:, p, :], bank[6 + p % 2][:, 0:S], ACT.Sigmoid, bias=col(C_A0 + p)).then_inc(sem("a_ready"), 1)
        for q in range(3):
            act.wait_ge(sem("lora_g"), q + 1)
            nc.scalar.activation(fl(gT[:, 2 * q:2 * q + 2, :]), bank[6 + q % 2][:, :], ACT.Copy).then_inc(sem("g_out"), 1)
        w_in_out(3)
        act.wait_ge(sem("win_free"), 4)
        for p in range(NP_):
            m = nc.scalar.activation(sq[:, p, :], uk[:, p, :], ACT.Square, scale=col(C_KK + p))
            if p % 2:
                m.then_inc(sem("head_sq"), 1)
        w_in_out(4)
        w_in_out(5)
        for q in range(3):
            root("kkn", q)
        for q in range(3):
            head_wide("kkn", q)
        w_in_out(6)
        act.wait_ge(sem("cum_ready"), 1)
        nc.scalar.activation(sfin[:, 1, :], c12[:, 1::2, 0], ACT.Exp, scale=-DECAY).then_inc(sem("mid_power"), 1)
        nc.scalar.activation(pr[:, :, :], pw[:, :, :], ACT.Exp, scale=-DECAY).then_inc(sem("powers"), 1)
        nc.scalar.activation(pw[:, :, :], pw[:, :, :], ACT.Exp, scale=DECAY).then_inc(sem("powers"), 1)
        for i in range(7, 10):
            w_in_out(i)
        slot_done(act, n_win + 10)
        nc.scalar.activation(fl(mq[:, :, :]), bank[10 % 4][:, :], ACT.Copy).then_inc(sem("mq_out"), 1)
        for j in range(8):
            act.wait_ge(sem("tp_t"), j + 1)
            if j == 4:
                act.wait_ge(sem("powers_used"), 4)
            q = j % 2
            dst = vt[:, j // 2, 384 * q:384 * q + 384] if j < 4 else (bt, ktp)[j // 2 - 2][:, 384 * q:384 * q + 384]
            nc.scalar.activation(dst, bank[4 + j % 2][:, 0:384], ACT.Copy).then_inc(sem("tp_out"), 1)
        for g in range(NG):
            act.wait_ge(sem("x1_t"), g + 1)
            nc.scalar.activation(fl(Xi[:, 4 * g:4 * g + 4, :]), bank[2 + g % 2][:, :], ACT.Copy).then_inc(sem("x_done"), 1)

        def level(lv, last=False):
            for g in range(NG):
                if not last:
                    act.wait_ge(sem("inv_b"), NG * lv + g + 1)
                    nc.scalar.activation(fl(Xi[:, 4 * g:4 * g + 4, :]), bank[2 + g % 2][:, :], ACT.Copy).then_inc(sem("x_done"), 1)
                act.wait_ge(sem("inv_c"), NG * lv + g + 1)
                nc.scalar.activation(fl(Zi[:, 4 * g:4 * g + 4, :]), bank[4 + g % 2][:, :], ACT.Copy).then_inc(sem("z_done"), 1)

        with act.Fori(0, 5) as lv:
            level(lv)
        level(5, True)
        for ch in range(2):
            for par in range(2):
                act.wait_ge(sem("rhs_ps"), 2 * ch + par + 1)
                nc.scalar.activation(fl(rhsb[:, NP_ * par:NP_ * par + NP_, :]), bank[par][:, 0:384], ACT.Copy)\
                    .then_inc(sem("rhs_out"), 1)
            for par in range(2):
                act.wait_ge(sem("u_ps"), 2 * ch + par + 1)
                if ch:
                    act.wait_ge(sem("y_ps"), 1)
                nc.scalar.activation(fl(uneg[:, NP_ * par:NP_ * par + NP_, :]), bank[2 + par][:, 0:384], ACT.Copy,
                                     scale=-1.0).then_inc(sem("u_out"), 1)
            act.wait_ge(sem("y_ps"), ch + 1)
            for q in range(2):
                nc.scalar.activation(yT[:, 3 * q:3 * q + 3, tokens(ch)], bank[4 + q][:, 0:384].rearrange("p (a t) -> p a t", a=3),
                                     ACT.Copy).then_inc(sem("y_out"), 1)
        nc.scalar.activation(head_pair("mq0", 0), mq[:, :, :], ACT.Square).then_inc(sem("head_sq"), 1)
        for q in range(3):
            act.wait_ge(sem("d_out"), q + 1)
            nc.scalar.activation(head_pair("gn", q), dT[:, 2 * q:2 * q + 2, :], ACT.Square).then_inc(sem("head_sq"), 1)
        root("mq0", 0)
        for q in range(3):
            root("gn", q)
        head_wide("mq0", 0)
        for q in range(3):
            head_wide("gn", q)

        def mixer_output(n):
            if n == 0:
                split2(n_wout[0])
            if n == 1:
                for p in range(NP_):
                    high(0, p, dT[:, p, :], sem("mix_f"), p + 1)

        attend("at0", mixer_output)
        split2(n_wout[0] + 1)
        split2(n_wout[0] + 2)
        split2(n_wout[0] + 3)
        norm("ffn1")
        ffn(1)
        norm("kv")
        for c in range(6):
            if c < 3:
                split2(n_kv + c + 3)
            else:
                slot_done(act, n_kv + c)
                act.wait_ge(sem("rcol_ready"), 1)
                for t in range(TT):
                    m = nc.scalar.activation(vt2[:, t, 256 * (c - 3):256 * (c - 3) + 256], bank[c % 4][:, S * t:S * t + S],
                                             ACT.Copy, scale=rcol[:, t:t + 1])
                m.then_inc(sem("v_out"), 1)
                if c < 5:
                    split2(n_ffn[2] + c - 3)
            if c == 2:
                for k in range(KT):
                    h_high("ffn2", k)
        split_units("ffn2", 1)
        ffn(2)
        norm("mix1")
        for q in range(3):
            nc.scalar.activation(head_pair("kvn", q), kT[:, 2 * q:2 * q + 2, :], ACT.Square).then_inc(sem("head_sq"), 1)
        for q in range(3):
            root("kvn", q)
        for c in range(4):
            act.wait_ge(sem("q_out"), c + 1)
            nc.scalar.activation(sq[:, 2 * c:2 * c + 2, :], qT[:, 2 * c:2 * c + 2, :], ACT.Square)\
                .then_inc(sem("head_sq"), 1)
            if c == 0:
                split2(n_bin + 3)
            else:
                root("bq", c - 1)
        root("mq1", 0)
        head_wide("bq", 2)
        head_wide("mq1", 0)

        def w_out_units(n):
            if n < 12 and n % 2 == 0:
                split(n_wout[1] + n // 4, n // 2 % 2)

        attend("at1", w_out_units)
        split2(n_wout[1] + 3)
        norm("ffn3")
        ffn(3)

    @block.vector
    def _(dve):
        TTo = nc.vector.tensor_tensor
        TS = nc.vector.tensor_scalar
        STT = nc.vector.scalar_tensor_tensor
        seq = sem("dve_seq")
        cnt = [0]

        def mark(ins):
            cnt[0] += 1
            ins.then_inc(seq, 1)
            return ins

        def settle():
            dve.wait_ge(seq, cnt[0])

        def split(n, half, r=None, rows=False, part=P):
            u = 2 * (n % RING) + half
            if r is None:
                r = n // RING
            dve.wait_ge(hi_ready[u], r + 1)
            TTo(unit_dst(wlo, n, half, rows)[0:part], unit_src(n, half, rows)[0:part],
                unit_dst(whi, n, half, rows)[0:part].bitcast(F32), ALU.subtract).then_inc(lo_ready[u], 1)

        def split2(n):
            split(n, 0)
            split(n, 1)

        def head_recip(name, q):
            v = head_stat(name, q)
            dve.wait_ge(*head_count(name, "std", q + 1))
            nc.vector.reciprocal(v, v).then_inc(sem("head_rec"), 1)

        def head_norm(name, q, src, dst, gain):
            dve.wait_ge(*head_count(name, "rb", q + 1))
            for e in range(2):
                p = 2 * q + e
                m = STT(dst[:, p, :], src[:, p, :], gain(p), bank[HEAD_BANKS[name][q]][:, S * e:S * e + S], ALU.mult, ALU.mult)
            m.then_inc(sem("head_done"), 1)

        def norm_mix():
            root_of_sums("mix0")
            i = norm_no["mix0"]

            def low(k):
                dve.wait_ge(sem("hhi_ready"), 8 * i + k + 1)
                TTo(hlo[:, k, :], sq[:, k, :], hhi[:, k, :].bitcast(F32), ALU.subtract).then_inc(sem("h_ready"), 1)

            for k in range(KT):
                STT(sq[:, k, :], xT[:, k, :], col(norm_gain["mix0"] + k), rb[:, :], ALU.mult, ALU.mult).then_inc(sem("hf_ready"), 1)
                if k >= 2:
                    low(k - 2)
            low(KT - 2)
            low(KT - 1)

        def split_units(name, later):
            n, units = PHASE[name]
            for c, half in units[later]:
                split(n + c, half, rows=(name[0:3] == "ffn" and c == 2))

        def h_low(name, k):
            dve.wait_ge(sem("hhi_ready"), 8 * norm_no[name] + k + 1)
            hi, lo = H[name]
            STT(lo[:, k, :], xT[:, k, :], col(norm_gain[name] + k), hi[:, k, :].bitcast(F32), ALU.mult, ALU.subtract)\
                .then_inc(sem("h_ready"), 1)

        def root_of_sums(name):
            i = stat_no[name]
            dve.wait_ge(sem("norm_stat"), i + 1)
            TS(rb[:, :], bank[6][:, 0:S], 1.0 / D, EPS, ALU.mult, ALU.add).then_inc(sem("norm_var"), 1)
            dve.wait_ge(sem("norm_std"), i + 1)
            nc.vector.reciprocal(rb[:, :], rb[:, :]).then_inc(sem("rb_ready"), 1)
            dve.wait_ge(sem("rb_ready"), i + 1)

        def new_x(name, update):
            if name is None or name == "mix0":
                for b in range(4):
                    update(b)
                if name:
                    split_units(name, 1)
                return
            update(0)
            for b in range(4):
                if b < 3:
                    update(b + 1)
                h_low(name, 2 * b)
                h_low(name, 2 * b + 1)
            split_units(name, 1)
            root_of_sums(name)

        def by_rb(o, b, n=2):
            return TTo(o.rearrange("p (n s) -> p n s", n=n), b.rearrange("p (n s) -> p n s", n=n),
                       rb[0:o.shape[0], :].unsqueeze(1).broadcast_to([o.shape[0], n, S]), ALU.mult)

        def ffn(f, following):
            n0, j0 = n_ffn[f], NJ * f
            q = [(n0 + c) // RING for c in range(3)]

            def normed(half, r, rows=P):
                dve.wait_ge(unit_used[2 * ((n0 + 1) % RING) + half], r + q[1] + 1)
                by_rb(pre[0:rows, half, :], bank[4 + half][0:rows, :]).then_inc(sem("pre_ready"), 1)

            def gate(j, half, rows=P):
                dve.wait_ge(sem("silu_done"), j0 + j + 1)
                TTo(g32[0:rows, half, :], sg[0:rows, half, :], pre[0:rows, half, S:2 * S], ALU.mult)\
                    .then_inc(sem("g32_done"), 1)

            def g_lo(j, half, rows=P):
                dve.wait_ge(sem("ghi_done"), j0 + j + 1)
                TTo(glo[0:rows, half, :], g32[0:rows, half, :], ghi[0:rows, half, :].bitcast(F32), ALU.subtract)\
                    .then_inc(sem("g_ready"), 1)

            def double(t, between=None):
                normed(0, t)
                split(n0, 0, t + 1 + q[0])
                gate(2 * t, 0)
                g_lo(2 * t, 0)
                split(n0 + 1, 0, t + 1 + q[1])
                split(n0 + 2, 1, t + q[2], True)
                if between:
                    between(2 * t)
                normed(1, t)
                split(n0, 1, t + 1 + q[0])
                gate(2 * t + 1, 1)
                g_lo(2 * t + 1, 1)
                split(n0 + 1, 1, t + 1 + q[1])
                split(n0 + 2, 0, t + 1 + q[2], True)
                if between:
                    between(2 * t + 1)

            first = PEEL if f == 0 else 0
            for t in range(first):
                double(t, mem_step)
            with dve.Fori(first, FULL) as t:
                double(t)
            normed(0, FULL)
            gate(NJ - 2, 0)
            g_lo(NJ - 2, 0)
            split(n0 + 2, 1, FULL + q[2], True, LASTROWS)
            normed(1, FULL, LASTROWS)
            gate(NJ - 1, 1, LASTROWS)
            g_lo(NJ - 1, 1, LASTROWS)
            if following is not None:
                split_units(following, 0)
            slot_done(dve, n0 + 3 * FULL + 2)

            def update(b):
                STT(fl(xT[:, 2 * b:2 * b + 2, :]), bank[b][:, :], 0.5, fl(xT[:, 2 * b:2 * b + 2, :]), ALU.mult, ALU.add)\
                    .then_inc(sem("x_ready"), 1)
            new_x(following, update)

        nc.vector.memset(stat[:, 10, :], 0.0).then_inc(sem("pre_ready"), 1)
        def mem_step(n):
            if n == 0:
                dve.wait_ge(sem("mem_ss"), 1)
                TS(stat[:, 9, 0:2], stat[:, 9, 0:2], 1.0 / D, EPS, ALU.mult, ALU.add).then_inc(sem("mem_var"), 1)
            if n == 1:
                dve.wait_ge(sem("mem_std"), 1)
                mark(nc.vector.reciprocal(stat[:, 9, 0:2], stat[:, 9, 0:2]))
                settle()
                for t in range(TT):
                    TS(mrow[:, t, :], mrow[:, t, :], stat[:, 9, t:t + 1], None, ALU.mult).then_inc(sem("mem_scaled"), 1)
                dve.wait_ge(sem("prm_t"), 1)
                mark(nc.vector.tensor_copy(prm[:, 16:rowsA + rowsB], bank[7][:, 16:rowsA + rowsB]))
                settle()
                mark(TS(omu[:, 0:20], prm[:, C_MU:C_MU + 20], -1.0, 1.0, ALU.mult, ALU.add))
                TS(omu[:, 20:26], prm[:, C_KA:C_KA + 6], -1.0, 1.0, ALU.mult, ALU.add).then_inc(sem("prm_ready"), 1)
            if n in (3, 4):
                for j in (2 * (n - 3), 2 * (n - 3) + 1):
                    dve.wait_ge(sem("m_t"), j + 1)
                    nc.vector.tensor_copy(fl(mT[:, 2 * j:2 * j + 2, :]), bank[6 + j % 2][:, :]).then_inc(sem("mt_out"), 1)
            if n == 4:
                dve.wait_ge(sem("mt_out"), 4)
            if n >= 4:
                l, k0 = (n - 4) // 2, 4 * (n % 2)
                for k in range(k0, k0 + 4):
                    dve.wait_ge(sem("mhi_ready"), 8 * l + k + 1)
                    STT(mem_h_at[l, "lo"][:, k, :], mT[:, k, :], col(G_MEM + 8 * l + k), mem_h_at[l, "hi"][:, k, :].bitcast(F32),
                        ALU.mult, ALU.subtract).then_inc(sem("mem_h"), 1)

        dve.wait_ge(sem("gains_t"), 1)
        nc.vector.tensor_copy(prm[:, 0:16], bank[7][:, 0:16]).then_inc(sem("gains_ready"), 1)
        dve.wait_ge(sem("gains_ready"), 1)
        for j in range(4):
            dve.wait_ge(sem("x_t"), j + 1)
            nc.vector.tensor_copy(fl(xT[:, 2 * j:2 * j + 2, :]), bank[j][:, :]).then_inc(sem("x_ready"), 1)
            if j == 1:
                split(0, 0)
            if j == 2:
                h_low("ffn0", 0)
                h_low("ffn0", 1)
                split(1, 0)
        for k in range(2, KT):
            h_low("ffn0", k)
        split_units("ffn0", 1)
        root_of_sums("ffn0")
        ffn(0, "mix0")
        def attend(name, meanwhile=None):
            heads = HEADS[name]

            def maxima(n):
                slope = heads[n][3]
                dve.wait_ge(*attn_count(name, "scores", n + 1))
                if n >= 3:
                    dve.wait_ge(*attn_count(name, "turn", n - 2))
                src = bank[n % 3][:, :]
                if slope is not None:
                    src = prb[:, n % 3, 0:3 * P]
                    mark(STT(src, fl(dist[:, :, :]), -slope / SCALE, bank[n % 3][:, 0:3 * P], ALU.mult, ALU.add))
                    settle()
                for t in range(TT):
                    mark(nc.vector.tensor_reduce(sml[:, n % 4, t:t + 1], src[:, query_cols(heads[n], t)], AX.X, ALU.max))
                settle()
                TS(sml[:, n % 4, 0:TT], sml[:, n % 4, 0:TT], -SCALE, None, ALU.mult).then_inc(sem("attn_max"), 1)

            def normalise(n):
                dve.wait_ge(*attn_count(name, "exp", n + 1))
                mark(nc.vector.reciprocal(sml[:, n % 4, 4:4 + TT], sml[:, n % 4, 2:2 + TT]))
                settle()
                for t in range(TT):
                    e = prb[:, n % 3, query_cols(heads[n], t)]
                    m = TS(e, e, sml[:, n % 4, 4 + t:5 + t], None, ALU.mult)
                m.then_inc(sem("attn_probs"), 1)

            def pair(p):
                low_mix(int(name[2]), OUT_TILE[name] + p, bank[5 + p % 2][:, 0:S])

            maxima(0)
            for n in range(len(heads)):
                if n + 1 < len(heads):
                    maxima(n + 1)
                normalise(n)
                if n >= 4 and n % 2 == 0:
                    pair(n // 2 - 2)
                if meanwhile:
                    meanwhile(n)
            pair(len(heads) // 2 - 2)
            pair(len(heads) // 2 - 1)

        def low_mix(l, k, src):
            dve.wait_ge(sem(f"mixhi{l}"), k + 1)
            TTo(hlo[:, k, :], src, hhi[:, k, :].bitcast(F32), ALU.subtract).then_inc(sem(f"mixed{l}"), 1)

        def w_out(l, following):
            split2(n_wout[l] + 3)
            if following is not None:
                split_units(following, 0)

            def update(c):
                slot_done(dve, n_wout[l] + c)
                x = fl(xT[:, 2 * c:2 * c + 2, :])
                TTo(x, bank[c][:, :], x, ALU.add).then_inc(sem("x_ready"), 1)
            new_x(following, update)

        dve.wait_ge(sem("all_consts"), 1)
        norm_mix()

        def shift(i):
            dve.wait_ge(sem("shift_a"), i + 1)
            for half in range(2):
                c = W_IN_ORDER[i] * 2 + half
                u = U_TILES[i][half]
                m = STT(u[:, 1:S], bank[i % 4][:, S * half:S * half + S - 1], col(C_MU + c), u[:, 1:S], ALU.mult, ALU.add)
            m.then_inc(sem("win_free"), 1)
            if i + 3 < 11:
                split2(n_win + i + 3)

        split2(n_mem + 3)
        for c in range(3):
            split2(n_win + c)
        for l in range(2):
            slot_done(dve, n_mem + 2 * l)
            nc.vector.tensor_copy(fl(kmT[:, l, :, :]), bank[(4, 3)[l]][:, :]).then_inc(sem("mem_k_out"), 1)
        dve.wait_ge(sem("mem_k_out"), 2)

        def key_norm(l):
            head_norm(f"kn{l}", 0, kmT[:, l, :, :], kmT[:, l, :, :], lambda p: col(C_MK + l))

        shift(0)
        mark(nc.vector.memset(pw[:, :, 0:1], 0.0))
        head_recip("kn0", 0)
        head_recip("kn1", 0)
        key_norm(0)
        key_norm(1)
        for i in range(1, 4):
            shift(i)
        for p in range(NP_):
            dve.wait_ge(sem("lw_ready"), p + 1)
            for j in (2 * p, 2 * p + 1):
                mark(nc.vector.tensor_tensor_scan(pw[:, j, 1:P + 1], ones[:, :], pw[:, j, 1:P + 1], 0.0, ALU.mult, ALU.add))
        settle()
        mark(nc.vector.tensor_copy(c12[:, :, :], pw[:, :, HD:HD + 1]))
        settle()
        TTo(pw[:, :, :], pw[:, :, :], c12[:, :, :].broadcast_to([P, 2 * NP_, P + 1]), ALU.subtract).then_inc(sem("cum_ready"), 1)
        shift(4)
        shift(5)

        def floor(q):
            dve.wait_ge(*head_count("kkn", "sum", q + 1))
            TS(head_stat("kkn", q), bank[HEAD_BANKS["kkn"][q]][:, 0:8], 1e-24, None, ALU.max).then_inc(sem("head_var"), 1)

        for q in range(3):
            floor(q)
        for q in range(3):
            head_recip("kkn", q)
        dve.wait_ge(sem("a_ready"), NP_)
        tmp = KR[:, :, :, :].rearrange("p a b c -> p (a b c)")[:, 0:NP_ * S].rearrange("p (a s) -> p a s", a=NP_)
        for p in range(NP_):
            mark(TS(tmp[:, p, :], ua[:, p, :], col(C_KA + p), omu[:, 20 + p:21 + p], ALU.mult, ALU.add))
        for q in range(3):
            head_norm("kkn", q, uk, kk, lambda p: col(C_KK + p))
        dve.wait_ge(*head_count("kkn", "done", 3))
        settle()
        mark(TTo(fl(uk[:, :, :]), fl(uk[:, :, :]), fl(tmp), ALU.mult))
        mark(TTo(fl(ua[:, :, :]), fl(kk[:, :, :]), fl(ua[:, :, :]), ALU.mult))
        settle()
        shift(6)
        shift(7)
        dve.wait_ge(sem("win_free"), 7)
        for p in range(NP_):
            m = STT(sq[:, p, :], ur[:, p, :], col(C_RK + p), uk[:, p, :], ALU.mult, ALU.mult)
            if p % 2:
                m.then_inc(sem("head_sq"), 1)
        shift(8)
        shift(9)
        dve.wait_ge(sem("powers"), 2)
        dve.wait_ge(sem("mid_power"), 1)
        for q in range(3):
            dve.wait_ge(*head_count("bn", "sum", q + 1))
            nc.vector.tensor_copy(head_stat("bn", q), bank[HEAD_BANKS["bn"][q]][:, 0:8]).then_inc(sem("head_rec"), 1)

        def per_chunk(t):
            return t[:, :, :].rearrange("p a (c t) -> p (a c) t", c=2)

        TTo(KR[:, :, 0, :], per_chunk(kk), pr[:, :, 0:P], ALU.mult).then_inc(sem("powers_used"), 1)
        TTo(KR[:, :, 1, :], per_chunk(ur), pr[:, :, 1:P + 1], ALU.mult).then_inc(sem("powers_used"), 1)
        TTo(sfin[:, 0, :], sfin[:, 1, :], pr[:, 0::2, P], ALU.mult).then_inc(sem("powers_used"), 1)
        mark(TTo(per_chunk(ua), per_chunk(ua), pw[:, :, 1:P + 1], ALU.mult))
        TTo(per_chunk(uk), per_chunk(uk), pw[:, :, 1:P + 1], ALU.mult).then_inc(sem("powers_used"), 1)
        dve.wait_ge(sem("tp_t"), 4)
        for q in range(3):
            v = fl(uv[:, 2 * q:2 * q + 2, :])
            dve.wait_ge(*head_count("bn", "rb", q + 1))
            TTo(v, v, bank[HEAD_BANKS["bn"][q]][:, :], ALU.mult).then_inc(sem("head_done"), 1)
        dve.wait_ge(sem("lt_unit"), 1)

        def lt(g):
            dve.wait_ge(sem("lt_ps"), g + 1)
            nc.vector.copy_predicated(LT[:, 4 * g:4 * g + 4, :], tri4[:, :, :].bitcast(I32),
                                      bank[g % 2][:, :].rearrange("p (a t) -> p a t", a=4)).then_inc(sem("lt_done"), 1)

        def z1(g):
            dve.wait_ge(sem("lt_done"), g + 1)
            TTo(Zi[:, 4 * g:4 * g + 4, :], LT[:, 4 * g:4 * g + 4, :], z1mask[:, :].unsqueeze(1).broadcast_to([P, 4, P]), ALU.mult)\
                .then_inc(sem("z_done"), 1)

        for g in range(NG):
            lt(g)
            z1(g)

        def level(lv, last=False):
            q = bass.ds(lv + 1, 1)
            for g in range(NG):
                dve.wait_ge(sem("inv_a"), NG * lv + g + 1)
                TTo(Ri[:, 4 * g:4 * g + 4, :], bank[g % 2][:, :].rearrange("p (a t) -> p a t", a=4),
                    invmask[:, q, :].broadcast_to([P, 4, P]), ALU.mult).then_inc(sem("r_done"), 1)
                if last:
                    triangles(g)

        def triangles(g):
            dve.wait_ge(sem("nmq_ps"), 3 * g + 1)
            nc.vector.copy_predicated(LT[:, 4 * g:4 * g + 4, :], upper4[:, :, :].bitcast(I32),
                                      bank[6][:, :].rearrange("p (a t) -> p a t", a=4)).then_inc(sem("nmq_done"), 1)
            if g == 0:
                dve.wait_ge(sem("mq_zero"), 1)
            for b in range(2):
                dve.wait_ge(sem("nmq_ps"), 3 * g + b + 2)
                i = 4 * g + 2 * b
                nc.vector.copy_predicated(fl(MQ[:, i:i + 2, :]), fl(tri_mq[:, :, :]).bitcast(I32), bank[(7, 3)[b]][:, :])\
                    .then_inc(sem("nmq_done"), 1)

        with dve.Fori(0, 5) as lv:
            level(lv)
        level(5, True)
        dve.wait_ge(sem("s_ps"), 1)
        TTo(sT[:, :, :], bank[0][:, 0:384].rearrange("p (a v) -> p a v", a=NP_),
            sfin[:, 0, :].unsqueeze(2).broadcast_to([P, NP_, HD]), ALU.mult).then_inc(sem("state"), 1)
        for q in range(3):
            dve.wait_ge(sem("centred"), q + 1)
            nc.vector.tensor_copy(fl(dT[:, 2 * q:2 * q + 2, :]), bank[q][:, :]).then_inc(sem("d_out"), 1)
        dve.wait_ge(sem("d_out"), 3)
        head_recip("mq0", 0)
        for q in range(3):
            head_recip("gn", q)
        head_norm("mq0", 0, mq, mq, lambda p: col(C_MQ))
        for q in range(3):
            head_norm("gn", q, dT, dT, lambda p: col(C_LNW + p))

        def mixer_output(n):
            if n == 0:
                dve.wait_ge(*head_count("gn", "done", 3))
                for p in range(NP_):
                    mark(STT(dT[:, p, :], dT[:, p, :], col(C_LNB + p), uv[:, p, :], ALU.add, ALU.add))
            if n == 1:
                settle()
                for p in range(NP_):
                    TTo(dT[:, p, :], dT[:, p, :], gT[:, p, :], ALU.mult).then_inc(sem("mix_f"), 1)
            if n == 2:
                for p in range(NP_):
                    low_mix(0, p, dT[:, p, :])
            if n == 3:
                split2(n_wout[0])

        attend("at0", mixer_output)
        split2(n_wout[0] + 1)
        split2(n_wout[0] + 2)
        w_out(0, "ffn1")
        ffn(1, "kv")
        for c in range(3):
            slot_done(dve, n_kv + c)
            by_rb(fl(kT[:, 2 * c:2 * c + 2, :]), bank[c][:, :]).then_inc(sem("k_out"), 1)
            if c == 0:
                dve.wait_ge(sem("rb_t"), 1)
                nc.vector.tensor_copy(rcol[:, :], bank[7][:, 0:S:P]).then_inc(sem("rcol_ready"), 1)
            split2(n_kv + c + 3)
        for k in range(KT):
            h_low("ffn2", k)
        split_units("ffn2", 0)
        split_units("ffn2", 1)
        ffn(2, "mix1")
        for c in range(4):
            slot_done(dve, n_bin + c)
            by_rb(fl(qT[:, 2 * c:2 * c + 2, :]), bank[c][:, :]).then_inc(sem("q_out"), 1)
            if c == 0:
                split2(n_bin + 3)
                for q in range(3):
                    head_recip("kvn", q)
            if c == 1:
                for q in range(3):
                    head_norm("kvn", q, kT, kT, lambda p: col(C_KVK))
            if c:
                head_recip("bq", c - 1)
            if c >= 2:
                head_norm("bq", c - 2, qT, qT, lambda p: col(C_BQ))
        head_recip("mq1", 0)
        dve.wait_ge(sem("q_out"), 4)
        head_norm("bq", 2, qT, qT, lambda p: col(C_BQ))
        head_norm("mq1", 0, qT[:, NP_:NP_ + 2, :], qT[:, NP_:NP_ + 2, :], lambda p: col(C_MQ + 1))

        def w_out_units(n):
            if n < 12 and n % 2 == 1:
                split(n_wout[1] + n // 4, n // 2 % 2)

        attend("at1", w_out_units)
        w_out(1, "ffn3")
        ffn(3, None)
        for t in range(TT):
            for half in range(2):
                dve.wait_ge(sem("out_t"), 2 * t + half + 1)
                nc.vector.tensor_copy(xrow[:, t, 512 * half:512 * half + 512], bank[4 + 2 * t + half][:, :])\
                    .then_inc(sem("out_rows_ready"), 1)

    ctx.close()


_INS = ["x", "mem", "ffn1_norm", "ffn1_w1", "ffn1_w3", "ffn1_w2", "mix_norm", "w_out", "mem_norm", "w_mem_kv",
        "mem_q_norm", "mem_k_norm", "ffn2_norm", "ffn2_w1", "ffn2_w3", "ffn2_w2", "rwkv_w_in", "rwkv_mu", "rwkv_w0",
        "rwkv_w2", "rwkv_a0", "rwkv_a2", "rwkv_g2", "rwkv_k_k", "rwkv_k_a", "rwkv_r_k", "rwkv_ln_w", "rwkv_ln_b",
        "kv_norm", "w_kv", "kv_k_norm", "moba_w_in", "moba_q_norm"]


def kernel(**inputs):
    import numpy as np
    import concourse.bacc as bacc
    from concourse.bass_utils import run_bass_kernel_spmd

    nc = bacc.Bacc("TRN2", target_bir_lowering=False, num_devices=1)
    arrays, T = {}, {}
    for name in _INS:
        arrays[name] = np.ascontiguousarray(inputs[name])
        T[name] = nc.dram_tensor(name, arrays[name].shape, F32, kind="ExternalInput").ap()
    out = nc.dram_tensor("out", (1, S, D), F32, kind="ExternalOutput").ap()
    build(nc, T, out)
    return run_bass_kernel_spmd(nc, [arrays], core_ids=[0]).results[0]["out"]
```
